# Optimizing a Trainium2 kernel written in Bass

```python
import math
import jax
import jax.numpy as jnp
from jax import lax
import numpy as np
import jax, jax.numpy as jnp

D_MODEL = 1024
BATCH = 1
SEQ = 256
DEPTH = 1

N_MOD = 6
EPS = 1e-6
GM_CHUNK = 128
GM_HEAD = 128
GM_GROUPS = D_MODEL // GM_HEAD
GM_WIDTH = GM_GROUPS * GM_HEAD
SSM_INNER = 2 * D_MODEL
SSM_HEAD_DIM = 64
SSM_HEADS = SSM_INNER // SSM_HEAD_DIM
SSM_GROUPS = 8
SSM_STATE = 128
SSM_CONV = 4
SSM_CHUNK = 128
CONV_DIM = SSM_INNER + 2 * SSM_GROUPS * SSM_STATE
D_FF = 4 * D_MODEL
IN_SIZES = (GM_WIDTH, GM_WIDTH, SSM_INNER, CONV_DIM, SSM_HEADS, D_MODEL, D_MODEL)
IN_WIDTH = sum(IN_SIZES)


def _split_offsets(sizes):
    offs, acc = [], 0
    for s in sizes[:-1]:
        acc += s
        offs.append(acc)
    return offs

def rms_norm(x, w=None):
    xf = x.astype(jnp.float32)
    y = xf * lax.rsqrt(jnp.mean(jnp.square(xf), axis=-1, keepdims=True) + EPS)
    if w is not None:
        y = y * w.astype(jnp.float32)
    return y.astype(x.dtype)

def gated_group_rms_norm(y, z, w, groups):
    g = y.astype(jnp.float32) * jax.nn.silu(z.astype(jnp.float32))
    gs = g.reshape(*g.shape[:-1], groups, -1)
    gs = gs * lax.rsqrt(jnp.mean(jnp.square(gs), axis=-1, keepdims=True) + EPS)
    return (gs.reshape(g.shape) * w.astype(jnp.float32)).astype(y.dtype)

def sgu_branch(u, v, norm_w, ws, bs):
    b, s, _ = v.shape
    u = jax.nn.gelu(u)
    v = rms_norm(jax.nn.gelu(v), norm_w)
    vc = v.reshape(b, s // GM_CHUNK, GM_CHUNK, GM_GROUPS, GM_HEAD)
    causal = jnp.tril(jnp.ones((GM_CHUNK, GM_CHUNK), dtype=bool))
    ws_c = jnp.where(causal[None], ws, jnp.zeros_like(ws))
    sv = jnp.einsum('gij,bnjgd->bnigd', ws_c, vc) + bs.T[None, None, :, :, None]
    return u * sv.reshape(b, s, GM_WIDTH)

def ssd_scan(xs, dt, A, Bm, Cm):
    b, s, h, p = xs.shape
    g, n = Bm.shape[-2], Bm.shape[-1]
    hpg = h // g
    q = SSM_CHUNK
    nc = s // q

    def to_chunks(t):
        return jnp.swapaxes(t.reshape(b, nc, q, *t.shape[2:]), 0, 1)

    xdt = (xs.astype(jnp.float32) * dt[..., None]).reshape(b, s, g, hpg, p)
    a = (dt * A).reshape(b, s, g, hpg)
    causal = jnp.tril(jnp.ones((q, q), dtype=bool))

    def step(state, inp):
        x_c, a_c, B_c, C_c = inp
        cum = jnp.cumsum(a_c, axis=1)
        cum_t = jnp.moveaxis(cum, 1, -1)
        seg = cum_t[..., :, None] - cum_t[..., None, :]
        decay = jnp.exp(jnp.where(causal, seg, -jnp.inf))
        cb = jnp.einsum('bign,bjgn->bgij', C_c, B_c)
        y_intra = jnp.einsum('bgij,bghij,bjghp->bighp', cb, decay, x_c)
        y_inter = jnp.einsum('bign,bghpn->bighp', C_c, state) * jnp.exp(cum)[..., None]
        last = cum[:, -1]
        w_end = jnp.exp(last[:, None] - cum)
        new_state = state * jnp.exp(last)[..., None, None] + jnp.einsum(
            'bjgn,bjgh,bjghp->bghpn', B_c, w_end, x_c)
        return new_state, y_intra + y_inter

    state0 = jnp.zeros((b, g, hpg, p, n), jnp.float32)
    _, ys = lax.scan(step, state0, (to_chunks(xdt), to_chunks(a),
                                    to_chunks(Bm.astype(jnp.float32)),
                                    to_chunks(Cm.astype(jnp.float32))))
    return jnp.swapaxes(ys, 0, 1).reshape(b, s, h, p)

def ssd_branch(z, xbc, dt_raw, conv_w, conv_b, dt_bias, a_log, d_skip, norm_w):
    b, s, _ = xbc.shape
    xbc = lax.conv_general_dilated(
        xbc, conv_w[:, None, :], window_strides=(1,), padding=[(SSM_CONV - 1, 0)],
        dimension_numbers=('NWC', 'WIO', 'NWC'), feature_group_count=CONV_DIM) + conv_b
    xbc = jax.nn.silu(xbc)
    gn = SSM_GROUPS * SSM_STATE
    xs = xbc[..., :SSM_INNER].reshape(b, s, SSM_HEADS, SSM_HEAD_DIM)
    Bm = xbc[..., SSM_INNER:SSM_INNER + gn].reshape(b, s, SSM_GROUPS, SSM_STATE)
    Cm = xbc[..., SSM_INNER + gn:].reshape(b, s, SSM_GROUPS, SSM_STATE)
    dt = jax.nn.softplus(dt_raw.astype(jnp.float32) + dt_bias.astype(jnp.float32))
    A = -jnp.exp(a_log.astype(jnp.float32))
    y = ssd_scan(xs, dt, A, Bm, Cm)
    y = y + xs.astype(jnp.float32) * d_skip.astype(jnp.float32)[:, None]
    y = y.reshape(b, s, SSM_INNER).astype(z.dtype)
    return gated_group_rms_norm(y, z, norm_w, SSM_GROUPS)

def first_inputs(seed: int = 0) -> dict:
    key = jax.random.key(seed)
    ks = jax.random.split(key, 22)
    f = jnp.float32
    L = DEPTH

    def nrm(k, shape, fan_in):
        return jax.random.normal(k, shape, f) * (fan_in ** -0.5)

    x = jax.random.normal(ks[0], (BATCH, SEQ, D_MODEL), f)
    c = jax.random.normal(ks[1], (BATCH, D_MODEL), f)
    w_mod = 0.5 * nrm(ks[2], (L, D_MODEL, N_MOD * D_MODEL), D_MODEL)
    b_mod = 0.01 * jax.random.normal(ks[3], (L, N_MOD * D_MODEL), f)
    w_in = nrm(ks[4], (L, D_MODEL, IN_WIDTH), D_MODEL)
    gm_norm_w = 1.0 + 0.05 * jax.random.normal(ks[5], (L, GM_WIDTH), f)
    gm_ws = nrm(ks[6], (L, GM_GROUPS, GM_CHUNK, GM_CHUNK), GM_CHUNK)
    gm_bs = 1.0 + 0.1 * jax.random.normal(ks[7], (L, GM_GROUPS, GM_CHUNK), f)
    conv_w = nrm(ks[8], (L, SSM_CONV, CONV_DIM), SSM_CONV)
    conv_b = 0.01 * jax.random.normal(ks[9], (L, CONV_DIM), f)
    dt0 = jnp.exp(jax.random.uniform(ks[10], (L, SSM_HEADS), f,
                                     minval=math.log(1e-3), maxval=math.log(1e-1)))
    dt_bias = dt0 + jnp.log(-jnp.expm1(-dt0))
    a_log = jnp.log(jax.random.uniform(ks[11], (L, SSM_HEADS), f, minval=1.0, maxval=16.0))
    d_skip = 1.0 + 0.1 * jax.random.normal(ks[12], (L, SSM_HEADS), f)
    ssm_norm_w = 1.0 + 0.05 * jax.random.normal(ks[13], (L, SSM_INNER), f)
    w_branch_gm = nrm(ks[14], (L, GM_WIDTH, D_MODEL), GM_WIDTH)
    w_branch_ssm = nrm(ks[15], (L, SSM_INNER, D_MODEL), SSM_INNER)
    w_out = nrm(ks[16], (L, D_MODEL, D_MODEL), D_MODEL)
    w_ff1 = nrm(ks[17], (L, D_MODEL, D_FF), D_MODEL)
    w_ff2 = nrm(ks[18], (L, D_FF, D_MODEL), D_FF)
    final_norm_w = 1.0 + 0.05 * jax.random.normal(ks[19], (D_MODEL,), f)
    return {'x': x, 'c': c, 'w_mod': w_mod, 'b_mod': b_mod, 'w_in': w_in,
            'gm_norm_w': gm_norm_w, 'gm_ws': gm_ws, 'gm_bs': gm_bs,
            'conv_w': conv_w, 'conv_b': conv_b, 'dt_bias': dt_bias, 'a_log': a_log,
            'd_skip': d_skip, 'ssm_norm_w': ssm_norm_w, 'w_branch_gm': w_branch_gm,
            'w_branch_ssm': w_branch_ssm, 'w_out': w_out, 'w_ff1': w_ff1,
            'w_ff2': w_ff2, 'final_norm_w': final_norm_w}

def first_block(x, c, w_mod, b_mod, w_in, gm_norm_w, gm_ws, gm_bs, conv_w, conv_b,
              dt_bias, a_log, d_skip, ssm_norm_w, w_branch_gm, w_branch_ssm, w_out,
              w_ff1, w_ff2, final_norm_w):
    c_act = jax.nn.silu(c)
    offs = _split_offsets(IN_SIZES)
    for l in range(DEPTH):
        mod = (c_act @ w_mod[l] + b_mod[l])[:, None, :]
        sh1, sc1, g1, sh2, sc2, g2 = jnp.split(mod, N_MOD, axis=-1)
        h = rms_norm(x) * (1.0 + sc1) + sh1
        proj = h @ w_in[l]
        u, v, z, xbc, dt_raw, gate_a, gate_b = jnp.split(proj, offs, axis=-1)
        y_a = sgu_branch(u, v, gm_norm_w[l], gm_ws[l], gm_bs[l])
        y_b = ssd_branch(z, xbc, dt_raw, conv_w[l], conv_b[l], dt_bias[l], a_log[l],
                         d_skip[l], ssm_norm_w[l])
        mixed = (jax.nn.sigmoid(gate_a) * (y_a @ w_branch_gm[l])
                 + jax.nn.sigmoid(gate_b) * (y_b @ w_branch_ssm[l]))
        x = x + g1 * (mixed @ w_out[l])
        h2 = rms_norm(x) * (1.0 + sc2) + sh2
        x = x + g2 * (jnp.square(jax.nn.relu(h2 @ w_ff1[l])) @ w_ff2[l])
    return rms_norm(x, final_norm_w)


DEPTH_2 = 2

N_MIXERS = 3
D_FF_2 = 2816
LN_EPS = 1e-5
DEEPNORM_ALPHA = (2 * DEPTH_2) ** 0.25
DEEPNORM_BETA = (8 * DEPTH_2) ** -0.25
A_HEADS = 8
A_HEAD_DIM = D_MODEL // A_HEADS
MOBA_BLOCK = 256
MOBA_TOPK = 3
MOBA_Q_CHUNK = 32
REL_BUCKETS = 32
REL_MAX_EXACT = REL_BUCKETS // 2
REL_MAX_DIST = 128
POOL_WINDOWS = (2, 4, 8, 16)
POOL_GROUP = D_MODEL // len(POOL_WINDOWS)
C_HEADS = 4
C_HEAD_DIM = D_MODEL // C_HEADS
C_CONV = 4
C_CHUNK = 64
N_A = len(range(0, DEPTH_2, N_MIXERS))
N_B = len(range(1, DEPTH_2, N_MIXERS))
N_C = len(range(2, DEPTH_2, N_MIXERS))


def layer_norm(x, g, b):
    xf = x.astype(jnp.float32)
    mu = jnp.mean(xf, axis=-1, keepdims=True)
    var = jnp.mean(jnp.square(xf - mu), axis=-1, keepdims=True)
    y = (xf - mu) * lax.rsqrt(var + LN_EPS)
    return (y * g.astype(jnp.float32) + b.astype(jnp.float32)).astype(x.dtype)

def swiglu(x, w_gu, w_down):
    g, u = jnp.split(x @ w_gu, 2, axis=-1)
    return (jax.nn.silu(g) * u) @ w_down

def t5_bucket(dist):
    n = jnp.maximum(dist, 0)
    is_small = n < REL_MAX_EXACT
    nf = jnp.maximum(n, 1).astype(jnp.float32)
    large = REL_MAX_EXACT + (jnp.log(nf / REL_MAX_EXACT) / math.log(REL_MAX_DIST / REL_MAX_EXACT)
                             * (REL_BUCKETS - REL_MAX_EXACT)).astype(jnp.int32)
    large = jnp.minimum(large, REL_BUCKETS - 1)
    return jnp.where(is_small, n, large)

def moba_attention(h, w_in, w_out, rel_bias):
    B, S, _ = h.shape
    H, dh, blk, qcs = A_HEADS, A_HEAD_DIM, MOBA_BLOCK, MOBA_Q_CHUNK
    qkv = (h @ w_in).reshape(B, S, 3, H, dh)
    q, k, v = [jnp.transpose(qkv[:, :, j], (0, 2, 1, 3)) for j in range(3)]
    nb = -(-S // blk)
    pad = nb * blk - S
    kb = jnp.pad(k, ((0, 0), (0, 0), (0, pad), (0, 0))).reshape(B, H, nb, blk, dh)
    vb = jnp.pad(v, ((0, 0), (0, 0), (0, pad), (0, 0))).reshape(B, H, nb, blk, dh)
    q_block = jnp.arange(S) // blk
    n_sel = min(MOBA_TOPK, nb - 1)
    scale = dh ** -0.5
    rel_t = rel_bias.T
    bi = jnp.arange(B)[:, None, None, None]
    hi = jnp.arange(H)[None, :, None, None]
    if n_sel > 0:
        k_mean = jnp.mean(kb.astype(jnp.float32), axis=3)
        gate = jnp.einsum('bhsd,bhnd->bhsn', q.astype(jnp.float32), k_mean)
        past = jnp.arange(nb)[None, :] < q_block[:, None]
        gate = jnp.where(past, gate, -jnp.inf)
        _, top_idx = lax.top_k(gate, n_sel)
        top_valid = top_idx < q_block[:, None]

    def chunk_attend(c):
        start = c * qcs
        qc = lax.dynamic_slice_in_dim(q, start, qcs, axis=2)
        qpos = start + jnp.arange(qcs)
        j = start // blk
        ko = lax.dynamic_index_in_dim(kb, j, axis=2, keepdims=False)
        vo = lax.dynamic_index_in_dim(vb, j, axis=2, keepdims=False)
        kpos = j * blk + jnp.arange(blk)
        dist = qpos[:, None] - kpos[None, :]
        bias_own = jnp.transpose(rel_bias[t5_bucket(dist)], (2, 0, 1))
        s_own = jnp.einsum('bhqd,bhkd->bhqk', qc, ko) * scale + bias_own
        s_own = jnp.where(dist >= 0, s_own, -jnp.inf).astype(jnp.float32)
        if n_sel > 0:
            idx = lax.dynamic_slice_in_dim(top_idx, start, qcs, axis=2)
            valid = lax.dynamic_slice_in_dim(top_valid, start, qcs, axis=2)
            kg = kb[bi, hi, idx]
            vg = vb[bi, hi, idx]
            kpos_sel = idx[..., None] * blk + jnp.arange(blk)
            bucket = t5_bucket(qpos[:, None, None] - kpos_sel)
            s_sel = jnp.einsum('bhqd,bhqnkd->bhqnk', qc, kg) * scale + rel_t[hi[..., None], bucket]
            s_sel = jnp.where(valid[..., None], s_sel, -jnp.inf).astype(jnp.float32)
            logits = jnp.concatenate([s_own, s_sel.reshape(B, H, qcs, n_sel * blk)], axis=-1)
            p = jax.nn.softmax(logits, axis=-1).astype(v.dtype)
            out = (jnp.einsum('bhqk,bhkd->bhqd', p[..., :blk], vo)
                   + jnp.einsum('bhqnk,bhqnkd->bhqd', p[..., blk:].reshape(B, H, qcs, n_sel, blk), vg))
        else:
            p = jax.nn.softmax(s_own, axis=-1).astype(v.dtype)
            out = jnp.einsum('bhqk,bhkd->bhqd', p, vo)
        return out

    outs = lax.map(chunk_attend, jnp.arange(S // qcs))
    o = jnp.transpose(outs, (1, 0, 3, 2, 4)).reshape(B, S, H * dh)
    return o @ w_out

def pool_mixer(h, w_in, w_group, scale, w_out):
    B, S, _ = h.shape
    u = h @ w_in
    counts = jnp.arange(1, S + 1, dtype=jnp.float32)
    pooled = []
    for g, w in enumerate(POOL_WINDOWS):
        ug = u[..., g * POOL_GROUP:(g + 1) * POOL_GROUP].astype(jnp.float32)
        cs = jnp.cumsum(ug, axis=1)
        cs_lag = jnp.pad(cs, ((0, 0), (w, 0), (0, 0)))[:, :S]
        mean = (cs - cs_lag) / jnp.minimum(counts, float(w))[:, None]
        pooled.append(mean - ug)
    p = jnp.stack(pooled, axis=2).astype(h.dtype)
    y = jnp.einsum('bsgc,gcd->bsgd', p, w_group).reshape(B, S, D_MODEL) * scale
    return y @ w_out

def causal_conv(x, w):
    S = x.shape[1]
    xp = jnp.pad(x, ((0, 0), (C_CONV - 1, 0), (0, 0)))
    y = w[0] * xp[:, 0:S]
    for j in range(1, C_CONV):
        y = y + w[j] * xp[:, j:j + S]
    return y

def mlstm_chunkwise(q, k, v, i_pre, log_f):
    B, H, S, dh = q.shape
    L = C_CHUNK
    nc = S // L

    def to_chunks(t):
        return jnp.moveaxis(t.reshape((B, H, nc, L) + t.shape[3:]), 2, 0)

    qc, kc, vc, ic = to_chunks(q), to_chunks(k), to_chunks(v), to_chunks(i_pre)
    bc = jnp.cumsum(to_chunks(log_f), axis=-1)
    causal = jnp.tril(jnp.ones((L, L), dtype=bool))

    def step(carry, xs):
        C, n, m = carry
        qx, kx, vx, ix, bx = xs
        d_intra = jnp.where(causal, bx[..., :, None] - bx[..., None, :] + ix[..., None, :], -jnp.inf)
        m_inter = bx + m[..., None]
        m_t = jnp.maximum(m_inter, jnp.max(d_intra, axis=-1))
        w = jnp.exp(d_intra - m_t[..., None]) * jnp.einsum('bhtd,bhsd->bhts', qx, kx)
        s_inter = jnp.exp(m_inter - m_t)
        num = s_inter[..., None] * jnp.einsum('bhtk,bhkv->bhtv', qx, C) + jnp.einsum('bhts,bhsv->bhtv', w, vx)
        den = s_inter * jnp.einsum('bhtk,bhk->bht', qx, n) + jnp.sum(w, axis=-1)
        h = num / jnp.maximum(jnp.abs(den), jnp.exp(-m_t))[..., None]
        b_last = bx[..., -1]
        g = b_last[..., None] - bx + ix
        m_new = jnp.maximum(b_last + m, jnp.max(g, axis=-1))
        decay = jnp.exp(b_last + m - m_new)
        wk = jnp.exp(g - m_new[..., None])
        C = decay[..., None, None] * C + jnp.einsum('bhsk,bhsv->bhkv', kx * wk[..., None], vx)
        n = decay[..., None] * n + jnp.einsum('bhs,bhsk->bhk', wk, kx)
        return (C, n, m_new), h

    init = (jnp.zeros((B, H, dh, dh), jnp.float32), jnp.zeros((B, H, dh), jnp.float32),
            jnp.zeros((B, H), jnp.float32))
    _, hs = lax.scan(step, init, (qc, kc, vc, ic, bc))
    return jnp.moveaxis(hs, 0, 2).reshape(B, H, S, dh)

def mlstm_mixer(h, w_in, b_gates, conv_w, norm_g, w_out):
    B, S, _ = h.shape
    H, dh, D = C_HEADS, C_HEAD_DIM, D_MODEL
    proj = h @ w_in
    qk = jax.nn.silu(causal_conv(proj[..., :2 * D], conv_w))
    v = proj[..., 2 * D:3 * D]
    o_pre = proj[..., 3 * D:4 * D]
    gates = (proj[..., 4 * D:] + b_gates).astype(jnp.float32)

    def heads(t):
        return jnp.transpose(t.reshape(B, S, H, dh).astype(jnp.float32), (0, 2, 1, 3))

    i_pre = jnp.transpose(gates[..., :H], (0, 2, 1))
    log_f = jnp.transpose(jax.nn.log_sigmoid(gates[..., H:]), (0, 2, 1))
    ht = mlstm_chunkwise(heads(qk[..., :D]), heads(qk[..., D:]) * dh ** -0.5, heads(v), i_pre, log_f)
    ht = jnp.transpose(ht, (0, 2, 1, 3))
    hc = jax.nn.sigmoid(o_pre.astype(jnp.float32)).reshape(B, S, H, dh) * ht
    mu = jnp.mean(hc, axis=-1, keepdims=True)
    var = jnp.mean(jnp.square(hc - mu), axis=-1, keepdims=True)
    hn = ((hc - mu) * lax.rsqrt(var + LN_EPS)).reshape(B, S, D) * norm_g.astype(jnp.float32)
    return hn.astype(h.dtype) @ w_out

def second_inputs(seed: int = 0) -> dict:
    key = jax.random.key(seed)
    ks = jax.random.split(key, 18)
    D, H, GC = D_MODEL, C_HEADS, POOL_GROUP

    def nrm(k, shape, std):
        return jax.random.normal(k, shape, jnp.float32) * std

    x = nrm(ks[0], (BATCH, SEQ, D), 1.0)
    rel_bias = nrm(ks[1], (REL_BUCKETS, A_HEADS), 0.2)
    ln_g = 1.0 + nrm(ks[2], (DEPTH_2, 3, D), 0.02)
    ln_b = nrm(ks[3], (DEPTH_2, 3, D), 0.02)
    ffn_w_gu = nrm(ks[4], (DEPTH_2, 2, D, 2 * D_FF_2), D ** -0.5)
    ffn_w_down = nrm(ks[5], (DEPTH_2, 2, D_FF_2, D), D_FF_2 ** -0.5 * DEEPNORM_BETA)
    a_w_in = nrm(ks[6], (N_A, D, 3 * D), D ** -0.5)
    a_w_out = nrm(ks[7], (N_A, D, D), D ** -0.5 * DEEPNORM_BETA)
    b_w_in = nrm(ks[8], (N_B, D, D), D ** -0.5)
    b_w_group = nrm(ks[9], (N_B, len(POOL_WINDOWS), GC, GC), GC ** -0.5)
    b_scale = 1.0 + nrm(ks[10], (N_B, D), 0.1)
    b_w_out = nrm(ks[11], (N_B, D, D), D ** -0.5 * DEEPNORM_BETA)
    c_w_in = nrm(ks[12], (N_C, D, 4 * D + 2 * H), D ** -0.5)
    c_b_gates = jnp.concatenate([nrm(ks[13], (N_C, H), 0.1),
                                 jnp.linspace(3.0, 6.0, H, dtype=jnp.float32)[None, :] + nrm(ks[14], (N_C, H), 0.1)],
                                axis=-1)
    c_conv_w = nrm(ks[15], (N_C, C_CONV, 2 * D), C_CONV ** -0.5)
    c_norm_g = 1.0 + nrm(ks[16], (N_C, D), 0.02)
    c_w_out = nrm(ks[17], (N_C, D, D), D ** -0.5 * DEEPNORM_BETA)
    return {"x": x, "rel_bias": rel_bias, "ln_g": ln_g, "ln_b": ln_b,
            "ffn_w_gu": ffn_w_gu, "ffn_w_down": ffn_w_down,
            "a_w_in": a_w_in, "a_w_out": a_w_out,
            "b_w_in": b_w_in, "b_w_group": b_w_group, "b_scale": b_scale, "b_w_out": b_w_out,
            "c_w_in": c_w_in, "c_b_gates": c_b_gates, "c_conv_w": c_conv_w, "c_norm_g": c_norm_g,
            "c_w_out": c_w_out}

def second_block(x, rel_bias, ln_g, ln_b, ffn_w_gu, ffn_w_down, a_w_in, a_w_out,
              b_w_in, b_w_group, b_scale, b_w_out,
              c_w_in, c_b_gates, c_conv_w, c_norm_g, c_w_out):
    for i in range(DEPTH_2):
        x = layer_norm(DEEPNORM_ALPHA * x + 0.5 * swiglu(x, ffn_w_gu[i, 0], ffn_w_down[i, 0]),
                       ln_g[i, 0], ln_b[i, 0])
        kind, j = i % N_MIXERS, i // N_MIXERS
        if kind == 0:
            y = moba_attention(x, a_w_in[j], a_w_out[j], rel_bias)
        elif kind == 1:
            y = pool_mixer(x, b_w_in[j], b_w_group[j], b_scale[j], b_w_out[j])
        else:
            y = mlstm_mixer(x, c_w_in[j], c_b_gates[j], c_conv_w[j], c_norm_g[j], c_w_out[j])
        x = layer_norm(DEEPNORM_ALPHA * x + y, ln_g[i, 1], ln_b[i, 1])
        x = layer_norm(DEEPNORM_ALPHA * x + 0.5 * swiglu(x, ffn_w_gu[i, 1], ffn_w_down[i, 1]),
                       ln_g[i, 2], ln_b[i, 2])
    return x


def setup_inputs(seed=0):
    out = dict(first_inputs(seed))
    for name, value in second_inputs(seed + 1).items():
        if name != "x":
            out[name + "_2"] = value
    return out


def reference(
    x, c, w_mod, b_mod, w_in, gm_norm_w, gm_ws, gm_bs, conv_w, conv_b, dt_bias, a_log, d_skip,
    ssm_norm_w, w_branch_gm, w_branch_ssm, w_out, w_ff1, w_ff2, final_norm_w, rel_bias_2,
    ln_g_2, ln_b_2, ffn_w_gu_2, ffn_w_down_2, a_w_in_2, a_w_out_2, b_w_in_2, b_w_group_2,
    b_scale_2, b_w_out_2, c_w_in_2, c_b_gates_2, c_conv_w_2, c_norm_g_2, c_w_out_2,
):
    x = first_block(
        x, c, w_mod, b_mod, w_in, gm_norm_w, gm_ws, gm_bs, conv_w, conv_b, dt_bias, a_log,
        d_skip, ssm_norm_w, w_branch_gm, w_branch_ssm, w_out, w_ff1, w_ff2, final_norm_w,
    )
    return second_block(
        x, rel_bias_2, ln_g_2, ln_b_2, ffn_w_gu_2, ffn_w_down_2, a_w_in_2, a_w_out_2, b_w_in_2,
        b_w_group_2, b_scale_2, b_w_out_2, c_w_in_2, c_b_gates_2, c_conv_w_2, c_norm_g_2,
        c_w_out_2,
    )


_drawn_inputs = setup_inputs


def setup_inputs(seed=0):
    import zlib

    import numpy as np

    out = dict(_drawn_inputs(seed))
    spreads = {}
    factors = {'b_mod': 3.4,
     'gm_norm_w': 22.004,
     'gm_bs': 4.761,
     'conv_b': 8.0,
     'd_skip': 6.682,
     'ssm_norm_w': 6.571,
     'rel_bias_2': 4.799}
    for name, (base, spread) in spreads.items():
        noise = np.random.default_rng([zlib.crc32(name.encode()), seed]).standard_normal(out[name].shape)
        drawn = base * np.exp(spread * noise) if base else spread * noise
        out[name] = jnp.asarray(drawn.astype(out[name].dtype))
    for name, factor in factors.items():
        out[name] = (out[name] * factor).astype(out[name].dtype)
    return out
```

```python
import concourse.bass as bass
from concourse import mybir
from contextlib import ExitStack

F32 = mybir.dt.float32
F32R = mybir.dt.float32r
ACT = mybir.ActivationFunctionType
ALU = mybir.AluOpType
AX = mybir.AxisListType

P = 128
T = 256
TT = T // P
D = 1024
KD = D // P
CHUNK = 512
PANEL = 4 * CHUNK
BANKS = 4
RAW = 4
SPLIT = 2
EPS = 1e-6
LN_EPS = 1e-5
ALPHA = (2 * 2) ** 0.25
HEADS = 8
HEAD_DIM = 128
SCALE = HEAD_DIM ** -0.5
SSM_HEADS = 32
HP = 64
SSM_GROUPS = 8
CONV = 4
WINDOWS = (2, 4, 8, 16)
MASKED = -1e30
BIAS_COLS = 2 * T

STAGES = (
    ("mod_norm", 8, 4, "mod"), ("u", 8, 2, "act"), ("v", 8, 2, "act"), ("gate_a", 8, 2, "act"),
    ("gate_b", 8, 2, "act"), ("branch_gm", 8, 2, "gate"), ("xbc", 8, 8, "conv"), ("z", 8, 4, "act"),
    ("mod_rest", 8, 8, "mod"), ("branch_ssm", 16, 2, "mix"), ("out", 8, 2, "add1"),
    ("ff1", 8, 8, "relu2"), ("ff2", 32, 2, "add1"),
    ("gu0", 8, 11, "glu"), ("down0", 22, 2, "deep"), ("qkv", 8, 6, "keep"), ("att_out", 8, 2, "deep"),
    ("gu1", 8, 11, "glu"), ("down1", 22, 2, "deep"), ("gu2", 8, 11, "glu"), ("down2", 22, 2, "deep"),
    ("pool_in", 8, 2, "keep"), ("pool_group", 2, 2, "scale"), ("pool_out", 8, 2, "deep"),
    ("gu3", 8, 11, "glu"), ("down3", 22, 2, "deep"),
)
INDEX = {s[0]: n for n, s in enumerate(STAGES)}
_ALL = ("mod", "act", "gate", "conv", "mix", "add1", "relu2", "glu", "deep", "keep", "scale")
COUNTED = {
    "corrected": _ALL[1:],
    "summed": _ALL,
    "activated": ("act", "conv", "glu"),
    "posted": ("gate", "conv", "mix", "add1", "relu2", "glu", "deep", "scale"),
    "operand": ("mix", "relu2", "glu", "scale"),
}


def panels_of(stage):
    name, kb, groups, kind = stage
    return kb * groups // 4


def before(sem, stage):
    return sum(s[2] for s in STAGES[:stage] if s[3] in COUNTED[sem])


FIRST_PANEL = [sum(map(panels_of, STAGES[:n])) for n in range(len(STAGES) + 1)]
FIRST_GROUP = [sum(s[2] for s in STAGES[:n]) for n in range(len(STAGES) + 1)]
PANELS = FIRST_PANEL[-1]

COLS, _at = {}, 0
for _name, _n in (("b_mod", 48), ("gm_norm", 8), ("conv_b", 32), ("conv_w", 32 * CONV), ("ssm_norm", 16),
                  ("final", 8), ("ln_g", 48), ("ln_b", 48), ("pool_scale", 8), ("d_skip", 16)):
    COLS[_name] = _at
    _at += _n
NCOLS = _at


def two_blocks(nc, panels, x_in, c_in, cols_in, heads_in, ws_in, bs_in, wdt_in, rel_in, onehot_in, inv_in,
               skew, out):
    ctx = ExitStack()
    with ctx:
        def sb(name, shape, dt=F32, stack=ctx):
            return stack.enter_context(nc.sbuf_tensor(name, shape, dt))

        raw = sb("raw", [P, RAW, PANEL])
        w_hi = sb("w_hi", [P, SPLIT, PANEL], F32R)
        w_lo = sb("w_lo", [P, SPLIT, PANEL], F32R)
        ev = sb("ev", [P, 2, BANKS, T])
        XS = sb("XS", [P, KD, 2, T])
        st = sb("st", [P, 4, T])
        ident = sb("ident", [P, P])
        ident_r = sb("ident_r", [32, 32], F32R)
        ones = sb("ones", [P, P])
        mean_w = sb("mean_w", [P, P])
        gmean_w = sb("gmean_w", [P, P])
        cols = sb("cols", [P, NCOLS])
        tiny = sb("tiny", [P, 2])
        mod = sb("mod", [P, 48])
        phase = ExitStack()
        H = sb("H", [P, KD, 2, T], F32R, phase)
        u_t = sb("u_t", [P, KD, T], F32, phase)
        v_t = sb("v_t", [P, KD, T], F32, phase)
        gate_a = sb("gate_a", [P, KD, T], F32, phase)
        gate_b = sb("gate_b", [P, KD, T], F32, phase)
        early = ExitStack()
        ws = sb("ws", [P, KD, P], F32, early)
        bs = sb("bs", [1, KD * P], F32, early)
        v_nat = sb("v_nat", [P, KD, TT, P], F32, early)
        YA = sb("YA", [P, KD, 2, T], F32R, early)
        mod_row = sb("mod_row", [2, 4 * CHUNK], F32, early)
        c_f = sb("c_f", [P, KD], F32, early)
        c_s = sb("c_s", [P, KD], F32, early)
        rel = sb("rel", [33, HEADS], F32, early)
        onehot = sb("onehot", [33, BIAS_COLS], F32, early)
        early.close()
        after_ssd = ExitStack()
        mod_row2 = sb("mod_row2", [2, 8 * CHUNK], F32, after_ssd)
        MX = sb("MX", [P, KD, 2, T], F32R, after_ssd)
        after_ssd.close()
        xbc = sb("xbc", [P, 32, T], F32, phase)
        conv_stack = ExitStack()
        pad = sb("pad", [P, BANKS, T + 4], F32, conv_stack)
        conv_stack.close()
        z_t = sb("z_t", [P, 16, T], F32, phase)
        tri = sb("tri", [P, P], F32, phase)
        heads = sb("heads", [P, 2, 32], F32, phase)
        c_r = sb("c_r", [P, KD, P], F32R, phase)
        dt_stack = ExitStack()
        wdt = sb("wdt", [P, KD, 32], F32, dt_stack)
        wdt_r = sb("wdt_r", [P, KD, 2, 32], F32R, dt_stack)
        dt_stack.close()
        cb = sb("cb", [P, 2, 3 * P], F32, phase)
        dtv = sb("dtv", [P, 5, TT, 32], F32, phase)
        ea = sb("ea", [P, 32], F32, phase)
        cum_r = sb("cum_r", [32, 2, T], F32R, phase)
        phase.close()
        rev_stack = ExitStack()
        for k in range(2):
            sb(f"rev_skip{k}", [P, 2 * KD, T], F32, rev_stack)
        rev = sb("rev", [P, HEADS, BIAS_COLS], F32, rev_stack)
        rev_stack.close()
        yb_stack = ExitStack()
        YB = sb("YB", [P, 16, 2, T], F32R, yb_stack)
        yb_stack.close()
        second = ExitStack()
        sb("H_again", [P, KD, 2, T], F32, second)
        near = sb("near", [P, HEADS, T], F32, second)
        mlp = ExitStack()
        HH = sb("HH", [P, 32, 2, T], F32R, mlp)
        mlp.close()
        attn = ExitStack()
        qkv = sb("qkv", [P, 24, T], F32, attn)
        v_tok = sb("v_tok", [P, TT, D], F32, attn)
        probs = sb("probs", [P, 2, 3 * P], F32, attn)
        probs_t = sb("probs_t", [P, 2, 3 * P], F32, attn)
        sm = sb("sm", [P, HEADS, 8], F32, attn)
        o_t = sb("o_t", [P, 2, T], F32, attn)
        attn.close()
        pooling = ExitStack()
        PG = sb("PG", [P, KD, 2, T], F32R, pooling)
        pu = sb("pu", [P, KD, T], F32, pooling)
        pw = sb("pw", [P, 4, KD, T], F32, pooling)
        pooled = sb("pooled", [P, KD, T], F32, pooling)
        pooling.close()
        inv_stack = ExitStack()
        sb("inv_skip", [P, 32, 2, T], F32, inv_stack)
        inv = sb("inv", [P, 4, 16], F32, inv_stack)
        inv_stack.close()
        second.close()

        banks = ctx.enter_context(nc.psum_tensor("banks", [P, 2 * BANKS, CHUNK], F32))

        def sem(name):
            return ctx.enter_context(nc.semaphore(name))

        loaded = [sem(f"panel_loaded_{r}") for r in range(RAW)]
        panel_hi, panel_lo, panel_used = sem("panel_hi"), sem("panel_lo"), sem("panel_used")
        corrected, summed, activated = sem("corrected"), sem("summed"), sem("activated")
        posted, operand_hi, operand_lo = sem("posted"), sem("operand_hi"), sem("operand_lo")
        act_step = sem("act_step")
        vec_step = sem("vec_step")
        S = {n: sem(n) for n in (
            "x_loaded params_loaded c_loaded late_loaded consts_ready c_silu c_hi c_lo c_zero mod_cols mod_ready "
            "squares stat_sums stat_var stat_root norm_y norm_hi norm_lo ident_r_ready "
            "sgu_vn sgu_vt sgu_vcopy sgu_mix sgu_y sgu_hi sgu_lo ws_masked "
            "wdt_hi wdt_lo dt_raw dt_corr dt_y dt_exp dt_one dt_ln dt_ea dt_a cum_done cum_got cum_hi cum_lo "
            "cb_done cb_copied cb_masked xt_done xdt_done row_done seg_done exp_done m_done y_done "
            "y_gated y_sq y_sums y_var y_root y_f y_hi y_lo "
            "rel_loaded rel_masked rev_done rev_copied rev_stored near_loaded "
            "vt_done v_copied s_done s_biased s_max conv_tap tiny_set p_exp p_norm pt_done pt_copied o_done o_copied o_hi o_lo "
            "pool_hi pool_lo pool_f inv_loaded x_stored").split()}

        block = ctx.enter_context(nc.Block())
        xb = XS[:, :, 0, :]
        conv_w = cols[:, COLS["conv_w"]:COLS["conv_w"] + 32 * CONV].rearrange("p (g n) -> p g n", n=BANKS * CONV)
        conv_b = cols[:, COLS["conv_b"]:COLS["conv_b"] + 32].rearrange("p (g b) -> p g b", b=BANKS)
        sq = XS[:, :, 1, :]
        ev8 = ev[:, :, :, :].rearrange("p a b t -> p (a b) t")

        def decay(n):
            flat = ev[:, :, :, :].rearrange("p a b t -> p (a b t)")
            return flat[:, n % 2 * 6 * P:(n % 2 + 1) * 6 * P]

        def xdt(g, t):
            return XS[:, 4 + 2 * (g % 2) + t, 1, :]

        def stat_bank(stage):
            return 0 if stage is None else BANKS * (FIRST_GROUP[INDEX[stage] + 1] % 2)

        def by_group(t):
            return t.rearrange("p (g b) t -> p g b t", b=BANKS)

        def need(eng, s, value):
            if not (isinstance(value, int) and value <= 0):
                eng.wait_ge(s, value)

        def groups(eng, s, body):
            n = STAGES[s][2]
            if n >= 4 and s:
                with eng.Fori(0, n // 2) as turn:
                    body(2 * turn, 0, turn)
                    body(2 * turn + 1, 1, turn)
                if n % 2:
                    body(n - 1, 0, None)
            else:
                for g in range(n):
                    body(g, g % 2, None)

        def split_slot(s, u, p):
            return (FIRST_PANEL[s] + 2 * u + p) % SPLIT

        def ahead(s, g, u, turn, p):
            q = FIRST_PANEL[s] + 2 * g + p + SPLIT
            place = FIRST_PANEL[s] + 2 * u + p + SPLIT
            if turn is None:
                return q, q % RAW, q % SPLIT, q // RAW
            return q, place % RAW, place % SPLIT, turn + place // RAW

        def through(s, g):
            kb = STAGES[s][1]
            return FIRST_PANEL[s] + (2 * g + 2 if kb == 8 else -(-kb * (g + 1) // 4))

        def run(eng, s, split, take_up):
            kb, n = STAGES[s][1:3]
            if kb == 8:
                def body(g, u, turn):
                    for p in range(2):
                        split(*ahead(s, g, u, turn, p))
                    take_up(s, g, (FIRST_GROUP[s] + u) % 2)
                groups(eng, s, body)
                return
            for q in range(FIRST_PANEL[s], FIRST_PANEL[s + 1]):
                a = q + SPLIT
                if a < PANELS:
                    split(a, a % RAW, a % SPLIT, a // RAW)
                for g in range(n):
                    if through(s, g) == q + 1:
                        take_up(s, g, (FIRST_GROUP[s] + g) % 2)

        @block.sync
        def _(sp):
            sp.dma_start(cols[:, :], cols_in).then_inc(S["params_loaded"], 16)
            sp.dma_start(c_f[:, :], c_in).then_inc(S["c_loaded"], 16)
            sp.dma_start(raw[:, 0, :], panels[0]).then_inc(loaded[0], 16)
            sp.dma_start(raw[:, 1, :], panels[1]).then_inc(loaded[1], 16)
            sp.dma_start(xb, x_in).then_inc(S["x_loaded"], 16)
            for r in range(2, RAW):
                sp.dma_start(raw[:, r, :], panels[r]).then_inc(loaded[r], 16)

            def refill(n, r):
                sp.wait_ge(panel_lo, 2 * (RAW * n + r - RAW + 1))
                sp.dma_start(raw[:, r, :], panels[RAW * n + r]).then_inc(loaded[r], 16)

            with sp.Fori(1, PANELS // RAW) as n:
                for r in range(RAW):
                    refill(n, r)
            for q in range(PANELS // RAW * RAW, PANELS):
                refill(q // RAW, q % RAW)
            sp.wait_ge(S["norm_y"], KD * 9)
            sp.dma_start(out, xb).then_inc(S["x_stored"], 16)
            sp.wait_ge(S["x_stored"], 16)

        @block.gpsimd
        def _(pool):
            pool.memset(c_r[:, :, :].bitcast(F32), 0.0).then_inc(S["c_zero"], 1)
            pool.memset(ident[:, :], 0.0).then_inc(S["consts_ready"], 1)
            pool.memset(ones[:, :], 1.0).then_inc(S["consts_ready"], 1)
            pool.memset(mean_w[:, :], 1.0 / D).then_inc(S["consts_ready"], 1)
            pool.memset(gmean_w[:, :], 1.0 / T).then_inc(S["consts_ready"], 1)
            pool.memset(tri[:, :], 1.0).then_inc(S["consts_ready"], 1)
            pool.wait_ge(S["consts_ready"], 5)
            pool.affine_select(out=ident[:, :], in_=ident[:, :], compare_op=ALU.not_equal, fill=1.0,
                               base=0, pattern=[[-1, P]], channel_multiplier=1).then_inc(S["consts_ready"], 1)
            pool.affine_select(out=tri[:, :], in_=tri[:, :], compare_op=ALU.is_ge, fill=0.0,
                               base=0, pattern=[[1, P]], channel_multiplier=-1).then_inc(S["consts_ready"], 1)
            pool.dma_start(ws[:, :, :], ws_in).then_inc(S["late_loaded"], 16)
            pool.dma_start(bs[:, :], bs_in).then_inc(S["late_loaded"], 16)
            pool.dma_start(wdt[:, :, :], wdt_in).then_inc(S["late_loaded"], 16)
            pool.dma_start(heads[:, :, :], heads_in).then_inc(S["late_loaded"], 16)
            pool.wait_ge(S["late_loaded"], 64)
            pool.affine_select(out=ws[:, :, :], in_=ws[:, :, :], compare_op=ALU.is_ge, fill=0.0, base=0,
                               pattern=[[0, KD], [1, P]], channel_multiplier=-1).then_inc(S["ws_masked"], 1)
            pool.wait_ge(S["ws_masked"], 1)
            pool.memset(rel[32:33, :], MASKED).then_inc(S["rel_masked"], 1)
            pool.dma_start(rel[0:32, :], rel_in).then_inc(S["rel_loaded"], 16)
            pool.dma_start(onehot[:, :], onehot_in).then_inc(S["rel_loaded"], 16)
            pool.wait_ge(S["rev_copied"], HEADS)
            pool.dma_start(skew.rearrange("q (h t) -> q h t", t=BIAS_COLS), rev[:, :, :]).then_inc(S["rev_stored"], 16)
            pool.wait_ge(S["rev_stored"], 16)
            for g in range(SSM_GROUPS):
                pool.wait_ge(S["cb_copied"], g + 1)
                both = cb[:, g % 2, :].rearrange("p (a i) -> p a i", i=P)[:, 0:3:2, :]
                pool.affine_select(out=both, in_=both, compare_op=ALU.is_ge, fill=0.0, base=0,
                                   pattern=[[0, 2], [1, P]], channel_multiplier=-1).then_inc(S["cb_masked"], 1)
            pool.wait_ge(panel_used, FIRST_PANEL[INDEX["out"]])
            row = HEADS * BIAS_COLS - 1
            skewed = skew.rearrange("q n -> (q n)")[P - 1:P - 1 + P * row].rearrange("(q n) -> q n", n=row)
            for h in range(HEADS):
                pool.dma_start(near[:, h, :], skewed[:, h * BIAS_COLS:h * BIAS_COLS + T]).then_inc(S["near_loaded"], 16)
            pool.wait_ge(panel_used, FIRST_PANEL[INDEX["ff1"]])
            pool.dma_start(inv[:, :, :], inv_in).then_inc(S["inv_loaded"], 16)

        @block.tensor
        def _(pe):
            def products(group_u, panel_slot, operand, k, starts, stops, banks_of=range(BANKS), chunks=range(4)):
                for b in banks_of:
                    acc = banks[:, BANKS * group_u + b, :]
                    for c in chunks:
                        at = c * CHUNK + b * P
                        kk = k + c - chunks[0]
                        pair = operand[:, kk, :, :].rearrange("p a t -> p (a t)")
                        pe.matmul(acc, w_hi[:, panel_slot, at:at + P], pair,
                                  start=starts and c == chunks[0], stop=False)
                        last = pe.matmul(acc[:, 0:T], w_lo[:, panel_slot, at:at + P], pair[:, 0:T],
                                         start=False, stop=stops and c == chunks[-1])
                return last

            def psum_free(s, g):
                need(pe, summed, FIRST_GROUP[s] + g - 1)

            def stage_k8(name, operand, ready=None):
                s = INDEX[name]

                def body(g, u, turn):
                    for p in range(2):
                        pe.wait_ge(panel_lo, 2 * (FIRST_PANEL[s] + 2 * g + p + 1))
                        if p == 0:
                            psum_free(s, g)
                        if ready is not None and isinstance(g, int) and g == 0:
                            ready(4 * p + 4)
                        products((FIRST_GROUP[s] + u) % 2, split_slot(s, u, p), operand, 4 * p, p == 0, p == 1)\
                            .then_inc(panel_used, 1)

                groups(pe, s, body)

            def operand_of(name, blocks):
                return lambda k: pe.wait_ge(operand_lo, before("operand", INDEX[name]) + -(-k // blocks))

            def stage_long(name, operand, kb, ready):
                s = INDEX[name]
                for q in range(panels_of(STAGES[s])):
                    pe.wait_ge(panel_lo, 2 * (FIRST_PANEL[s] + q + 1))
                    parts = {}
                    for c in range(4):
                        parts.setdefault((4 * q + c) // kb, []).append(c)
                    for g, chunks in parts.items():
                        k = 4 * q + chunks[0] - g * kb
                        if k == 0:
                            psum_free(s, g)
                        if g == 0:
                            ready(k + len(chunks))
                        last = products((FIRST_GROUP[s] + g) % 2, (FIRST_PANEL[s] + q) % SPLIT, operand, k,
                                        k == 0, k + len(chunks) == kb, chunks=chunks)
                    last.then_inc(panel_used, 1)

            def stage_mod(name):
                s = INDEX[name]

                def body(g, u, turn):
                    acc = banks[:, BANKS * ((FIRST_GROUP[s] + u) % 2), :]
                    for p in range(2):
                        pe.wait_ge(panel_lo, 2 * (FIRST_PANEL[s] + 2 * g + p + 1))
                        if p == 0:
                            psum_free(s, g)
                        sl = split_slot(s, u, p)
                        for c in range(4):
                            w = slice(c * CHUNK, c * CHUNK + CHUNK)
                            pe.matmul(acc, c_r[:, 4 * p + c, :], w_hi[:, sl, w], start=p == 0 and c == 0, stop=False)
                            last = pe.matmul(acc, c_r[:, 4 * p + c, :], w_lo[:, sl, w], start=False,
                                             stop=p == 1 and c == 3)
                        last.then_inc(panel_used, 1)

                groups(pe, s, body)

            def mod_columns(rows, first, n, s):
                pe.wait_ge(summed, FIRST_GROUP[s + 1])
                for m in range(n):
                    last = pe.matmul(banks[:, 7, first + m:first + m + 1], rows[0:2, m * P:m * P + P],
                                     ones[0:2, 0:1], start=True, stop=True)
                last.then_inc(S["mod_cols"], 1)

            def stats(n, mean, stage=None):
                for m in range(KD):
                    if m % 4 == 0:
                        pe.wait_ge(S["squares"], 2 * n + m // 4 + 1)
                    rhs = XS[:, m, :, :].rearrange("p a t -> p (a t)") if mean else sq[:, m, :]
                    b = stat_bank(stage)
                    to = banks[:, b, :] if mean else banks[:, b, T:2 * T]
                    last = pe.matmul(to, mean_w[:, :], rhs, start=m == 0, stop=m == KD - 1)
                last.then_inc(S["stat_sums"], 1)

            def bias_rows():
                pe.wait_ge(S["rel_loaded"], 32)
                pe.wait_ge(S["rel_masked"], 1)
                for h in range(HEADS):
                    if h >= 2:
                        pe.wait_ge(S["rev_copied"], h - 1)
                    pe.matmul(banks[:, 1 + h % 2, :], rel[0:33, h:h + 1].to_broadcast([33, P]), onehot[:, :],
                              start=True, stop=True).then_inc(S["rev_done"], 1)

            pe.wait_ge(S["consts_ready"], 7)
            stats(0, False)
            bias_rows()
            pe.wait_ge(S["rev_copied"], HEADS)
            pe.wait_ge(S["c_lo"], 1)
            stage_mod("mod_norm")
            mod_columns(mod_row, 0, 16, INDEX["mod_norm"])
            pe.wait_ge(S["norm_lo"], 2)
            for name in ("u", "v", "gate_a", "gate_b"):
                stage_k8(name, H)

            pe.wait_ge(summed, FIRST_GROUP[INDEX["branch_gm"]])
            stats(1, False)
            for m in range(KD):
                if m % 4 == 0:
                    pe.wait_ge(S["sgu_vn"], m // 4 + 1)
                for t in range(TT):
                    last = pe.transpose(banks[:, 1 + m // 2, (m % 2 * TT + t) * P:(m % 2 * TT + t + 1) * P],
                                        v_t[:, m, t * P:t * P + P], ident[:, :])
                if m % 2:
                    last.then_inc(S["sgu_vt"], 1)
            pe.wait_ge(S["ws_masked"], 1)
            for m in range(KD):
                if m % 2 == 0:
                    pe.wait_ge(S["sgu_vcopy"], m // 2 + 1)
                for t in range(TT):
                    to = banks[:, (5, 6, 7, 0)[m // 2], (m % 2 * TT + t) * P:(m % 2 * TT + t + 1) * P]
                    pe.matmul(to, v_nat[:, m, t, :], ws[:, m, :], start=True, stop=False)
                    last = pe.matmul(to, ones[0:1, :], bs[0:1, m * P:m * P + P], start=False, stop=True)
                if m % 2:
                    last.then_inc(S["sgu_mix"], 1)
            stage_k8("branch_gm", YA, lambda k: pe.wait_ge(S["sgu_lo"], 4))
            stage_k8("xbc", H)
            stage_k8("z", H)

            pe.wait_ge(summed, FIRST_GROUP[INDEX["mod_rest"]])
            pe.wait_ge(S["wdt_lo"], 1)
            for t in range(TT):
                acc = banks[:, 4, t * 64:t * 64 + 64]
                for k in range(KD):
                    pe.matmul(acc, H[:, k, 0, t * P:t * P + P], wdt_r[:, k, :, :].rearrange("p a h -> p (a h)"),
                              start=k == 0, stop=False)
                    last = pe.matmul(acc[:, 0:32], H[:, k, 1, t * P:t * P + P], wdt_r[:, k, 0, :],
                                     start=False, stop=k == KD - 1)
            last.then_inc(S["dt_raw"], 1)
            a_v = dtv[:, 3, :, :]
            pe.wait_ge(S["dt_a"], 1)
            pe.matmul(banks[:, 5, 0:32], tri[:, :], a_v[:, 0, :], start=True, stop=True)
            pe.matmul(banks[:, 5, 32:64], ones[:, :], a_v[:, 0, :], start=True, stop=False)
            pe.matmul(banks[:, 5, 32:64], tri[:, :], a_v[:, 1, :], start=False, stop=True)
            pe.matmul(banks[0:32, 6, 0:P], a_v[:, 0, :], tri[:, :], start=True, stop=True)
            pe.matmul(banks[0:32, 6, P:T], a_v[:, 0, :], ones[:, :], start=True, stop=False)
            pe.matmul(banks[0:32, 6, P:T], a_v[:, 1, :], tri[:, :], start=False, stop=True)\
                .then_inc(S["cum_done"], 1)

            B = xbc[:, 16:24, :]
            C = xbc[:, 24:32, :]

            def scores_and_tokens(g):
                if g >= 2:
                    pe.wait_ge(S["cb_copied"], g - 1)
                pe.matmul(banks[:, g % 2, 0:T], B[:, g, 0:P], C[:, g, :], start=True, stop=True)
                pe.matmul(banks[:, g % 2, T:3 * P], B[:, g, P:T], C[:, g, P:T], start=True, stop=True)\
                    .then_inc(S["cb_done"], 1)
                if g:
                    pe.wait_ge(S["xdt_done"], 2 * g)
                for t in range(TT):
                    for m in range(2):
                        last = pe.transpose(banks[:, 2, (2 * t + m) * P:(2 * t + m + 1) * P],
                                            xbc[:, 2 * g + m, t * P:t * P + P], ident[:, :])
                last.then_inc(S["xt_done"], 1)

            def decay_rows(n):
                if n >= 2:
                    pe.wait_ge(S["seg_done"], 4 * (n - 1))
                for r in range(2):
                    h = 2 * n + r
                    pick = ident_r[:, h:h + 1].to_broadcast([32, P])
                    pe.matmul(banks[:, 3 + n % 2, r * T:r * T + T], pick, cum_r[:, 0, :], start=True, stop=False)
                    last = pe.matmul(banks[:, 3 + n % 2, r * T:r * T + T], pick, cum_r[:, 1, :], start=False, stop=True)
                last.then_inc(S["row_done"], 1)

            def head_outputs(n):
                g = n // 2
                pe.wait_ge(S["m_done"], n + 1)
                pe.wait_ge(S["xdt_done"], 2 * (g + 1))
                if n >= 2:
                    pe.wait_ge(S["y_gated"], n - 1)
                m_of = decay(n)
                for r in range(2):
                    to = banks[HP * r:HP * r + HP, 5 + n % 2, 0:T]
                    cut = slice((n % 2 * 2 + r) * HP, (n % 2 * 2 + r + 1) * HP)
                    pe.matmul(to, xdt(g, 0)[:, cut], m_of[:, r * 3 * P:r * 3 * P + T], start=True, stop=False)
                    last = pe.matmul(to[:, P:T], xdt(g, 1)[:, cut], m_of[:, r * 3 * P + T:(r + 1) * 3 * P],
                                     start=False, stop=True)
                last.then_inc(S["y_done"], 1)

            def group_sums(g):
                pe.wait_ge(S["y_sq"], 2 * (g + 1))
                if g:
                    pe.wait_ge(S["y_var"], g)
                for m in range(2):
                    last = pe.matmul(banks[:, 7, 0:T], gmean_w[:, :], sq[:, 2 * (g % 2) + m, :],
                                     start=m == 0, stop=m == 1)
                last.then_inc(S["y_sums"], 1)

            pe.wait_ge(S["cum_lo"], 1)
            pe.wait_ge(S["cum_got"], 1)
            pe.wait_ge(S["ident_r_ready"], 1)
            pairs = 2 * SSM_GROUPS
            for n in range(pairs + 3):
                if n < pairs and n % 2 == 0:
                    scores_and_tokens(n // 2)
                if n < pairs:
                    decay_rows(n)
                if 0 < n <= pairs:
                    head_outputs(n - 1)
                if n >= 4 and n % 2 == 0:
                    group_sums((n - 4) // 2)

            stage_mod("mod_rest")
            mod_columns(mod_row2, 16, 32, INDEX["mod_rest"])
            pe.wait_ge(S["mod_ready"], 2)
            stage_long("branch_ssm", YB, 16, lambda k: pe.wait_ge(S["y_lo"], k // 2))
            stage_k8("out", MX, operand_of("branch_ssm", 4))
            stats(2, False, "out")
            pe.wait_ge(S["norm_lo"], 4)
            stage_k8("ff1", H)
            stage_long("ff2", HH, 32, operand_of("ff1", 4))
            stats(3, False, "ff2")

            norm = [4]

            def normed():
                pe.wait_ge(S["norm_lo"], 2 * (norm[0] - 1))

            def feed_forward(i):
                normed()
                stage_k8(f"gu{i}", H)
                stage_long(f"down{i}", HH, 22, operand_of(f"gu{i}", 2))
                stats(norm[0], True, f"down{i}")
                norm[0] += 1

            feed_forward(0)

            normed()
            stage_k8("qkv", H)
            pe.wait_ge(summed, FIRST_GROUP[INDEX["att_out"]])
            for h in range(HEADS):
                for t in range(TT):
                    last = pe.transpose(banks[:, h // 2, (h % 2 * TT + t) * P:(h % 2 * TT + t + 1) * P],
                                        qkv[:, 16 + h, t * P:t * P + P], ident[:, :])
                if h % 2:
                    last.then_inc(S["vt_done"], 1)

            def att_scores(h):
                if h >= 2:
                    pe.wait_ge(S["s_max"], h - 1)
                to = banks[:, 4 + h % 2, :]
                pe.matmul(to[:, 0:P], qkv[:, h, 0:P], qkv[:, 8 + h, 0:P], start=True, stop=True)
                pe.matmul(to[:, P:3 * P], qkv[:, h, P:T], qkv[:, 8 + h, :], start=True, stop=True)\
                    .then_inc(S["s_done"], 1)

            def att_transpose(h):
                pe.wait_ge(S["p_norm"], h + 1)
                if h >= 1:
                    pe.wait_ge(S["pt_copied"], h)
                for n in range(3):
                    last = pe.transpose(banks[:, 6, n * P:n * P + P], probs[:, h % 2, n * P:n * P + P], ident[:, :])
                last.then_inc(S["pt_done"], 1)

            def att_values(h):
                pe.wait_ge(S["pt_copied"], h + 1)
                if h >= 1:
                    pe.wait_ge(S["o_copied"], h)
                pe.matmul(banks[:, 7, 0:T], v_tok[:, 0, h * P:h * P + P], probs_t[:, h % 2, 0:T], start=True, stop=False)
                pe.matmul(banks[:, 7, P:T], v_tok[:, 1, h * P:h * P + P], probs_t[:, h % 2, T:3 * P],
                          start=False, stop=True).then_inc(S["o_done"], 1)

            pe.wait_ge(S["v_copied"], 4)
            for h in range(HEADS + 2):
                if h < HEADS:
                    att_scores(h)
                if 1 <= h <= HEADS:
                    att_transpose(h - 1)
                if h >= 2:
                    att_values(h - 2)
            pe.wait_ge(S["o_lo"], HEADS)
            stage_k8("att_out", H)
            stats(norm[0], True, "att_out")
            norm[0] += 1
            feed_forward(1)
            feed_forward(2)

            normed()
            stage_k8("pool_in", H)
            s = INDEX["pool_group"]
            pe.wait_ge(S["pool_lo"], 1)
            pe.wait_ge(panel_lo, 2 * (FIRST_PANEL[s] + 1))
            pe.wait_ge(summed, FIRST_GROUP[s])
            for m in range(KD):
                for k in range(2):
                    at = (m // 2) * CHUNK + k * T + (m % 2) * P
                    pair = PG[:, m // 2 * 2 + k, :, :].rearrange("p a t -> p (a t)")
                    acc = banks[:, BANKS * ((FIRST_GROUP[s] + m // 4) % 2) + m % 4, :]
                    pe.matmul(acc, w_hi[:, FIRST_PANEL[s] % SPLIT, at:at + P], pair, start=k == 0, stop=False)
                    last = pe.matmul(acc[:, 0:T], w_lo[:, FIRST_PANEL[s] % SPLIT, at:at + P], pair[:, 0:T],
                                     start=False, stop=k == 1)
            last.then_inc(panel_used, 1)
            stage_k8("pool_out", H, operand_of("pool_group", 4))
            stats(norm[0], True, "pool_out")
            norm[0] += 1
            feed_forward(3)

        @block.scalar
        def _(act):
            def split(q, r, sl, turn):
                act.wait_ge(loaded[r], 16 * turn + 16)
                need(act, panel_used, q - SPLIT + 1)
                for half in range(2):
                    w = slice(half * PANEL // 2, (half + 1) * PANEL // 2)
                    act.activation(w_hi[:, sl, w], raw[:, r, w], ACT.Copy).then_inc(panel_hi, 1)

            def correction(s, g, G):
                kind = STAGES[s][3]
                act.wait_ge(panel_used, through(s, g))
                if kind in ("gate", "conv", "add1", "deep"):
                    need(act, posted, before("posted", s) + g - 1)
                elif kind in COUNTED["operand"]:
                    need(act, operand_lo, before("operand", s) + g - 1)
                elif kind == "keep":
                    need(act, summed, FIRST_GROUP[s] + g - 1)
                act.activation(ev[:, G, :, :], banks[:, BANKS * G:BANKS * G + BANKS, T:CHUNK], ACT.Copy)\
                    .then_inc(corrected, 1)

            def stage(name, post):
                def take_up(s, g, G):
                    if STAGES[s][3] != "mod":
                        correction(s, g, G)
                        post(s, g, G)
                run(act, INDEX[name], split, take_up)

            def nothing(s, g, G):
                pass

            def activate_into(func, dest):
                def post(s, g, G):
                    act.wait_ge(summed, FIRST_GROUP[s] + g + 1)
                    act.activation(by_group(dest[:, :, :])[:, g, :, :], ev[:, G, :, :], func).then_inc(activated, 1)
                return post

            def v_post(s, g, G):
                activate_into(ACT.Gelu_apprx_tanh, v_t)(s, g, G)
                act.wait_ge(activated, before("activated", s) + g + 1)
                act.activation(by_group(sq)[:, g, :, :], by_group(v_t[:, :, :])[:, g, :, :], ACT.Square)\
                    .then_inc(S["squares"], 1)

            def conv_post(s, g, G):
                act.wait_ge(posted, before("posted", s) + g + 1)
                for b in range(BANKS):
                    last = act.activation(by_group(xbc[:, :, :])[:, g, b, :], ev[:, G, b, :], ACT.Silu,
                                          bias=conv_b[:, g, b:b + 1])
                last.then_inc(activated, 1)

            def round_into(dest, blocks=BANKS):
                view = dest[:, :, 0, :].rearrange("p (g b) t -> p g b t", b=blocks)

                def post(s, g, G):
                    act.wait_ge(posted, before("posted", s) + g + 1)
                    act.activation(view[:, g, :, :], ev[:, G, 0:blocks, :], ACT.Copy).then_inc(operand_hi, 1)
                return post

            def glu_post(s, g, G):
                act.wait_ge(summed, FIRST_GROUP[s] + g + 1)
                act.activation(ev[:, G, 0:2, :], ev[:, G, 0:2, :], ACT.Silu).then_inc(activated, 1)
                round_into(HH, 2)(s, g, G)

            def squares_post(s, g, G):
                act.wait_ge(posted, before("posted", s) + g + 1)
                act.activation(by_group(sq)[:, g, :, :], by_group(xb)[:, g, :, :], ACT.Square)\
                    .then_inc(S["squares"], 1)

            act.wait_ge(S["tiny_set"], 1)

            def load_table(func):
                act.activation(tiny[:, 1:2], tiny[:, 0:1], func).then_inc(act_step, 1)

            def root(n):
                load_table(ACT.Sqrt)
                act.wait_ge(S["stat_var"], n + 1)
                act.activation(st[:, 1, :], st[:, 1, :], ACT.Sqrt).then_inc(S["stat_root"], 1)

            def norm_rounded(k, src):
                for g in range(2):
                    act.wait_ge(S["norm_y"], KD * k + BANKS * (g + 1))
                    act.activation(by_group(H[:, :, 0, :])[:, g, :, :], by_group(src)[:, g, :, :], ACT.Copy)\
                        .then_inc(S["norm_hi"], 1)

            act.wait_ge(S["consts_ready"], 7)
            act.activation(ident_r[:, :], ident[0:32, 0:32], ACT.Copy).then_inc(S["ident_r_ready"], 1)
            act.wait_ge(S["c_loaded"], 16)
            act.activation(c_s[:, :], c_f[:, :], ACT.Silu).then_inc(S["c_silu"], 1)
            act.wait_ge(S["c_silu"], 1)
            act.wait_ge(S["c_zero"], 1)
            act.activation(c_r[:, :, 0], c_s[:, :], ACT.Copy).then_inc(S["c_hi"], 1)
            split(0, 0, 0, 0)
            split(1, 1, 1, 0)
            act.wait_ge(S["x_loaded"], 16)
            for g in range(2):
                act.activation(by_group(sq)[:, g, :, :], by_group(xb)[:, g, :, :], ACT.Square)\
                    .then_inc(S["squares"], 1)
            root(0)
            for h in range(HEADS):
                act.wait_ge(S["rev_done"], h + 1)
                act.activation(rev[:, h, :], banks[:, 1 + h % 2, :], ACT.Copy).then_inc(S["rev_copied"], 1)
            stage("mod_norm", nothing)
            norm_rounded(0, ev8)

            stage("u", activate_into(ACT.Gelu_apprx_tanh, u_t))
            stage("v", v_post)
            act.wait_ge(S["rev_stored"], 16)
            stage("gate_a", activate_into(ACT.Sigmoid, gate_a))
            stage("gate_b", activate_into(ACT.Sigmoid, gate_b))
            root(1)
            for j in range(4):
                act.wait_ge(S["sgu_vt"], j + 1)
                act.activation(v_nat[:, 2 * j:2 * j + 2, :, :].rearrange("p m t d -> p (m t d)"),
                               banks[:, 1 + j, :], ACT.Copy).then_inc(S["sgu_vcopy"], 1)
            for j in range(4):
                act.wait_ge(S["sgu_y"], j + 1)
                act.activation(YA[:, 2 * j:2 * j + 2, 0, :], ev8[:, 2 * j:2 * j + 2, :], ACT.Copy)\
                    .then_inc(S["sgu_hi"], 1)
            stage("branch_gm", nothing)
            load_table(ACT.Silu)
            stage("xbc", conv_post)
            stage("z", activate_into(ACT.Silu, z_t))

            act.wait_ge(S["late_loaded"], 64)
            act.activation(wdt_r[:, :, 0, :], wdt[:, :, :], ACT.Copy).then_inc(S["wdt_hi"], 1)
            act.activation(ea[:, :], heads[:, 1, :], ACT.Exp).then_inc(S["dt_ea"], 1)
            act.wait_ge(S["dt_raw"], 1)
            act.activation(dtv[:, 0, :, :], banks[:, 4, 0:P].rearrange("p (t a h) -> p t a h", t=TT, a=2)[:, :, 1, :],
                           ACT.Copy).then_inc(S["dt_corr"], 1)
            act.wait_ge(S["dt_y"], 1)
            act.activation(dtv[:, 0, :, :], dtv[:, 0, :, :], ACT.Exp).then_inc(S["dt_exp"], 1)
            act.wait_ge(S["dt_one"], 1)
            act.activation(dtv[:, 0, :, :], dtv[:, 0, :, :], ACT.Ln).then_inc(S["dt_ln"], 1)
            act.wait_ge(S["cum_done"], 1)
            act.activation(cum_r[:, 0, :], banks[0:32, 6, 0:T], ACT.Copy).then_inc(S["cum_hi"], 1)

            pairs = 2 * SSM_GROUPS
            for n in range(pairs + 5):
                if n < pairs and n % 2 == 0:
                    g = n // 2
                    act.wait_ge(S["cb_done"], g + 1)
                    if g >= 2:
                        act.wait_ge(S["m_done"], 2 * (g - 1))
                    act.activation(cb[:, g % 2, :], banks[:, g % 2, 0:3 * P], ACT.Copy).then_inc(S["cb_copied"], 1)
                if n < pairs:
                    act.wait_ge(S["seg_done"], 4 * (n + 1))
                    act.activation(decay(n), decay(n), ACT.Exp).then_inc(S["exp_done"], 1)
                if 2 <= n < pairs + 2:
                    m = n - 2
                    act.wait_ge(S["y_gated"], m + 1)
                    if m >= 4:
                        act.wait_ge(S["y_sums"], m // 2 - 1)
                    act.activation(sq[:, m % 4, :], xbc[:, m, :], ACT.Square).then_inc(S["y_sq"], 1)
                if n >= 4 and n % 2 == 0 and n < pairs + 4:
                    g = (n - 4) // 2
                    act.wait_ge(S["y_var"], g + 1)
                    act.activation(st[:, g % 2, :], st[:, g % 2, :], ACT.Sqrt).then_inc(S["y_root"], 1)
                if 5 <= n < pairs + 5 and n % 2 == 1:
                    g = (n - 5) // 2
                    act.wait_ge(S["y_f"], 2 * (g + 1))
                    act.activation(YB[:, 2 * g:2 * g + 2, 0, :], xbc[:, 2 * g:2 * g + 2, :], ACT.Copy)\
                        .then_inc(S["y_hi"], 1)
            stage("mod_rest", nothing)
            stage("branch_ssm", round_into(MX))
            stage("out", squares_post)
            root(2)
            norm_rounded(1, ev8)
            stage("ff1", round_into(HH))
            stage("ff2", squares_post)
            root(3)
            norm_rounded(2, xb)

            norms = [3]

            def layer_norm(last=False):
                root(norms[0] + 1)
                if not last:
                    norm_rounded(norms[0], xb)
                norms[0] += 1

            def feed_forward(i, last=False):
                load_table(ACT.Silu)
                stage(f"gu{i}", glu_post)
                stage(f"down{i}", squares_post)
                layer_norm(last)

            feed_forward(0)
            stage("qkv", nothing)
            for j in range(4):
                act.wait_ge(S["vt_done"], j + 1)
                act.activation(v_tok[:, :, 2 * j * P:(2 * j + 2) * P].rearrange("p t (h d) -> p h t d", h=2),
                               banks[:, j, :].rearrange("p (h t d) -> p h t d", h=2, t=TT), ACT.Copy)\
                    .then_inc(S["v_copied"], 1)
            for h in range(HEADS + 3):
                if h < HEADS:
                    act.wait_ge(S["s_max"], h + 1)
                    act.activation(probs[:, h % 2, 0:P], probs[:, h % 2, 0:P], ACT.Exp, bias=sm[:, h, 2:3],
                                   accum_out=sm[:, h, 4:5]).then_inc(S["p_exp"], 1)
                    act.activation(probs[:, h % 2, P:3 * P], probs[:, h % 2, P:3 * P], ACT.Exp, bias=sm[:, h, 3:4],
                                   accum_out=sm[:, h, 5:6]).then_inc(S["p_exp"], 1)
                if 1 <= h <= HEADS:
                    m = h - 1
                    act.wait_ge(S["pt_done"], m + 1)
                    if m >= 2:
                        act.wait_ge(S["o_done"], m - 1)
                    act.activation(probs_t[:, m % 2, :], banks[:, 6, 0:3 * P], ACT.Copy).then_inc(S["pt_copied"], 1)
                if h >= 3:
                    m = h - 3
                    act.wait_ge(S["o_copied"], m + 1)
                    act.activation(H[:, m, 0, :], o_t[:, m % 2, :], ACT.Copy).then_inc(S["o_hi"], 1)
            stage("att_out", squares_post)
            layer_norm()
            feed_forward(1)
            feed_forward(2)
            stage("pool_in", nothing)
            act.wait_ge(S["pool_f"], 1)
            act.activation(PG[:, :, 0, :], pooled[:, :, :], ACT.Copy).then_inc(S["pool_hi"], 1)
            stage("pool_group", round_into(H))
            stage("pool_out", squares_post)
            layer_norm()
            feed_forward(3, last=True)

        @block.vector
        def _(vec):
            steps = [0]

            def step(ins):
                steps[0] += 1
                ins.then_inc(vec_step, 1)
                vec.wait_ge(vec_step, steps[0])

            def split(q, r, sl, turn):
                for half in range(2):
                    w = slice(half * PANEL // 2, (half + 1) * PANEL // 2)
                    vec.wait_ge(panel_hi, 2 * q + half + 1)
                    vec.tensor_tensor(w_lo[:, sl, w], raw[:, r, w], w_hi[:, sl, w], ALU.subtract).then_inc(panel_lo, 1)

            def take_sum(s, g, G, dest=None):
                vec.wait_ge(corrected, before("corrected", s) + g + 1)
                to = ev[:, G, :, :] if dest is None else dest
                vec.tensor_tensor(to, banks[:, BANKS * G:BANKS * G + BANKS, 0:T], ev[:, G, :, :], ALU.add)\
                    .then_inc(summed, 1)

            def own_sum(s, g):
                vec.wait_ge(summed, FIRST_GROUP[s] + g + 1)

            def stage(name, post, dest=None):
                def take_up(s, g, G):
                    if STAGES[s][3] == "mod":
                        vec.wait_ge(panel_used, through(s, g))
                        vec.tensor_copy(dest[0:2, g, :], banks[0:2, BANKS * G, :]).then_inc(summed, 1)
                        return
                    take_sum(s, g, G, None if dest is None else by_group(dest[:, :, :])[:, g, :, :])
                    post(s, g, G)
                run(vec, INDEX[name], split, take_up)

            def nothing(s, g, G):
                pass

            def lo_into(dest, blocks=BANKS):
                view = dest.rearrange("p (g b) a t -> p g b a t", b=blocks)

                def post(s, g, G):
                    vec.wait_ge(operand_hi, before("operand", s) + g + 1)
                    vec.tensor_tensor(view[:, g, :, 1, :], ev[:, G, 0:blocks, :], view[:, g, :, 0, :], ALU.subtract)\
                        .then_inc(operand_lo, 1)
                return post

            def glu_post(s, g, G):
                vec.wait_ge(activated, before("activated", s) + g + 1)
                vec.scalar_tensor_tensor(ev[:, G, 0:2, :], ev[:, G, 0:2, :], 0.5, ev[:, G, 2:4, :], ALU.mult, ALU.mult)\
                    .then_inc(posted, 1)
                lo_into(HH[:, 0:22, :, :], 2)(s, g, G)

            def relu2_post(s, g, G):
                own_sum(s, g)
                vec.scalar_tensor_tensor(ev[:, G, :, :], ev[:, G, :, :], 0.0, ev[:, G, :, :], ALU.max, ALU.mult)\
                    .then_inc(posted, 1)
                lo_into(HH[:, :, :, :])(s, g, G)

            def deep_post(s, g, G):
                own_sum(s, g)
                x = by_group(xb)[:, g, :, :]
                vec.scalar_tensor_tensor(x, x, ALPHA, ev[:, G, :, :], ALU.mult, ALU.add).then_inc(posted, 1)

            def add_gated(col):
                def post(s, g, G):
                    own_sum(s, g)
                    for b in range(BANKS):
                        m = BANKS * g + b
                        last = vec.scalar_tensor_tensor(xb[:, m, :], ev[:, G, b, :], mod[:, col + m:col + m + 1],
                                                        xb[:, m, :], ALU.mult, ALU.add)
                    last.then_inc(posted, 1)
                return post

            def gate_post(s, g, G):
                own_sum(s, g)
                a = by_group(gate_a[:, :, :])[:, g, :, :]
                vec.tensor_tensor(a, a, ev[:, G, :, :], ALU.mult).then_inc(posted, 1)

            def mix_post(s, g, G):
                own_sum(s, g)
                e = ev[:, G, :, :]
                step(vec.tensor_tensor(e, e, by_group(gate_b[:, :, :])[:, g, :, :], ALU.mult))
                vec.tensor_tensor(e, e, by_group(gate_a[:, :, :])[:, g, :, :], ALU.add).then_inc(posted, 1)
                lo_into(MX[:, :, :, :])(s, g, G)

            def scale_post(s, g, G):
                own_sum(s, g)
                for b in range(BANKS):
                    at = COLS["pool_scale"] + BANKS * g + b
                    last = vec.tensor_scalar(ev[:, G, b, :], ev[:, G, b, :], cols[:, at:at + 1], None, ALU.mult)
                last.then_inc(posted, 1)
                lo_into(H[:, :, :, :])(s, g, G)

            def variance(n, mean, eps, stage=None):
                vec.wait_ge(S["stat_sums"], n + 1)
                b = stat_bank(stage)
                if mean:
                    step(vec.tensor_copy(st[:, 0, :], banks[:, b, 0:T]))
                    step(vec.tensor_tensor(st[:, 3, :], st[:, 0, :], st[:, 0, :], ALU.mult))
                    step(vec.tensor_tensor(st[:, 1, :], banks[:, b, T:2 * T], st[:, 3, :], ALU.subtract))
                    vec.tensor_scalar(st[:, 1, :], st[:, 1, :], 0.0, eps, ALU.max, ALU.add).then_inc(S["stat_var"], 1)
                else:
                    vec.tensor_scalar(st[:, 1, :], banks[:, b, T:2 * T], eps, None, ALU.add).then_inc(S["stat_var"], 1)

            def inverse_root(n, mean=False):
                vec.wait_ge(S["stat_root"], n + 1)
                step(vec.reciprocal(st[:, 2, :], st[:, 1, :]))
                if mean:
                    step(vec.tensor_tensor(st[:, 3, :], st[:, 0, :], st[:, 2, :], ALU.mult))

            def over_blocks(row):
                return row.unsqueeze(1).to_broadcast([P, BANKS, T])

            def apply_norm(k, dest, scale, bias, mean, operand=True):
                def lo(g):
                    vec.wait_ge(S["norm_hi"], 2 * k + g + 1)
                    vec.tensor_tensor(H[:, BANKS * g:BANKS * g + BANKS, 1, :], dest[:, BANKS * g:BANKS * g + BANKS, :],
                                      H[:, BANKS * g:BANKS * g + BANKS, 0, :], ALU.subtract).then_inc(S["norm_lo"], 1)

                for g in range(2):
                    e = ev[:, g, :, :]
                    step(vec.tensor_tensor(e, by_group(xb)[:, g, :, :], over_blocks(st[:, 2, :]), ALU.mult))
                    if g and operand:
                        lo(0)
                    if mean:
                        step(vec.tensor_tensor(e, e, over_blocks(st[:, 3, :]), ALU.subtract))
                    for b in range(BANKS):
                        m = BANKS * g + b
                        vec.tensor_scalar(dest[:, m, :], ev[:, g, b, :], scale[:, m:m + 1],
                                          0.0 if bias is None else bias[:, m:m + 1], ALU.mult, ALU.add)\
                            .then_inc(S["norm_y"], 1)
                if operand:
                    lo(1)

            def mod_taken(n, first, count, scales):
                vec.wait_ge(S["mod_cols"], n)
                step(vec.tensor_tensor(mod[:, first:first + count], banks[:, 7, first:first + count],
                                       cols[:, COLS["b_mod"] + first:COLS["b_mod"] + first + count], ALU.add))
                vec.tensor_scalar(mod[:, scales:scales + 8], mod[:, scales:scales + 8], 1.0, None, ALU.add)\
                    .then_inc(S["mod_ready"], 1)
                vec.wait_ge(S["mod_ready"], n)

            vec.memset(tiny[:, :], 1.0).then_inc(S["tiny_set"], 1)
            vec.wait_ge(S["c_hi"], 1)
            vec.tensor_tensor(c_r[:, :, 1], c_s[:, :], c_r[:, :, 0], ALU.subtract).then_inc(S["c_lo"], 1)
            vec.wait_ge(S["params_loaded"], 16)
            split(0, 0, 0, 0)
            split(1, 1, 1, 0)
            variance(0, False, EPS)
            stage("mod_norm", None, mod_row[:, :].rearrange("p (g n) -> p g n", n=CHUNK))
            inverse_root(0)
            mod_taken(1, 0, 16, 8)
            apply_norm(0, ev8, mod[:, 8:16], mod[:, 0:8], False)

            stage("u", nothing)
            stage("v", nothing)
            stage("gate_a", nothing)
            stage("gate_b", nothing)

            variance(1, False, EPS)
            inverse_root(1)
            for g in range(2):
                v4 = by_group(v_t[:, :, :])[:, g, :, :]
                step(vec.tensor_tensor(v4, v4, over_blocks(st[:, 2, :]), ALU.mult))
                for b in range(BANKS):
                    m = BANKS * g + b
                    at = COLS["gm_norm"] + m
                    last = vec.tensor_scalar(v_t[:, m, :], v_t[:, m, :], cols[:, at:at + 1], None, ALU.mult)
                last.then_inc(S["sgu_vn"], 1)
            for j in range(5):
                if j < 4:
                    two = slice(2 * j, 2 * j + 2)
                    vec.wait_ge(S["sgu_mix"], j + 1)
                    mixed = banks[:, (5, 6, 7, 0)[j], :].rearrange("p (m t) -> p m t", m=2)
                    vec.tensor_tensor(ev8[:, two, :], mixed, u_t[:, two, :], ALU.mult).then_inc(S["sgu_y"], 1)
                if j:
                    two = slice(2 * j - 2, 2 * j)
                    vec.wait_ge(S["sgu_hi"], j)
                    vec.tensor_tensor(YA[:, two, 1, :], ev8[:, two, :], YA[:, two, 0, :], ALU.subtract)\
                        .then_inc(S["sgu_lo"], 1)
            stage("branch_gm", gate_post)

            step(vec.memset(pad[:, :, 0:CONV - 1], 0.0))

            def conv_post(s, g, G):
                own_sum(s, g)
                for tap in range(CONV):
                    if tap:
                        vec.wait_ge(S["conv_tap"], (CONV - 1) * g + tap)
                    for b in range(BANKS):
                        w = conv_w[:, g, CONV * b + tap:CONV * b + tap + 1]
                        x = pad[:, b, tap:tap + T]
                        if tap == 0:
                            last = vec.tensor_scalar(ev[:, G, b, :], x, w, None, ALU.mult)
                        else:
                            last = vec.scalar_tensor_tensor(ev[:, G, b, :], x, w, ev[:, G, b, :], ALU.mult, ALU.add)
                    last.then_inc(S["conv_tap"] if tap < CONV - 1 else posted, 1)

            def conv_take_up(s, g, G):
                take_sum(s, g, G, pad[:, :, CONV - 1:CONV - 1 + T])
                conv_post(s, g, G)

            run(vec, INDEX["xbc"], split, conv_take_up)
            stage("z", nothing)

            vec.wait_ge(S["wdt_hi"], 1)
            vec.tensor_tensor(wdt_r[:, :, 1, :], wdt[:, :, :], wdt_r[:, :, 0, :], ALU.subtract).then_inc(S["wdt_lo"], 1)
            scratch, y_v, dt_v, a_v, ncum = (dtv[:, n, :, :] for n in range(5))
            vec.wait_ge(S["dt_corr"], 1)
            step(vec.tensor_tensor(y_v, banks[:, 4, 0:P].rearrange("p (t a h) -> p t a h", t=TT, a=2)[:, :, 0, :],
                                   scratch, ALU.add))
            step(vec.tensor_tensor(y_v, y_v, heads[:, 0, :].unsqueeze(1).to_broadcast([P, TT, 32]), ALU.add))
            vec.scalar_tensor_tensor(scratch, y_v, -1.0, y_v, ALU.mult, ALU.min).then_inc(S["dt_y"], 1)
            vec.wait_ge(S["dt_exp"], 1)
            vec.tensor_scalar(scratch, scratch, 1.0, None, ALU.add).then_inc(S["dt_one"], 1)
            vec.wait_ge(S["dt_ln"], 1)
            step(vec.scalar_tensor_tensor(dt_v, y_v, 0.0, scratch, ALU.max, ALU.add))
            vec.wait_ge(S["dt_ea"], 1)
            vec.scalar_tensor_tensor(a_v, dt_v, -1.0, ea[:, :].unsqueeze(1).to_broadcast([P, TT, 32]),
                                     ALU.mult, ALU.mult).then_inc(S["dt_a"], 1)
            vec.wait_ge(S["cum_done"], 1)
            vec.tensor_scalar(ncum, banks[:, 5, 0:64].rearrange("p (t h) -> p t h", t=TT), -1.0, None, ALU.mult)\
                .then_inc(S["cum_got"], 1)
            vec.wait_ge(S["cum_hi"], 1)
            vec.tensor_tensor(cum_r[:, 1, :], banks[0:32, 6, 0:T], cum_r[:, 0, :], ALU.subtract)\
                .then_inc(S["cum_lo"], 1)
            vec.wait_ge(S["cum_got"], 1)

            pairs = 2 * SSM_GROUPS
            for n in range(pairs + 7):
                if n < pairs and n % 2 == 0:
                    g = n // 2
                    vec.wait_ge(S["xt_done"], g + 1)
                    if g >= 2:
                        vec.wait_ge(S["y_done"], 2 * (g - 1))
                    for t in range(TT):
                        vec.tensor_tensor(xdt(g, t).rearrange("p (h d) -> p h d", h=4),
                                          banks[:, 2, t * T:t * T + T].rearrange("p (h d) -> p h d", h=4),
                                          dtv[:, 2, t, 4 * g:4 * g + 4].unsqueeze(2).to_broadcast([P, 4, HP]),
                                          ALU.mult).then_inc(S["xdt_done"], 1)
                if n < pairs:
                    vec.wait_ge(S["row_done"], n + 1)
                    if n >= 2:
                        vec.wait_ge(S["y_done"], n - 1)
                    for r in range(2):
                        h = 2 * n + r
                        for t, (at, size) in enumerate(((0, T), (T, P))):
                            vec.tensor_scalar(decay(n)[:, 3 * P * r + at:3 * P * r + at + size],
                                              banks[:, 3 + n % 2, r * T + t * P:r * T + T],
                                              ncum[:, t, h:h + 1], 0.0, ALU.add, ALU.min).then_inc(S["seg_done"], 1)
                if 1 <= n <= pairs:
                    m = n - 1
                    vec.wait_ge(S["exp_done"], m + 1)
                    vec.wait_ge(S["cb_masked"], m // 2 + 1)
                    two = decay(m).rearrange("p (r i) -> p r i", r=2)
                    vec.tensor_tensor(two, two, cb[:, m // 2 % 2, :].unsqueeze(1).to_broadcast([P, 2, 3 * P]),
                                      ALU.mult).then_inc(S["m_done"], 1)
                if 2 <= n <= pairs + 1:
                    m = n - 2
                    at = COLS["d_skip"] + m
                    vec.wait_ge(S["y_done"], m + 1)
                    step(vec.scalar_tensor_tensor(xbc[:, m, :], xbc[:, m, :], cols[:, at:at + 1],
                                                  banks[:, 5 + m % 2, 0:T], ALU.mult, ALU.add))
                    vec.tensor_tensor(xbc[:, m, :], xbc[:, m, :], z_t[:, m, :], ALU.mult).then_inc(S["y_gated"], 1)
                if n >= 4 and n % 2 == 0 and n < pairs + 4:
                    g = (n - 4) // 2
                    vec.wait_ge(S["y_sums"], g + 1)
                    vec.tensor_scalar(st[:, g % 2, :], banks[:, 7, 0:T], EPS, None, ALU.add).then_inc(S["y_var"], 1)
                if 5 <= n < pairs + 5 and n % 2 == 1:
                    g = (n - 5) // 2
                    vec.wait_ge(S["y_root"], g + 1)
                    step(vec.reciprocal(st[:, 2 + g % 2, :], st[:, g % 2, :]))
                    for m in (2 * g, 2 * g + 1):
                        at = COLS["ssm_norm"] + m
                        vec.scalar_tensor_tensor(xbc[:, m, :], xbc[:, m, :], cols[:, at:at + 1], st[:, 2 + g % 2, :],
                                                 ALU.mult, ALU.mult).then_inc(S["y_f"], 1)
                if 6 <= n < pairs + 6 and n % 2 == 0:
                    g = (n - 6) // 2
                    two = slice(2 * g, 2 * g + 2)
                    vec.wait_ge(S["y_hi"], g + 1)
                    vec.tensor_tensor(YB[:, two, 1, :], xbc[:, two, :], YB[:, two, 0, :], ALU.subtract)\
                        .then_inc(S["y_lo"], 1)
            stage("mod_rest", None, mod_row2[:, :].rearrange("p (g n) -> p g n", n=CHUNK))
            mod_taken(2, 16, 32, 32)
            stage("branch_ssm", mix_post)
            stage("out", add_gated(16))
            variance(2, False, EPS, "out")
            inverse_root(2)
            apply_norm(1, ev8, mod[:, 32:40], mod[:, 24:32], False)
            stage("ff1", relu2_post)
            stage("ff2", add_gated(40))
            variance(3, False, EPS, "ff2")
            inverse_root(3)
            apply_norm(2, xb, cols[:, COLS["final"]:COLS["final"] + KD], None, False)

            norms = [3]

            def layer_norm(stage_name, i, last=False):
                k = norms[0]
                at = KD * i
                variance(k + 1, True, LN_EPS, stage_name)
                inverse_root(k + 1, True)
                apply_norm(k, xb, cols[:, COLS["ln_g"] + at:COLS["ln_g"] + at + KD],
                           cols[:, COLS["ln_b"] + at:COLS["ln_b"] + at + KD], True, not last)
                norms[0] += 1

            def feed_forward(i, ln, last=False):
                stage(f"gu{i}", glu_post)
                stage(f"down{i}", deep_post)
                layer_norm(f"down{i}", ln, last)

            feed_forward(0, 0)
            stage("qkv", nothing, qkv)
            vec.wait_ge(S["near_loaded"], 16 * HEADS)
            for h in range(HEADS + 4):
                if h < HEADS:
                    vec.wait_ge(S["s_done"], h + 1)
                    if h >= 2:
                        vec.wait_ge(S["pt_done"], h - 1)
                    b = banks[:, 4 + h % 2, :]
                    pr = probs[:, h % 2, :]
                    vec.scalar_tensor_tensor(pr[:, 0:P], b[:, 0:P], SCALE, near[:, h, P:T], ALU.mult, ALU.add)\
                        .then_inc(S["s_biased"], 1)
                    vec.scalar_tensor_tensor(pr[:, P:3 * P], b[:, P:3 * P], SCALE, near[:, h, :], ALU.mult, ALU.add)\
                        .then_inc(S["s_biased"], 1)
                    vec.wait_ge(S["s_biased"], 2 * h + 1)
                    step(vec.reduce_max(sm[:, h, 0:1], pr[:, 0:P], AX.X))
                    vec.wait_ge(S["s_biased"], 2 * h + 2)
                    step(vec.reduce_max(sm[:, h, 1:2], pr[:, P:3 * P], AX.X))
                    vec.tensor_scalar(sm[:, h, 2:4], sm[:, h, 0:2], -1.0, None, ALU.mult).then_inc(S["s_max"], 1)
                if 1 <= h <= HEADS:
                    m = h - 1
                    vec.wait_ge(S["p_exp"], 2 * (m + 1))
                    step(vec.reciprocal(sm[:, m, 6:8], sm[:, m, 4:6]))
                    pr = probs[:, m % 2, :]
                    vec.tensor_scalar(pr[:, 0:P], pr[:, 0:P], sm[:, m, 6:7], None, ALU.mult)
                    vec.tensor_scalar(pr[:, P:3 * P], pr[:, P:3 * P], sm[:, m, 7:8], None, ALU.mult)\
                        .then_inc(S["p_norm"], 1)
                if 3 <= h <= HEADS + 2:
                    m = h - 3
                    vec.wait_ge(S["o_done"], m + 1)
                    if m >= 2:
                        vec.wait_ge(S["o_lo"], m - 1)
                    vec.tensor_copy(o_t[:, m % 2, :], banks[:, 7, 0:T]).then_inc(S["o_copied"], 1)
                if h >= 4:
                    m = h - 4
                    vec.wait_ge(S["o_hi"], m + 1)
                    vec.tensor_tensor(H[:, m, 1, :], o_t[:, m % 2, :], H[:, m, 0, :], ALU.subtract)\
                        .then_inc(S["o_lo"], 1)
            stage("att_out", deep_post)
            layer_norm("att_out", 1)
            feed_forward(1, 2)
            feed_forward(2, 3)

            stage("pool_in", nothing, pu)
            own_sum(INDEX["pool_in"], 1)
            src, reach = pu, 1
            for w in range(4):
                b = slice(2 * w, KD)
                step(vec.tensor_copy(pw[:, w, b, 0:reach], src[:, b, 0:reach]))
                step(vec.tensor_tensor(pw[:, w, b, reach:T], src[:, b, reach:T], src[:, b, 0:T - reach], ALU.add))
                src, reach = pw[:, w, :, :], 2 * reach
            vec.wait_ge(S["inv_loaded"], 16)
            edge = max(WINDOWS)
            for w, width in enumerate(WINDOWS):
                b = slice(2 * w, 2 * w + 2)
                vec.scalar_tensor_tensor(pooled[:, b, edge:T], pw[:, w, b, edge:T], 1.0 / width, pu[:, b, edge:T],
                                         ALU.mult, ALU.subtract)
                step(vec.tensor_tensor(pooled[:, b, 0:edge], pw[:, w, b, 0:edge],
                                       inv[:, w, :].unsqueeze(1).to_broadcast([P, 2, edge]), ALU.mult))
                last = vec.tensor_tensor(pooled[:, b, 0:edge], pooled[:, b, 0:edge], pu[:, b, 0:edge], ALU.subtract)
            last.then_inc(S["pool_f"], 1)
            vec.wait_ge(S["pool_hi"], 1)
            vec.tensor_tensor(PG[:, :, 1, :], pooled[:, :, :], PG[:, :, 0, :], ALU.subtract).then_inc(S["pool_lo"], 1)
            stage("pool_group", scale_post)
            stage("pool_out", deep_post)
            layer_norm("pool_out", 4)
            feed_forward(3, 5, last=True)


def kernel(**inputs):
    import numpy as np
    import concourse.bacc as bacc
    from concourse.bass_utils import run_bass_kernel_spmd as launch

    f = {n: np.asarray(a) for n, a in inputs.items()}

    def chunks(w):
        k, n = w.shape
        return w.reshape(k // P, P, n // CHUNK, CHUNK).transpose(2, 0, 1, 3).reshape(-1, P, CHUNK)

    def glu_chunks(w):
        k, n = w.shape
        return chunks(w.reshape(k, 2, n // 2 // T, T).transpose(0, 2, 1, 3).reshape(k, n))

    w_in, w_mod = f["w_in"][0], f["w_mod"][0]
    u, v, z, xbc, dt, ga, gb = np.split(w_in, np.cumsum([D, D, 2 * D, 4 * D, SSM_HEADS, D])[:], axis=1)
    gu, down = f["ffn_w_gu_2"], f["ffn_w_down_2"]
    a_in, b_in = f["a_w_in_2"][0], f["b_w_in_2"][0]
    grouped = f["b_w_group_2"][0].reshape(4, 2, P, T).transpose(0, 2, 1, 3).reshape(4, P, CHUNK)
    stream = np.concatenate([
        chunks(w_mod[:, :2 * D]), chunks(u), chunks(v), chunks(ga), chunks(gb), chunks(f["w_branch_gm"][0]),
        chunks(xbc), chunks(z), chunks(w_mod[:, 2 * D:]), chunks(f["w_branch_ssm"][0]), chunks(f["w_out"][0]),
        chunks(f["w_ff1"][0]), chunks(f["w_ff2"][0]),
        glu_chunks(gu[0, 0]), chunks(down[0, 0]), chunks(a_in), chunks(f["a_w_out_2"][0]),
        glu_chunks(gu[0, 1]), chunks(down[0, 1]), glu_chunks(gu[1, 0]), chunks(down[1, 0]),
        chunks(b_in), grouped, chunks(f["b_w_out_2"][0]), glu_chunks(gu[1, 1]), chunks(down[1, 1])])
    panels = stream.reshape(PANELS, 4, P, CHUNK).transpose(0, 2, 1, 3).reshape(PANELS, P, PANEL)

    def columns(a):
        return a.reshape(-1, P).T

    conv_w = f["conv_w"][0].reshape(CONV, 32, P).transpose(2, 1, 0).reshape(P, 32 * CONV)
    cols = np.concatenate([
        columns(f["b_mod"][0]), columns(f["gm_norm_w"][0]), columns(f["conv_b"][0]), conv_w,
        columns(f["ssm_norm_w"][0]), columns(f["final_norm_w"]), columns(f["ln_g_2"].reshape(-1)),
        columns(f["ln_b_2"].reshape(-1)), columns(f["b_scale_2"][0]),
        columns(np.repeat(f["d_skip"][0], HP))], axis=1)
    heads = np.broadcast_to(np.stack([f["dt_bias"][0], f["a_log"][0]]), (P, 2, SSM_HEADS))
    dist = T - 1 - np.arange(BIAS_COLS)
    near = np.maximum(dist, 1).astype(np.float32)
    large = 16 + (np.log(near / np.float32(16)) / np.float32(np.log(8.0)) * np.float32(16)).astype(np.int32)
    bucket = np.where(dist < 0, 32, np.where(dist < 16, dist, np.minimum(large, 31)))
    onehot = (np.arange(33)[:, None] == bucket[None, :]).astype(np.float32)
    tokens = np.arange(1, 17, dtype=np.float32)
    inv = np.broadcast_to(np.stack([1 / np.minimum(tokens, np.float32(w)) for w in WINDOWS]), (P, 4, 16))
    arrays = {
        "panels": panels,
        "x_t": f["x"][0].T.reshape(KD, P, T).transpose(1, 0, 2),
        "c_t": columns(f["c"][0]),
        "cols": cols,
        "heads": heads,
        "ws_t": f["gm_ws"][0].transpose(2, 0, 1),
        "bs": f["gm_bs"][0].reshape(1, -1),
        "wdt": dt.reshape(KD, P, SSM_HEADS).transpose(1, 0, 2),
        "rel": f["rel_bias_2"],
        "onehot": onehot,
        "inv": inv,
    }
    arrays = {f"in_{n}": np.ascontiguousarray(a, dtype=np.float32) for n, a in arrays.items()}
    nc = bacc.Bacc("TRN2", target_bir_lowering=False, num_devices=1)
    args = [nc.dram_tensor(n, a.shape, F32, kind="ExternalInput").ap() for n, a in arrays.items()]
    args.append(nc.dram_tensor("bias_rows", (P, HEADS * BIAS_COLS), F32).ap())
    args.append(nc.dram_tensor("out_t", (P, KD, T), F32, kind="ExternalOutput").ap())
    two_blocks(nc, *args)
    result = launch(nc, [arrays], core_ids=[0]).results[0]["out_t"]
    return result.transpose(1, 0, 2).reshape(D, T).T[None]
```

```python
import concourse.bass as bass
from concourse import mybir
from contextlib import ExitStack

F32 = mybir.dt.float32
F32R = mybir.dt.float32r
ACT = mybir.ActivationFunctionType
ALU = mybir.AluOpType
AX = mybir.AxisListType

P = 128
T = 256
TT = T // P
D = 1024
KD = D // P
CHUNK = 512
PANEL = 4 * CHUNK
BANKS = 4
RAW = 4
SPLIT = 2
EPS = 1e-6
LN_EPS = 1e-5
ALPHA = (2 * 2) ** 0.25
HEADS = 8
HEAD_DIM = 128
SCALE = HEAD_DIM ** -0.5
SSM_HEADS = 32
HP = 64
SSM_GROUPS = 8
CONV = 4
WINDOWS = (2, 4, 8, 16)
MASKED = -1e30
BIAS_COLS = 2 * T

STAGES = (
    ("mod_norm", 8, 4, "mod"), ("u", 8, 2, "act"), ("v", 8, 2, "act"), ("gate_a", 8, 2, "act"),
    ("gate_b", 8, 2, "act"), ("branch_gm", 8, 2, "gate"), ("xbc", 8, 8, "conv"), ("z", 8, 4, "act"),
    ("mod_rest", 8, 8, "mod"), ("branch_ssm", 16, 2, "mix"), ("out", 8, 2, "add1"),
    ("ff1", 8, 8, "relu2"), ("ff2", 32, 2, "add1"),
    ("gu0", 8, 11, "glu"), ("down0", 22, 2, "deep"), ("qkv", 8, 6, "keep"), ("att_out", 8, 2, "deep"),
    ("gu1", 8, 11, "glu"), ("down1", 22, 2, "deep"), ("gu2", 8, 11, "glu"), ("down2", 22, 2, "deep"),
    ("pool_in", 8, 2, "keep"), ("pool_group", 2, 2, "scale"), ("pool_out", 8, 2, "deep"),
    ("gu3", 8, 11, "glu"), ("down3", 22, 2, "deep"),
)
INDEX = {s[0]: n for n, s in enumerate(STAGES)}
NORMED = ("out", "ff2", "down0", "att_out", "down1", "down2", "pool_out", "down3")
_ALL = ("mod", "act", "gate", "conv", "mix", "add1", "relu2", "glu", "deep", "keep", "scale")
COUNTED = {
    "corrected": _ALL[1:],
    "summed": _ALL,
    "activated": ("act", "conv", "glu"),
    "posted": ("gate", "conv", "mix", "add1", "relu2", "glu", "deep", "scale"),
    "operand": ("mix", "relu2", "glu", "scale"),
}


def panels_of(stage):
    name, kb, groups, kind = stage
    return kb * groups // 4


def before(sem, stage):
    return sum(s[2] for s in STAGES[:stage] if s[3] in COUNTED[sem])


FIRST_PANEL = [sum(map(panels_of, STAGES[:n])) for n in range(len(STAGES) + 1)]
FIRST_GROUP = [sum(s[2] for s in STAGES[:n]) for n in range(len(STAGES) + 1)]
PANELS = FIRST_PANEL[-1]

COLS, _at = {}, 0
for _name, _n in (("b_mod", 48), ("gm_norm", 8), ("conv_b", 32), ("conv_w", 32 * CONV), ("ssm_norm", 16),
                  ("final", 8), ("ln_g", 48), ("ln_b", 48), ("pool_scale", 8), ("d_skip", 16)):
    COLS[_name] = _at
    _at += _n
NCOLS = _at


def two_blocks(nc, panels, x_in, c_in, cols_in, heads_in, ws_in, bs_in, wdt_in, rel_in, onehot_in, inv_in,
               skew, out):
    ctx = ExitStack()
    with ctx:
        def sb(name, shape, dt=F32, stack=ctx):
            return stack.enter_context(nc.sbuf_tensor(name, shape, dt))

        raw = sb("raw", [P, RAW, PANEL])
        w_hi = sb("w_hi", [P, SPLIT, PANEL], F32R)
        w_lo = sb("w_lo", [P, SPLIT, PANEL], F32R)
        ev = sb("ev", [P, 2, BANKS, T])
        XS = sb("XS", [P, KD, 2, T])
        st = sb("st", [P, 4, T])
        ident = sb("ident", [P, P])
        ident_r = sb("ident_r", [32, 32], F32R)
        ones = sb("ones", [P, P])
        mean_w = sb("mean_w", [P, P])
        gmean_w = sb("gmean_w", [P, P])
        cols = sb("cols", [P, NCOLS])
        tiny = sb("tiny", [P, 2])
        mod = sb("mod", [P, 48])
        phase = ExitStack()
        H = sb("H", [P, KD, 2, T], F32R, phase)
        u_t = sb("u_t", [P, KD, T], F32, phase)
        v_t = sb("v_t", [P, KD, T], F32, phase)
        gate_a = sb("gate_a", [P, KD, T], F32, phase)
        gate_b = sb("gate_b", [P, KD, T], F32, phase)
        early = ExitStack()
        ws = sb("ws", [P, KD, P], F32, early)
        bs = sb("bs", [1, KD * P], F32, early)
        v_nat = sb("v_nat", [P, KD, TT, P], F32, early)
        YA = sb("YA", [P, KD, 2, T], F32R, early)
        mod_row = sb("mod_row", [2, 4 * CHUNK], F32, early)
        c_f = sb("c_f", [P, KD], F32, early)
        c_s = sb("c_s", [P, KD], F32, early)
        rel = sb("rel", [33, HEADS], F32, early)
        onehot = sb("onehot", [33, BIAS_COLS], F32, early)
        early.close()
        after_ssd = ExitStack()
        MX = sb("MX", [P, KD, 2, T], F32R, after_ssd)
        after_ssd.close()
        xbc = sb("xbc", [P, 32, T], F32, phase)
        conv_stack = ExitStack()
        pad = sb("pad", [P, BANKS, T + 4], F32, conv_stack)
        conv_stack.close()
        z_t = sb("z_t", [P, 16, T], F32, phase)
        tri = sb("tri", [P, P], F32, phase)
        heads = sb("heads", [P, 2, 32], F32, phase)
        c_r = sb("c_r", [P, KD, P], F32R, phase)
        dt_stack = ExitStack()
        wdt = sb("wdt", [P, KD, 32], F32, dt_stack)
        wdt_r = sb("wdt_r", [P, KD, 2, 32], F32R, dt_stack)
        dt_stack.close()
        cb = sb("cb", [P, 2, 3 * P], F32, phase)
        dtv = sb("dtv", [P, 5, TT, 32], F32, phase)
        ea = sb("ea", [P, 32], F32, phase)
        cum_r = sb("cum_r", [32, 2, T], F32R, phase)
        phase.close()
        rev_stack = ExitStack()
        for k in range(2):
            sb(f"rev_skip{k}", [P, 2 * KD, T], F32, rev_stack)
        rev = sb("rev", [P, HEADS, BIAS_COLS], F32, rev_stack)
        rev_stack.close()
        yb_stack = ExitStack()
        YB = sb("YB", [P, 16, 2, T], F32R, yb_stack)
        yb_stack.close()
        second = ExitStack()
        sb("H_again", [P, KD, 2, T], F32, second)
        near = sb("near", [P, HEADS, T], F32, second)
        mlp = ExitStack()
        HH = sb("HH", [P, 32, 2, T], F32R, mlp)
        mlp.close()
        attn = ExitStack()
        qkv = sb("qkv", [P, 24, T], F32, attn)
        v_tok = sb("v_tok", [P, TT, D], F32, attn)
        probs = sb("probs", [P, 2, 3 * P], F32, attn)
        probs_t = sb("probs_t", [P, 2, 3 * P], F32, attn)
        sm = sb("sm", [P, HEADS, 8], F32, attn)
        o_t = sb("o_t", [P, 2, T], F32, attn)
        attn.close()
        pooling = ExitStack()
        PG = sb("PG", [P, KD, 2, T], F32R, pooling)
        pu = sb("pu", [P, KD, T], F32, pooling)
        pw = sb("pw", [P, 4, KD, T], F32, pooling)
        pooled = sb("pooled", [P, KD, T], F32, pooling)
        pooling.close()
        inv_stack = ExitStack()
        sb("inv_skip", [P, 32, 2, T], F32, inv_stack)
        inv = sb("inv", [P, 4, 16], F32, inv_stack)
        inv_stack.close()
        second.close()

        banks = ctx.enter_context(nc.psum_tensor("banks", [P, 2 * BANKS, CHUNK], F32))

        def sem(name):
            return ctx.enter_context(nc.semaphore(name))

        loaded = [sem(f"panel_loaded_{r}") for r in range(RAW)]
        panel_hi, panel_lo, panel_used = sem("panel_hi"), sem("panel_lo"), sem("panel_used")
        corrected, summed, activated = sem("corrected"), sem("summed"), sem("activated")
        posted, operand_hi, operand_lo = sem("posted"), sem("operand_hi"), sem("operand_lo")
        bank_done, bank_corr, bank_sum, bank_x = (sem(f"bank_{n}") for n in ("done", "corrected", "summed", "x"))
        act_step = sem("act_step")
        vec_step = sem("vec_step")
        S = {n: sem(n) for n in (
            "x_loaded params_loaded c_loaded late_loaded consts_ready c_silu c_hi c_lo c_zero mod_cols mod_ready "
            "squares stat_sums stat_var stat_root norm_scaled norm_y norm_hi norm_lo norm_x ident_r_ready "
            "sgu_vn sgu_vt sgu_vcopy sgu_mix sgu_y sgu_hi sgu_lo ws_masked "
            "wdt_hi wdt_lo dt_raw dt_corr dt_y dt_exp dt_one dt_ln dt_ea dt_a cum_done cum_got cum_hi cum_lo "
            "cb_done cb_copied cb_masked xt_done xdt_done row_done seg_done exp_done m_done y_done y_skip "
            "y_gated y_sq y_sums y_var y_root y_f y_hi y_lo "
            "rel_loaded rel_masked rev_done rev_copied rev_stored near_loaded "
            "vt_done v_copied s_done s_biased s_max conv_first conv_tap tiny_set p_exp p_norm pt_done pt_copied o_done o_copied o_hi o_lo "
            "pool_hi pool_lo pool_f inv_loaded x_stored").split()}

        block = ctx.enter_context(nc.Block())
        xb = XS[:, :, 0, :]
        conv_w = cols[:, COLS["conv_w"]:COLS["conv_w"] + 32 * CONV].rearrange("p (g n) -> p g n", n=BANKS * CONV)
        conv_b = cols[:, COLS["conv_b"]:COLS["conv_b"] + 32].rearrange("p (g b) -> p g b", b=BANKS)
        sq = XS[:, :, 1, :]
        ev8 = ev[:, :, :, :].rearrange("p a b t -> p (a b) t")

        def decay(n):
            flat = ev[:, :, :, :].rearrange("p a b t -> p (a b t)")
            return flat[:, n % 2 * 6 * P:(n % 2 + 1) * 6 * P]

        mod_tail = ev[0:2, :, :, :].rearrange("p a b t -> p (a b t)")[:, 12 * P:16 * P]

        def xdt(g, t):
            return XS[:, 4 + 2 * (g % 2) + t, 1, :]

        def stat_bank(stage):
            return 0 if stage is None else BANKS * (FIRST_GROUP[INDEX[stage] + 1] % 2)

        def by_group(t):
            return t.rearrange("p (g b) t -> p g b t", b=BANKS)

        def need(eng, s, value):
            if not (isinstance(value, int) and value <= 0):
                eng.wait_ge(s, value)

        def groups(eng, s, body):
            n = STAGES[s][2]
            if n >= 4 and s:
                with eng.Fori(0, n // 2) as turn:
                    body(2 * turn, 0, turn)
                    body(2 * turn + 1, 1, turn)
                if n % 2:
                    body(n - 1, 0, None)
            else:
                for g in range(n):
                    body(g, g % 2, None)

        def by_bank(s, g):
            return STAGES[s][0] in NORMED and isinstance(g, int) and g == STAGES[s][2] - 1

        def bank_count(s, b):
            return (BANKS - 1) * NORMED.index(STAGES[s][0]) + b + 1

        def split_slot(s, u, p):
            return (FIRST_PANEL[s] + 2 * u + p) % SPLIT

        def ahead(s, g, u, turn, p):
            q = FIRST_PANEL[s] + 2 * g + p + SPLIT
            place = FIRST_PANEL[s] + 2 * u + p + SPLIT
            if turn is None:
                return q, q % RAW, q % SPLIT, q // RAW
            return q, place % RAW, place % SPLIT, turn + place // RAW

        def through(s, g):
            kb = STAGES[s][1]
            return FIRST_PANEL[s] + (2 * g + 2 if kb == 8 else -(-kb * (g + 1) // 4))

        def run(eng, s, split, take_up):
            kb, n = STAGES[s][1:3]
            if kb == 8:
                def body(g, u, turn):
                    split(*ahead(s, g, u, turn, 0))
                    last = isinstance(g, int) and g == n - 1
                    if last:
                        take_up(s, g, (FIRST_GROUP[s] + u) % 2)
                    split(*ahead(s, g, u, turn, 1))
                    if not last:
                        take_up(s, g, (FIRST_GROUP[s] + u) % 2)
                groups(eng, s, body)
                return
            for q in range(FIRST_PANEL[s], FIRST_PANEL[s + 1]):
                a = q + SPLIT
                last = q == FIRST_PANEL[s + 1] - 1
                if a < PANELS and not last:
                    split(a, a % RAW, a % SPLIT, a // RAW)
                for g in range(n):
                    if through(s, g) == q + 1:
                        take_up(s, g, (FIRST_GROUP[s] + g) % 2)
                if a < PANELS and last:
                    split(a, a % RAW, a % SPLIT, a // RAW)

        @block.sync
        def _(sp):
            sp.dma_start(cols[:, :], cols_in).then_inc(S["params_loaded"], 16)
            sp.dma_start(c_f[:, :], c_in).then_inc(S["c_loaded"], 16)
            sp.dma_start(raw[:, 0, :], panels[0]).then_inc(loaded[0], 16)
            sp.dma_start(raw[:, 1, :], panels[1]).then_inc(loaded[1], 16)
            sp.dma_start(xb, x_in).then_inc(S["x_loaded"], 16)
            for r in range(2, RAW):
                sp.dma_start(raw[:, r, :], panels[r]).then_inc(loaded[r], 16)

            def refill(n, r):
                sp.wait_ge(panel_lo, 2 * (RAW * n + r - RAW + 1))
                sp.dma_start(raw[:, r, :], panels[RAW * n + r]).then_inc(loaded[r], 16)

            with sp.Fori(1, PANELS // RAW) as n:
                for r in range(RAW):
                    refill(n, r)
            for q in range(PANELS // RAW * RAW, PANELS):
                refill(q // RAW, q % RAW)
            for g in range(2):
                sp.wait_ge(S["norm_x"], KD * 5 + BANKS * (g + 1))
                half = slice(BANKS * g, BANKS * g + BANKS)
                sp.dma_start(out[:, half, :], xb[:, half, :]).then_inc(S["x_stored"], 16)
            sp.wait_ge(S["x_stored"], 32)

        @block.gpsimd
        def _(pool):
            pool.memset(c_r[:, :, :].bitcast(F32), 0.0).then_inc(S["c_zero"], 1)
            pool.memset(ident[:, :], 0.0).then_inc(S["consts_ready"], 1)
            pool.memset(ones[:, :], 1.0).then_inc(S["consts_ready"], 1)
            pool.memset(mean_w[:, :], 1.0 / D).then_inc(S["consts_ready"], 1)
            pool.memset(gmean_w[:, :], 1.0 / T).then_inc(S["consts_ready"], 1)
            pool.memset(tri[:, :], 1.0).then_inc(S["consts_ready"], 1)
            pool.wait_ge(S["consts_ready"], 5)
            pool.affine_select(out=ident[:, :], in_=ident[:, :], compare_op=ALU.not_equal, fill=1.0,
                               base=0, pattern=[[-1, P]], channel_multiplier=1).then_inc(S["consts_ready"], 1)
            pool.affine_select(out=tri[:, :], in_=tri[:, :], compare_op=ALU.is_ge, fill=0.0,
                               base=0, pattern=[[1, P]], channel_multiplier=-1).then_inc(S["consts_ready"], 1)
            pool.dma_start(ws[:, :, :], ws_in).then_inc(S["late_loaded"], 16)
            pool.dma_start(bs[:, :], bs_in).then_inc(S["late_loaded"], 16)
            pool.dma_start(wdt[:, :, :], wdt_in).then_inc(S["late_loaded"], 16)
            pool.dma_start(heads[:, :, :], heads_in).then_inc(S["late_loaded"], 16)
            pool.wait_ge(S["late_loaded"], 64)
            pool.affine_select(out=ws[:, :, :], in_=ws[:, :, :], compare_op=ALU.is_ge, fill=0.0, base=0,
                               pattern=[[0, KD], [1, P]], channel_multiplier=-1).then_inc(S["ws_masked"], 1)
            pool.wait_ge(S["ws_masked"], 1)
            pool.memset(rel[32:33, :], MASKED).then_inc(S["rel_masked"], 1)
            pool.dma_start(rel[0:32, :], rel_in).then_inc(S["rel_loaded"], 16)
            pool.dma_start(onehot[:, :], onehot_in).then_inc(S["rel_loaded"], 16)
            pool.wait_ge(S["rev_copied"], HEADS)
            pool.dma_start(skew.rearrange("q (h t) -> q h t", t=BIAS_COLS), rev[:, :, :]).then_inc(S["rev_stored"], 16)
            pool.wait_ge(S["rev_stored"], 16)
            pairs = 2 * SSM_GROUPS
            for n in range(pairs + 5):
                if n < pairs and n % 2 == 0:
                    g = n // 2
                    pool.wait_ge(S["cb_copied"], g + 1)
                    both = cb[:, g % 2, :].rearrange("p (a i) -> p a i", i=P)[:, 0:3:2, :]
                    pool.affine_select(out=both, in_=both, compare_op=ALU.is_ge, fill=0.0, base=0,
                                       pattern=[[0, 2], [1, P]], channel_multiplier=-1).then_inc(S["cb_masked"], 1)
                if n < pairs:
                    pool.wait_ge(S["exp_done"], n + 1)
                    pool.wait_ge(S["cb_masked"], n // 2 + 1)
                    two = decay(n).rearrange("p (r i) -> p r i", r=2)
                    pool.tensor_tensor(two, two, cb[:, n // 2 % 2, :].unsqueeze(1).to_broadcast([P, 2, 3 * P]),
                                       ALU.mult).then_inc(S["m_done"], 1)
                if 2 <= n < pairs + 2:
                    m = n - 2
                    pool.wait_ge(S["y_skip"], m + 1)
                    pool.tensor_tensor(xbc[:, m, :], xbc[:, m, :], z_t[:, m, :], ALU.mult).then_inc(S["y_gated"], 1)
                if n >= 6 and n % 2 == 0:
                    g = (n - 6) // 2
                    two = slice(2 * g, 2 * g + 2)
                    pool.wait_ge(S["y_hi"], g + 1)
                    pool.tensor_tensor(YB[:, two, 1, :], xbc[:, two, :], YB[:, two, 0, :], ALU.subtract)\
                        .then_inc(S["y_lo"], 1)
            pool.wait_ge(panel_used, FIRST_PANEL[INDEX["out"]])
            row = HEADS * BIAS_COLS - 1
            skewed = skew.rearrange("q n -> (q n)")[P - 1:P - 1 + P * row].rearrange("(q n) -> q n", n=row)
            for h in range(HEADS):
                pool.dma_start(near[:, h, :], skewed[:, h * BIAS_COLS:h * BIAS_COLS + T]).then_inc(S["near_loaded"], 16)
            pool.wait_ge(panel_used, FIRST_PANEL[INDEX["ff1"]])
            pool.dma_start(inv[:, :, :], inv_in).then_inc(S["inv_loaded"], 16)
            for i in range(5):
                for m in range(KD):
                    pool.wait_ge(S["norm_lo"], KD * (3 + i) + m + 1)
                    at = COLS["ln_b"] + KD * i + m
                    pool.tensor_scalar(xb[:, m, :], xb[:, m, :], cols[:, at:at + 1], None, ALU.add)\
                        .then_inc(S["norm_x"], 1)

        @block.tensor
        def _(pe):
            def products(group_u, panel_slot, operand, k, starts, stops, chunks=range(4), ready=None, each=None):
                order = [(b, c) for b in range(BANKS) for c in chunks]
                if ready is not None:
                    order.sort(key=lambda bc: bc[1])
                for b, c in order:
                    acc = banks[:, BANKS * group_u + b, :]
                    at = c * CHUNK + b * P
                    kk = k + c - chunks[0]
                    if ready is not None and b == 0:
                        ready(kk + 1)
                    pair = operand[:, kk, :, :].rearrange("p a t -> p (a t)")
                    pe.matmul(acc, w_hi[:, panel_slot, at:at + P], pair,
                              start=starts and c == chunks[0], stop=False)
                    last = pe.matmul(acc[:, 0:T], w_lo[:, panel_slot, at:at + P], pair[:, 0:T],
                                     start=False, stop=stops and c == chunks[-1])
                    if each is not None and b < BANKS - 1 and c == chunks[-1]:
                        last.then_inc(each, 1)
                return last

            def psum_free(s, g):
                need(pe, summed, FIRST_GROUP[s] + g - 1)

            def stage_k8(name, operand, ready=None):
                s = INDEX[name]

                def body(g, u, turn):
                    for p in range(2):
                        pe.wait_ge(panel_lo, 2 * (FIRST_PANEL[s] + 2 * g + p + 1))
                        if p == 0:
                            psum_free(s, g)
                        first = isinstance(g, int) and g == 0
                        products((FIRST_GROUP[s] + u) % 2, split_slot(s, u, p), operand, 4 * p, p == 0, p == 1,
                                 ready=ready if first else None, each=bank_done if p and by_bank(s, g) else None)\
                            .then_inc(panel_used, 1)

                n = STAGES[s][2]
                if ready is None or n < 4:
                    groups(pe, s, body)
                    return
                body(0, 0, None)
                with pe.Fori(0, (n - 1) // 2) as turn:
                    body(2 * turn + 1, 1, turn)
                    body(2 * turn + 2, 0, turn)
                if n % 2 == 0:
                    body(n - 1, 1, None)

            def norm_block(n):
                return lambda k: pe.wait_ge(S["norm_lo"], KD * n + k)

            def operand_of(name, blocks):
                return lambda k: pe.wait_ge(operand_lo, before("operand", INDEX[name]) + -(-k // blocks))

            def stage_long(name, operand, kb, ready):
                s = INDEX[name]
                for q in range(panels_of(STAGES[s])):
                    pe.wait_ge(panel_lo, 2 * (FIRST_PANEL[s] + q + 1))
                    parts = {}
                    for c in range(4):
                        parts.setdefault((4 * q + c) // kb, []).append(c)
                    for g, chunks in parts.items():
                        k = 4 * q + chunks[0] - g * kb
                        if k == 0:
                            psum_free(s, g)
                        if g == 0:
                            ready(k + len(chunks))
                        last = products((FIRST_GROUP[s] + g) % 2, (FIRST_PANEL[s] + q) % SPLIT, operand, k,
                                        k == 0, k + len(chunks) == kb, chunks=chunks,
                                        each=bank_done if k + len(chunks) == kb and by_bank(s, g) else None)
                    last.then_inc(panel_used, 1)

            def mod_panel(s, g, p, acc):
                q = FIRST_PANEL[s] + 2 * g + p
                pe.wait_ge(panel_lo, 2 * (q + 1))
                if p == 0:
                    need(pe, summed, FIRST_GROUP[s] + g - (0 if s else 1))
                for c in range(4):
                    w = slice(c * CHUNK, c * CHUNK + CHUNK)
                    pe.matmul(acc, c_r[:, 4 * p + c, :], w_hi[:, q % SPLIT, w], start=p == 0 and c == 0, stop=False)
                    last = pe.matmul(acc, c_r[:, 4 * p + c, :], w_lo[:, q % SPLIT, w], start=False,
                                     stop=p == 1 and c == 3)
                last.then_inc(panel_used, 1)

            def mod_columns(rows, to, n):
                for m in range(n):
                    last = pe.matmul(to[:, m:m + 1], rows[0:2, m * P:m * P + P], ones[0:2, 0:1], start=True, stop=True)
                last.then_inc(S["mod_cols"], 1)

            def stats(n, mean, stage=None):
                for m in range(KD):
                    pe.wait_ge(S["squares"], KD * n + m + 1)
                    rhs = XS[:, m, :, :].rearrange("p a t -> p (a t)") if mean else sq[:, m, :]
                    b = stat_bank(stage)
                    to = banks[:, b, :] if mean else banks[:, b, T:2 * T]
                    last = pe.matmul(to, mean_w[:, :], rhs, start=m == 0, stop=m == KD - 1)
                last.then_inc(S["stat_sums"], 1)

            def bias_rows():
                pe.wait_ge(S["rel_loaded"], 32)
                pe.wait_ge(S["rel_masked"], 1)
                for h in range(HEADS):
                    if h >= 2:
                        pe.wait_ge(S["rev_copied"], h - 1)
                    pe.matmul(banks[:, 1 + h % 2, :], rel[0:33, h:h + 1].to_broadcast([33, P]), onehot[:, :],
                              start=True, stop=True).then_inc(S["rev_done"], 1)

            pe.wait_ge(S["consts_ready"], 7)
            stats(0, False)
            bias_rows()
            pe.wait_ge(S["rev_copied"], HEADS)
            pe.wait_ge(S["c_lo"], 1)
            for g in range(4):
                for p in range(2):
                    mod_panel(0, g, p, banks[:, BANKS * (g % 2), :])
            pe.wait_ge(summed, 4)
            mod_columns(mod_row, banks[:, 7, 0:16], 16)
            stage_k8("u", H, norm_block(0))
            for name in ("v", "gate_a", "gate_b"):
                stage_k8(name, H)

            pe.wait_ge(summed, FIRST_GROUP[INDEX["branch_gm"]])
            stats(1, False)
            for m in range(KD):
                if m % 4 == 0:
                    pe.wait_ge(S["sgu_vn"], m // 4 + 1)
                for t in range(TT):
                    last = pe.transpose(banks[:, 1 + m // 2, (m % 2 * TT + t) * P:(m % 2 * TT + t + 1) * P],
                                        v_t[:, m, t * P:t * P + P], ident[:, :])
                if m % 2:
                    last.then_inc(S["sgu_vt"], 1)
            pe.wait_ge(S["ws_masked"], 1)
            for m in range(KD):
                if m % 2 == 0:
                    pe.wait_ge(S["sgu_vcopy"], m // 2 + 1)
                for t in range(TT):
                    to = banks[:, (5, 6, 7, 0)[m // 2], (m % 2 * TT + t) * P:(m % 2 * TT + t + 1) * P]
                    pe.matmul(to, v_nat[:, m, t, :], ws[:, m, :], start=True, stop=False)
                    last = pe.matmul(to, ones[0:1, :], bs[0:1, m * P:m * P + P], start=False, stop=True)
                if m % 2:
                    last.then_inc(S["sgu_mix"], 1)
            stage_k8("branch_gm", YA, lambda k: pe.wait_ge(S["sgu_lo"], 4))
            stage_k8("xbc", H)
            stage_k8("z", H)

            pe.wait_ge(summed, FIRST_GROUP[INDEX["mod_rest"]])
            pe.wait_ge(S["wdt_lo"], 1)
            for t in range(TT):
                acc = banks[:, 4, t * 64:t * 64 + 64]
                for k in range(KD):
                    pe.matmul(acc, H[:, k, 0, t * P:t * P + P], wdt_r[:, k, :, :].rearrange("p a h -> p (a h)"),
                              start=k == 0, stop=False)
                    last = pe.matmul(acc[:, 0:32], H[:, k, 1, t * P:t * P + P], wdt_r[:, k, 0, :],
                                     start=False, stop=k == KD - 1)
            last.then_inc(S["dt_raw"], 1)
            a_v = dtv[:, 3, :, :]
            pe.wait_ge(S["dt_a"], 1)
            pe.matmul(banks[:, 5, 0:32], tri[:, :], a_v[:, 0, :], start=True, stop=True)
            pe.matmul(banks[:, 5, 32:64], ones[:, :], a_v[:, 0, :], start=True, stop=False)
            pe.matmul(banks[:, 5, 32:64], tri[:, :], a_v[:, 1, :], start=False, stop=True)
            pe.matmul(banks[0:32, 6, 0:P], a_v[:, 0, :], tri[:, :], start=True, stop=True)
            pe.matmul(banks[0:32, 6, P:T], a_v[:, 0, :], ones[:, :], start=True, stop=False)
            pe.matmul(banks[0:32, 6, P:T], a_v[:, 1, :], tri[:, :], start=False, stop=True)\
                .then_inc(S["cum_done"], 1)

            B = xbc[:, 16:24, :]
            C = xbc[:, 24:32, :]

            rest = INDEX["mod_rest"]

            def rest_columns(g):
                pe.wait_ge(summed, FIRST_GROUP[rest] + g + 1)
                mod_columns(mod_tail, banks[:, 1, 3 * P + 4 * g:3 * P + 4 * g + 4], 4)

            def scores_and_tokens(g):
                if g:
                    pe.wait_ge(S["cb_copied"], g)
                pe.matmul(banks[:, 1, 0:T], B[:, g, 0:P], C[:, g, :], start=True, stop=True)
                pe.matmul(banks[:, 1, T:3 * P], B[:, g, P:T], C[:, g, P:T], start=True, stop=True)\
                    .then_inc(S["cb_done"], 1)
                if g:
                    pe.wait_ge(S["xdt_done"], 2 * g)
                for t in range(TT):
                    for m in range(2):
                        last = pe.transpose(banks[:, 2, (2 * t + m) * P:(2 * t + m + 1) * P],
                                            xbc[:, 2 * g + m, t * P:t * P + P], ident[:, :])
                last.then_inc(S["xt_done"], 1)

            def decay_rows(n):
                if n >= 2:
                    pe.wait_ge(S["seg_done"], 4 * (n - 1))
                for r in range(2):
                    h = 2 * n + r
                    pick = ident_r[:, h:h + 1].to_broadcast([32, P])
                    pe.matmul(banks[:, 3 + n % 2, r * T:r * T + T], pick, cum_r[:, 0, :], start=True, stop=False)
                    last = pe.matmul(banks[:, 3 + n % 2, r * T:r * T + T], pick, cum_r[:, 1, :], start=False, stop=True)
                last.then_inc(S["row_done"], 1)

            def head_outputs(n):
                g = n // 2
                pe.wait_ge(S["m_done"], n + 1)
                pe.wait_ge(S["xdt_done"], 2 * (g + 1))
                if n >= 2:
                    pe.wait_ge(S["y_skip"], n - 1)
                m_of = decay(n)
                for r in range(2):
                    to = banks[HP * r:HP * r + HP, 5 + n % 2, 0:T]
                    cut = slice((n % 2 * 2 + r) * HP, (n % 2 * 2 + r + 1) * HP)
                    pe.matmul(to, xdt(g, 0)[:, cut], m_of[:, r * 3 * P:r * 3 * P + T], start=True, stop=False)
                    last = pe.matmul(to[:, P:T], xdt(g, 1)[:, cut], m_of[:, r * 3 * P + T:(r + 1) * 3 * P],
                                     start=False, stop=True)
                last.then_inc(S["y_done"], 1)

            def group_sums(g):
                pe.wait_ge(S["y_sq"], 2 * (g + 1))
                if g:
                    pe.wait_ge(S["y_var"], g)
                for m in range(2):
                    last = pe.matmul(banks[:, 7, 0:T], gmean_w[:, :], sq[:, 2 * (g % 2) + m, :],
                                     start=m == 0, stop=m == 1)
                last.then_inc(S["y_sums"], 1)

            pe.wait_ge(S["cum_lo"], 1)
            pe.wait_ge(S["cum_got"], 1)
            pe.wait_ge(S["ident_r_ready"], 1)
            pairs = 2 * SSM_GROUPS
            for n in range(pairs + 3):
                if n < pairs and n % 2 == 0:
                    scores_and_tokens(n // 2)
                if n < pairs:
                    decay_rows(n)
                    if n % 2 and n > 1:
                        pe.wait_ge(S["cb_copied"], n // 2 + 1)
                        rest_columns(n // 2 - 1)
                    mod_panel(rest, n // 2, n % 2, banks[:, 0, :])
                if 0 < n <= pairs:
                    head_outputs(n - 1)
                if n >= 4 and n % 2 == 0:
                    group_sums((n - 4) // 2)

            pe.wait_ge(S["cb_copied"], SSM_GROUPS)
            rest_columns(SSM_GROUPS - 1)
            pe.wait_ge(S["mod_ready"], 2)
            stage_long("branch_ssm", YB, 16, lambda k: pe.wait_ge(S["y_lo"], k // 2))
            stage_k8("out", MX, operand_of("branch_ssm", 4))
            stats(2, False, "out")
            stage_k8("ff1", H, norm_block(1))
            stage_long("ff2", HH, 32, operand_of("ff1", 4))
            stats(3, False, "ff2")

            norm = [4]

            def feed_forward(i):
                stage_k8(f"gu{i}", H, norm_block(norm[0] - 2))
                stage_long(f"down{i}", HH, 22, operand_of(f"gu{i}", 2))
                stats(norm[0], True, f"down{i}")
                norm[0] += 1

            feed_forward(0)

            stage_k8("qkv", H, norm_block(norm[0] - 2))
            pe.wait_ge(summed, FIRST_GROUP[INDEX["att_out"]])
            for h in range(HEADS):
                for t in range(TT):
                    last = pe.transpose(banks[:, h // 2, (h % 2 * TT + t) * P:(h % 2 * TT + t + 1) * P],
                                        qkv[:, 16 + h, t * P:t * P + P], ident[:, :])
                if h % 2:
                    last.then_inc(S["vt_done"], 1)

            def att_scores(h):
                if h >= 2:
                    pe.wait_ge(S["s_max"], h - 1)
                to = banks[:, 4 + h % 2, :]
                pe.matmul(to[:, 0:P], qkv[:, h, 0:P], qkv[:, 8 + h, 0:P], start=True, stop=True)
                pe.matmul(to[:, P:3 * P], qkv[:, h, P:T], qkv[:, 8 + h, :], start=True, stop=True)\
                    .then_inc(S["s_done"], 1)

            def att_transpose(h):
                pe.wait_ge(S["p_norm"], h + 1)
                if h >= 1:
                    pe.wait_ge(S["pt_copied"], h)
                for n in range(3):
                    last = pe.transpose(banks[:, 6, n * P:n * P + P], probs[:, h % 2, n * P:n * P + P], ident[:, :])
                last.then_inc(S["pt_done"], 1)

            def att_values(h):
                pe.wait_ge(S["pt_copied"], h + 1)
                if h >= 1:
                    pe.wait_ge(S["o_copied"], h)
                pe.matmul(banks[:, 7, 0:T], v_tok[:, 0, h * P:h * P + P], probs_t[:, h % 2, 0:T], start=True, stop=False)
                pe.matmul(banks[:, 7, P:T], v_tok[:, 1, h * P:h * P + P], probs_t[:, h % 2, T:3 * P],
                          start=False, stop=True).then_inc(S["o_done"], 1)

            pe.wait_ge(S["v_copied"], 4)
            for h in range(HEADS + 2):
                if h < HEADS:
                    att_scores(h)
                if 1 <= h <= HEADS:
                    att_transpose(h - 1)
                if h >= 2:
                    att_values(h - 2)
            pe.wait_ge(S["o_lo"], HEADS)
            stage_k8("att_out", H)
            stats(norm[0], True, "att_out")
            norm[0] += 1
            feed_forward(1)
            feed_forward(2)

            stage_k8("pool_in", H, norm_block(norm[0] - 2))
            s = INDEX["pool_group"]
            pe.wait_ge(panel_lo, 2 * (FIRST_PANEL[s] + 1))
            pe.wait_ge(summed, FIRST_GROUP[s])
            for m in range(KD):
                if m % 4 == 0:
                    pe.wait_ge(S["pool_lo"], m // 4 + 1)
                for k in range(2):
                    at = (m // 2) * CHUNK + k * T + (m % 2) * P
                    pair = PG[:, m // 2 * 2 + k, :, :].rearrange("p a t -> p (a t)")
                    acc = banks[:, BANKS * ((FIRST_GROUP[s] + m // 4) % 2) + m % 4, :]
                    pe.matmul(acc, w_hi[:, FIRST_PANEL[s] % SPLIT, at:at + P], pair, start=k == 0, stop=False)
                    last = pe.matmul(acc[:, 0:T], w_lo[:, FIRST_PANEL[s] % SPLIT, at:at + P], pair[:, 0:T],
                                     start=False, stop=k == 1)
            last.then_inc(panel_used, 1)
            stage_k8("pool_out", H, operand_of("pool_group", 4))
            stats(norm[0], True, "pool_out")
            norm[0] += 1
            feed_forward(3)

        @block.scalar
        def _(act):
            def split(q, r, sl, turn):
                act.wait_ge(loaded[r], 16 * turn + 16)
                need(act, panel_used, q - SPLIT + 1)
                for half in range(2):
                    w = slice(half * PANEL // 2, (half + 1) * PANEL // 2)
                    act.activation(w_hi[:, sl, w], raw[:, r, w], ACT.Copy).then_inc(panel_hi, 1)

            def square(s, g, b):
                if b < BANKS - 1:
                    act.wait_ge(bank_x, bank_count(s, b))
                else:
                    act.wait_ge(posted, before("posted", s) + g + 1)
                act.activation(sq[:, BANKS * g + b, :], xb[:, BANKS * g + b, :], ACT.Square).then_inc(S["squares"], 1)

            def correction(s, g, G):
                kind = STAGES[s][3]
                if kind in ("act", "conv"):
                    need(act, activated, before("activated", s) + g - 1)
                elif kind in ("gate", "add1", "deep"):
                    need(act, posted, before("posted", s) + g - 1)
                elif kind in COUNTED["operand"]:
                    need(act, operand_lo, before("operand", s) + g - 1)
                elif kind == "keep":
                    need(act, summed, FIRST_GROUP[s] + g - 1)
                if by_bank(s, g):
                    for b in range(BANKS):
                        if b < BANKS - 1:
                            act.wait_ge(bank_done, bank_count(s, b))
                        else:
                            act.wait_ge(panel_used, through(s, g))
                        act.activation(ev[:, G, b, :], banks[:, BANKS * G + b, T:CHUNK], ACT.Copy)\
                            .then_inc(bank_corr if b < BANKS - 1 else corrected, 1)
                        if b:
                            square(s, g, b - 1)
                    square(s, g, BANKS - 1)
                    return
                act.wait_ge(panel_used, through(s, g))
                act.activation(ev[:, G, :, :], banks[:, BANKS * G:BANKS * G + BANKS, T:CHUNK], ACT.Copy)\
                    .then_inc(corrected, 1)

            def stage(name, post):
                def take_up(s, g, G):
                    if STAGES[s][3] != "mod":
                        correction(s, g, G)
                        post(s, g, G)
                run(act, INDEX[name], split, take_up)

            def nothing(s, g, G):
                pass

            def activate_into(func, dest):
                def post(s, g, G):
                    act.wait_ge(summed, FIRST_GROUP[s] + g + 1)
                    act.activation(by_group(dest[:, :, :])[:, g, :, :], ev[:, G, :, :], func).then_inc(activated, 1)
                return post

            def v_post(s, g, G):
                activate_into(ACT.Gelu_apprx_tanh, v_t)(s, g, G)
                act.wait_ge(activated, before("activated", s) + g + 1)
                act.activation(by_group(sq)[:, g, :, :], by_group(v_t[:, :, :])[:, g, :, :], ACT.Square)\
                    .then_inc(S["squares"], BANKS)

            def conv_first_tap(s, g, G):
                act.wait_ge(summed, FIRST_GROUP[s] + g + 1)
                for b in range(BANKS):
                    last = act.activation(ev[:, G, b, :], pad[:, b, 0:T], ACT.Identity, bias=conv_b[:, g, b:b + 1],
                                          scale=conv_w[:, g, CONV * b:CONV * b + 1])
                last.then_inc(S["conv_first"], 1)

            def conv_silu(s, g, G):
                act.wait_ge(posted, before("posted", s) + g + 1)
                act.activation(by_group(xbc[:, :, :])[:, g, :, :], ev[:, G, :, :], ACT.Silu).then_inc(activated, 1)

            def round_into(dest, blocks=BANKS):
                view = dest[:, :, 0, :].rearrange("p (g b) t -> p g b t", b=blocks)

                def post(s, g, G):
                    act.wait_ge(posted, before("posted", s) + g + 1)
                    act.activation(view[:, g, :, :], ev[:, G, 0:blocks, :], ACT.Copy).then_inc(operand_hi, 1)
                return post

            def glu_post(s, g, G):
                act.wait_ge(summed, FIRST_GROUP[s] + g + 1)
                act.activation(ev[:, G, 0:2, :], ev[:, G, 0:2, :], ACT.Silu).then_inc(activated, 1)
                round_into(HH, 2)(s, g, G)

            def squares_post(s, g, G):
                if by_bank(s, g):
                    return
                act.wait_ge(posted, before("posted", s) + g + 1)
                act.activation(by_group(sq)[:, g, :, :], by_group(xb)[:, g, :, :], ACT.Square)\
                    .then_inc(S["squares"], BANKS)

            act.wait_ge(S["tiny_set"], 1)

            def load_table(func):
                act.activation(tiny[:, 1:2], tiny[:, 0:1], func).then_inc(act_step, 1)

            def root(n):
                load_table(ACT.Sqrt)
                act.wait_ge(S["stat_var"], n + 1)
                act.activation(st[:, 1, :], st[:, 1, :], ACT.Sqrt).then_inc(S["stat_root"], 1)

            def norm_rounded(k, src, bias):
                for m in range(KD):
                    act.wait_ge(S["norm_y"], KD * k + m + 1)
                    if bias is None:
                        ins = act.activation(H[:, m, 0, :], src[:, m, :], ACT.Copy)
                    else:
                        ins = act.activation(H[:, m, 0, :], src[:, m, :], ACT.Identity, bias=bias[:, m:m + 1])
                    ins.then_inc(S["norm_hi"], 1)

            act.wait_ge(S["consts_ready"], 7)
            act.activation(ident_r[:, :], ident[0:32, 0:32], ACT.Copy).then_inc(S["ident_r_ready"], 1)
            act.wait_ge(S["c_loaded"], 16)
            act.activation(c_s[:, :], c_f[:, :], ACT.Silu).then_inc(S["c_silu"], 1)
            act.wait_ge(S["c_silu"], 1)
            act.wait_ge(S["c_zero"], 1)
            act.activation(c_r[:, :, 0], c_s[:, :], ACT.Copy).then_inc(S["c_hi"], 1)
            split(0, 0, 0, 0)
            split(1, 1, 1, 0)
            act.wait_ge(S["x_loaded"], 16)
            for g in range(2):
                act.activation(by_group(sq)[:, g, :, :], by_group(xb)[:, g, :, :], ACT.Square)\
                    .then_inc(S["squares"], BANKS)
            root(0)
            for h in range(HEADS):
                act.wait_ge(S["rev_done"], h + 1)
                act.activation(rev[:, h, :], banks[:, 1 + h % 2, :], ACT.Copy).then_inc(S["rev_copied"], 1)
            stage("mod_norm", nothing)
            norm_rounded(0, ev8, mod[:, 0:8])

            stage("u", activate_into(ACT.Gelu_apprx_tanh, u_t))
            stage("v", v_post)
            act.wait_ge(S["rev_stored"], 16)
            stage("gate_a", activate_into(ACT.Sigmoid, gate_a))
            stage("gate_b", activate_into(ACT.Sigmoid, gate_b))
            root(1)
            for j in range(4):
                act.wait_ge(S["sgu_vt"], j + 1)
                act.activation(v_nat[:, 2 * j:2 * j + 2, :, :].rearrange("p m t d -> p (m t d)"),
                               banks[:, 1 + j, :], ACT.Copy).then_inc(S["sgu_vcopy"], 1)
            for j in range(4):
                act.wait_ge(S["sgu_y"], j + 1)
                act.activation(YA[:, 2 * j:2 * j + 2, 0, :], ev8[:, 2 * j:2 * j + 2, :], ACT.Copy)\
                    .then_inc(S["sgu_hi"], 1)
            stage("branch_gm", nothing)
            load_table(ACT.Silu)
            s = INDEX["xbc"]
            G = FIRST_GROUP[s] % 2

            def conv_body(g, u, turn, silu=True):
                split(*ahead(s, g, u, turn, 0))
                split(*ahead(s, g, u, turn, 1))
                correction(s, g, (G + u) % 2)
                conv_first_tap(s, g, (G + u) % 2)
                if silu:
                    conv_silu(s, g - 1, (G + u + 1) % 2)

            n = STAGES[s][2]
            conv_body(0, 0, None, False)
            conv_body(1, 1, None)
            with act.Fori(1, n // 2) as turn:
                conv_body(2 * turn, 0, turn)
                conv_body(2 * turn + 1, 1, turn)
            conv_silu(s, n - 1, (G + 1) % 2)
            stage("z", activate_into(ACT.Silu, z_t))

            act.wait_ge(S["late_loaded"], 64)
            act.activation(wdt_r[:, :, 0, :], wdt[:, :, :], ACT.Copy).then_inc(S["wdt_hi"], 1)
            act.activation(ea[:, :], heads[:, 1, :], ACT.Exp).then_inc(S["dt_ea"], 1)
            act.wait_ge(S["dt_raw"], 1)
            act.activation(dtv[:, 0, :, :], banks[:, 4, 0:P].rearrange("p (t a h) -> p t a h", t=TT, a=2)[:, :, 1, :],
                           ACT.Copy).then_inc(S["dt_corr"], 1)
            act.wait_ge(S["dt_y"], 1)
            act.activation(dtv[:, 0, :, :], dtv[:, 0, :, :], ACT.Exp).then_inc(S["dt_exp"], 1)
            act.wait_ge(S["dt_one"], 1)
            act.activation(dtv[:, 0, :, :], dtv[:, 0, :, :], ACT.Ln).then_inc(S["dt_ln"], 1)
            act.wait_ge(S["cum_done"], 1)
            act.activation(cum_r[:, 0, :], banks[0:32, 6, 0:T], ACT.Copy).then_inc(S["cum_hi"], 1)

            pairs = 2 * SSM_GROUPS
            for n in range(pairs + 5):
                if n < pairs and n % 2 == 0:
                    g = n // 2
                    act.wait_ge(S["cb_done"], g + 1)
                    if g >= 2:
                        act.wait_ge(S["m_done"], 2 * (g - 1))
                    act.activation(cb[:, g % 2, :], banks[:, 1, 0:3 * P], ACT.Copy).then_inc(S["cb_copied"], 1)
                if n < pairs:
                    act.wait_ge(S["seg_done"], 4 * (n + 1))
                    act.activation(decay(n), decay(n), ACT.Exp).then_inc(S["exp_done"], 1)
                    q = FIRST_PANEL[INDEX["mod_rest"]] + n + SPLIT
                    split(q, q % RAW, q % SPLIT, q // RAW)
                if 2 <= n < pairs + 2:
                    m = n - 2
                    act.wait_ge(S["y_gated"], m + 1)
                    if m >= 4:
                        act.wait_ge(S["y_sums"], m // 2 - 1)
                    act.activation(sq[:, m % 4, :], xbc[:, m, :], ACT.Square).then_inc(S["y_sq"], 1)
                if n >= 4 and n % 2 == 0 and n < pairs + 4:
                    g = (n - 4) // 2
                    act.wait_ge(S["y_var"], g + 1)
                    act.activation(st[:, g % 2, :], st[:, g % 2, :], ACT.Sqrt).then_inc(S["y_root"], 1)
                if 5 <= n < pairs + 5 and n % 2 == 1:
                    g = (n - 5) // 2
                    act.wait_ge(S["y_f"], 2 * (g + 1))
                    act.activation(YB[:, 2 * g:2 * g + 2, 0, :], xbc[:, 2 * g:2 * g + 2, :], ACT.Copy)\
                        .then_inc(S["y_hi"], 1)
            stage("branch_ssm", round_into(MX))
            stage("out", squares_post)
            root(2)
            norm_rounded(1, ev8, mod[:, 24:32])
            stage("ff1", round_into(HH))
            stage("ff2", squares_post)
            root(3)
            norm_rounded(2, xb, None)

            norms = [3]

            def layer_norm(last=False):
                root(norms[0] + 1)
                if not last:
                    at = COLS["ln_b"] + KD * (norms[0] - 3)
                    norm_rounded(norms[0], xb, cols[:, at:at + KD])
                norms[0] += 1

            def feed_forward(i, last=False):
                load_table(ACT.Silu)
                stage(f"gu{i}", glu_post)
                stage(f"down{i}", squares_post)
                layer_norm(last)

            feed_forward(0)
            stage("qkv", nothing)
            for j in range(4):
                act.wait_ge(S["vt_done"], j + 1)
                act.activation(v_tok[:, :, 2 * j * P:(2 * j + 2) * P].rearrange("p t (h d) -> p h t d", h=2),
                               banks[:, j, :].rearrange("p (h t d) -> p h t d", h=2, t=TT), ACT.Copy)\
                    .then_inc(S["v_copied"], 1)
            for h in range(HEADS + 3):
                if h < HEADS:
                    act.wait_ge(S["s_max"], h + 1)
                    act.activation(probs[:, h % 2, 0:P], probs[:, h % 2, 0:P], ACT.Exp, bias=sm[:, h, 2:3],
                                   accum_out=sm[:, h, 4:5]).then_inc(S["p_exp"], 1)
                    act.activation(probs[:, h % 2, P:3 * P], probs[:, h % 2, P:3 * P], ACT.Exp, bias=sm[:, h, 3:4],
                                   accum_out=sm[:, h, 5:6]).then_inc(S["p_exp"], 1)
                if 1 <= h <= HEADS:
                    m = h - 1
                    act.wait_ge(S["pt_done"], m + 1)
                    if m >= 2:
                        act.wait_ge(S["o_done"], m - 1)
                    act.activation(probs_t[:, m % 2, :], banks[:, 6, 0:3 * P], ACT.Copy).then_inc(S["pt_copied"], 1)
                if h >= 3:
                    m = h - 3
                    act.wait_ge(S["o_copied"], m + 1)
                    act.activation(H[:, m, 0, :], o_t[:, m % 2, :], ACT.Copy).then_inc(S["o_hi"], 1)
            stage("att_out", squares_post)
            layer_norm()
            feed_forward(1)
            feed_forward(2)
            stage("pool_in", nothing)
            for g in range(2):
                b = slice(BANKS * g, BANKS * g + BANKS)
                act.wait_ge(S["pool_f"], g + 1)
                act.activation(PG[:, b, 0, :], pooled[:, b, :], ACT.Copy).then_inc(S["pool_hi"], 1)
            stage("pool_group", round_into(H))
            stage("pool_out", squares_post)
            layer_norm()
            feed_forward(3, last=True)

        @block.vector
        def _(vec):
            steps = [0]

            def step(ins):
                steps[0] += 1
                ins.then_inc(vec_step, 1)
                vec.wait_ge(vec_step, steps[0])

            def mark(ins):
                steps[0] += 1
                ins.then_inc(vec_step, 1)

            def split(q, r, sl, turn):
                for half in range(2):
                    w = slice(half * PANEL // 2, (half + 1) * PANEL // 2)
                    vec.wait_ge(panel_hi, 2 * q + half + 1)
                    vec.tensor_tensor(w_lo[:, sl, w], raw[:, r, w], w_hi[:, sl, w], ALU.subtract).then_inc(panel_lo, 1)

            def take_sum(s, g, G, dest=None):
                vec.wait_ge(corrected, before("corrected", s) + g + 1)
                to = ev[:, G, :, :] if dest is None else dest
                vec.tensor_tensor(to, banks[:, BANKS * G:BANKS * G + BANKS, 0:T], ev[:, G, :, :], ALU.add)\
                    .then_inc(summed, 1)

            def own_sum(s, g):
                vec.wait_ge(summed, FIRST_GROUP[s] + g + 1)

            def bank_post(s, g, G, b, new_x):
                last = b == BANKS - 1
                e = ev[:, G, b, :]
                if last:
                    vec.wait_ge(corrected, before("corrected", s) + g + 1)
                else:
                    vec.wait_ge(bank_corr, bank_count(s, b))
                vec.tensor_tensor(e, banks[:, BANKS * G + b, 0:T], e, ALU.add).then_inc(summed if last else bank_sum, 1)
                if last:
                    own_sum(s, g)
                else:
                    vec.wait_ge(bank_sum, bank_count(s, b))
                new_x(BANKS * g + b, e).then_inc(posted if last else bank_x, 1)

            def stage(name, post, dest=None):
                def take_up(s, g, G):
                    if STAGES[s][3] == "mod":
                        vec.wait_ge(panel_used, through(s, g))
                        vec.tensor_copy(dest[0:2, g, :], banks[0:2, BANKS * G, :]).then_inc(summed, 1)
                        return
                    take_sum(s, g, G, None if dest is None else by_group(dest[:, :, :])[:, g, :, :])
                    post(s, g, G)
                run(vec, INDEX[name], split, take_up)

            def nothing(s, g, G):
                pass

            def lo_into(dest, blocks=BANKS):
                view = dest.rearrange("p (g b) a t -> p g b a t", b=blocks)

                def post(s, g, G):
                    vec.wait_ge(operand_hi, before("operand", s) + g + 1)
                    vec.tensor_tensor(view[:, g, :, 1, :], ev[:, G, 0:blocks, :], view[:, g, :, 0, :], ALU.subtract)\
                        .then_inc(operand_lo, 1)
                return post

            def glu_post(s, g, G):
                vec.wait_ge(activated, before("activated", s) + g + 1)
                vec.scalar_tensor_tensor(ev[:, G, 0:2, :], ev[:, G, 0:2, :], 0.5, ev[:, G, 2:4, :], ALU.mult, ALU.mult)\
                    .then_inc(posted, 1)
                lo_into(HH[:, 0:22, :, :], 2)(s, g, G)

            def relu2_post(s, g, G):
                own_sum(s, g)
                vec.scalar_tensor_tensor(ev[:, G, :, :], ev[:, G, :, :], 0.0, ev[:, G, :, :], ALU.max, ALU.mult)\
                    .then_inc(posted, 1)
                lo_into(HH[:, :, :, :])(s, g, G)

            def deep_x(m, e):
                return vec.scalar_tensor_tensor(xb[:, m, :], xb[:, m, :], ALPHA, e, ALU.mult, ALU.add)

            def gated_x(col):
                def new_x(m, e):
                    return vec.scalar_tensor_tensor(xb[:, m, :], e, mod[:, col + m:col + m + 1], xb[:, m, :],
                                                    ALU.mult, ALU.add)
                return new_x

            def stage_x(name, new_x, biased=0):
                def take_up(s, g, G):
                    if biased:
                        vec.wait_ge(S["norm_x"], KD * biased)
                    if by_bank(s, g):
                        for b in range(BANKS):
                            bank_post(s, g, G, b, new_x)
                        return
                    take_sum(s, g, G)
                    own_sum(s, g)
                    for b in range(BANKS):
                        last = new_x(BANKS * g + b, ev[:, G, b, :])
                    last.then_inc(posted, 1)
                run(vec, INDEX[name], split, take_up)

            def gate_post(s, g, G):
                own_sum(s, g)
                a = by_group(gate_a[:, :, :])[:, g, :, :]
                vec.tensor_tensor(a, a, ev[:, G, :, :], ALU.mult).then_inc(posted, 1)

            def mix_post(s, g, G):
                own_sum(s, g)
                e = ev[:, G, :, :]
                step(vec.tensor_tensor(e, e, by_group(gate_b[:, :, :])[:, g, :, :], ALU.mult))
                vec.tensor_tensor(e, e, by_group(gate_a[:, :, :])[:, g, :, :], ALU.add).then_inc(posted, 1)
                lo_into(MX[:, :, :, :])(s, g, G)

            def scale_post(s, g, G):
                own_sum(s, g)
                for b in range(BANKS):
                    at = COLS["pool_scale"] + BANKS * g + b
                    last = vec.tensor_scalar(ev[:, G, b, :], ev[:, G, b, :], cols[:, at:at + 1], None, ALU.mult)
                last.then_inc(posted, 1)
                lo_into(H[:, :, :, :])(s, g, G)

            def variance(n, mean, eps, stage=None):
                vec.wait_ge(S["stat_sums"], n + 1)
                b = stat_bank(stage)
                if mean:
                    step(vec.tensor_copy(st[:, 0, :], banks[:, b, 0:T]))
                    step(vec.tensor_tensor(st[:, 3, :], st[:, 0, :], st[:, 0, :], ALU.mult))
                    step(vec.tensor_tensor(st[:, 1, :], banks[:, b, T:2 * T], st[:, 3, :], ALU.subtract))
                    vec.tensor_scalar(st[:, 1, :], st[:, 1, :], 0.0, eps, ALU.max, ALU.add).then_inc(S["stat_var"], 1)
                else:
                    vec.tensor_scalar(st[:, 1, :], banks[:, b, T:2 * T], eps, None, ALU.add).then_inc(S["stat_var"], 1)

            def inverse_root(n, mean=False):
                vec.wait_ge(S["stat_root"], n + 1)
                step(vec.reciprocal(st[:, 2, :], st[:, 1, :]))
                if mean:
                    step(vec.scalar_tensor_tensor(st[:, 3, :], st[:, 0, :], -1.0, st[:, 2, :], ALU.mult, ALU.mult))

            def over_blocks(row):
                return row.unsqueeze(1).to_broadcast([P, BANKS, T])

            def apply_norm(k, dest, scale, bias, mean, operand=True):
                def scaled(m):
                    vec.scalar_tensor_tensor(dest[:, m, :], xb[:, m, :], scale[:, m:m + 1], st[:, 2, :], ALU.mult,
                                             ALU.mult).then_inc(S["norm_scaled" if mean else "norm_y"], 1)

                def centred(m):
                    vec.wait_ge(S["norm_scaled"], KD * (k - 3) + m + 1)
                    vec.scalar_tensor_tensor(dest[:, m, :], st[:, 3, :], scale[:, m:m + 1], dest[:, m, :], ALU.mult,
                                             ALU.add).then_inc(S["norm_y"], 1)

                def lo(m):
                    vec.wait_ge(S["norm_hi"], KD * k + m + 1)
                    if bias is None:
                        ins = vec.tensor_tensor(H[:, m, 1, :], dest[:, m, :], H[:, m, 0, :], ALU.subtract)
                    else:
                        ins = vec.scalar_tensor_tensor(H[:, m, 1, :], dest[:, m, :], bias[:, m:m + 1], H[:, m, 0, :],
                                                       ALU.add, ALU.subtract)
                    ins.then_inc(S["norm_lo"], 1)

                def biased(m):
                    vec.wait_ge(S["norm_y"], KD * k + m + 1)
                    vec.tensor_scalar(dest[:, m, :], dest[:, m, :], bias[:, m:m + 1], None, ALU.add)\
                        .then_inc(S["norm_x"], 1)

                for m in range(KD + 2):
                    if m < KD:
                        scaled(m)
                    if mean and 1 <= m <= KD:
                        centred(m - 1)
                    if m >= 2:
                        (lo if operand else biased)(m - 2)

            def mod_taken(n, taken, first, count, scales):
                vec.wait_ge(S["mod_cols"], 1 if n == 1 else 1 + SSM_GROUPS)
                step(vec.tensor_tensor(mod[:, first:first + count], taken,
                                       cols[:, COLS["b_mod"] + first:COLS["b_mod"] + first + count], ALU.add))
                vec.tensor_scalar(mod[:, scales:scales + 8], mod[:, scales:scales + 8], 1.0, None, ALU.add)\
                    .then_inc(S["mod_ready"], 1)
                vec.wait_ge(S["mod_ready"], n)

            vec.memset(tiny[:, :], 1.0).then_inc(S["tiny_set"], 1)
            vec.wait_ge(S["c_hi"], 1)
            vec.tensor_tensor(c_r[:, :, 1], c_s[:, :], c_r[:, :, 0], ALU.subtract).then_inc(S["c_lo"], 1)
            vec.wait_ge(S["params_loaded"], 16)
            split(0, 0, 0, 0)
            split(1, 1, 1, 0)
            variance(0, False, EPS)
            stage("mod_norm", None, mod_row[:, :].rearrange("p (g n) -> p g n", n=CHUNK))
            inverse_root(0)
            mod_taken(1, banks[:, 7, 0:16], 0, 16, 8)
            apply_norm(0, ev8, mod[:, 8:16], mod[:, 0:8], False)

            stage("u", nothing)
            stage("v", nothing)
            stage("gate_a", nothing)
            stage("gate_b", nothing)

            variance(1, False, EPS)
            inverse_root(1)
            for g in range(2):
                v4 = by_group(v_t[:, :, :])[:, g, :, :]
                step(vec.tensor_tensor(v4, v4, over_blocks(st[:, 2, :]), ALU.mult))
                for b in range(BANKS):
                    m = BANKS * g + b
                    at = COLS["gm_norm"] + m
                    last = vec.tensor_scalar(v_t[:, m, :], v_t[:, m, :], cols[:, at:at + 1], None, ALU.mult)
                last.then_inc(S["sgu_vn"], 1)
            for j in range(5):
                if j < 4:
                    two = slice(2 * j, 2 * j + 2)
                    vec.wait_ge(S["sgu_mix"], j + 1)
                    mixed = banks[:, (5, 6, 7, 0)[j], :].rearrange("p (m t) -> p m t", m=2)
                    vec.tensor_tensor(ev8[:, two, :], mixed, u_t[:, two, :], ALU.mult).then_inc(S["sgu_y"], 1)
                if j:
                    two = slice(2 * j - 2, 2 * j)
                    vec.wait_ge(S["sgu_hi"], j)
                    vec.tensor_tensor(YA[:, two, 1, :], ev8[:, two, :], YA[:, two, 0, :], ALU.subtract)\
                        .then_inc(S["sgu_lo"], 1)
            stage("branch_gm", gate_post)

            step(vec.memset(pad[:, :, 0:CONV - 1], 0.0))

            def conv_post(s, g, G):
                own_sum(s, g)
                vec.wait_ge(S["conv_first"], g + 1)
                for tap in range(1, CONV):
                    if tap > 1:
                        vec.wait_ge(S["conv_tap"], (CONV - 2) * g + tap - 1)
                    for b in range(BANKS):
                        w = conv_w[:, g, CONV * b + tap:CONV * b + tap + 1]
                        last = vec.scalar_tensor_tensor(ev[:, G, b, :], pad[:, b, tap:tap + T], w, ev[:, G, b, :],
                                                        ALU.mult, ALU.add)
                    last.then_inc(S["conv_tap"] if tap < CONV - 1 else posted, 1)

            def conv_take_up(s, g, G):
                vec.wait_ge(posted, before("posted", s) + g)
                take_sum(s, g, G, pad[:, :, CONV - 1:CONV - 1 + T])
                conv_post(s, g, G)

            run(vec, INDEX["xbc"], split, conv_take_up)
            stage("z", nothing)

            vec.wait_ge(S["wdt_hi"], 1)
            vec.tensor_tensor(wdt_r[:, :, 1, :], wdt[:, :, :], wdt_r[:, :, 0, :], ALU.subtract).then_inc(S["wdt_lo"], 1)
            scratch, y_v, dt_v, a_v, ncum = (dtv[:, n, :, :] for n in range(5))
            vec.wait_ge(S["dt_corr"], 1)
            step(vec.tensor_tensor(y_v, banks[:, 4, 0:P].rearrange("p (t a h) -> p t a h", t=TT, a=2)[:, :, 0, :],
                                   scratch, ALU.add))
            step(vec.tensor_tensor(y_v, y_v, heads[:, 0, :].unsqueeze(1).to_broadcast([P, TT, 32]), ALU.add))
            vec.scalar_tensor_tensor(scratch, y_v, -1.0, y_v, ALU.mult, ALU.min).then_inc(S["dt_y"], 1)
            vec.wait_ge(S["dt_exp"], 1)
            vec.tensor_scalar(scratch, scratch, 1.0, None, ALU.add).then_inc(S["dt_one"], 1)
            vec.wait_ge(S["dt_ln"], 1)
            step(vec.scalar_tensor_tensor(dt_v, y_v, 0.0, scratch, ALU.max, ALU.add))
            vec.wait_ge(S["dt_ea"], 1)
            vec.scalar_tensor_tensor(a_v, dt_v, -1.0, ea[:, :].unsqueeze(1).to_broadcast([P, TT, 32]),
                                     ALU.mult, ALU.mult).then_inc(S["dt_a"], 1)
            vec.wait_ge(S["cum_done"], 1)
            vec.tensor_scalar(ncum, banks[:, 5, 0:64].rearrange("p (t h) -> p t h", t=TT), -1.0, None, ALU.mult)\
                .then_inc(S["cum_got"], 1)
            vec.wait_ge(S["cum_hi"], 1)
            vec.tensor_tensor(cum_r[:, 1, :], banks[0:32, 6, 0:T], cum_r[:, 0, :], ALU.subtract)\
                .then_inc(S["cum_lo"], 1)
            vec.wait_ge(S["cum_got"], 1)

            pairs = 2 * SSM_GROUPS
            rest = INDEX["mod_rest"]
            for n in range(pairs + 5):
                if n < pairs and n % 2 == 0:
                    g = n // 2
                    vec.wait_ge(S["xt_done"], g + 1)
                    if g >= 2:
                        vec.wait_ge(S["y_done"], 2 * (g - 1))
                    for t in range(TT):
                        vec.tensor_tensor(xdt(g, t).rearrange("p (h d) -> p h d", h=4),
                                          banks[:, 2, t * T:t * T + T].rearrange("p (h d) -> p h d", h=4),
                                          dtv[:, 2, t, 4 * g:4 * g + 4].unsqueeze(2).to_broadcast([P, 4, HP]),
                                          ALU.mult).then_inc(S["xdt_done"], 1)
                if n < pairs:
                    vec.wait_ge(S["row_done"], n + 1)
                    if n >= 2:
                        vec.wait_ge(S["y_done"], n - 1)
                    for r in range(2):
                        h = 2 * n + r
                        for t, (at, size) in enumerate(((0, T), (T, P))):
                            vec.tensor_scalar(decay(n)[:, 3 * P * r + at:3 * P * r + at + size],
                                              banks[:, 3 + n % 2, r * T + t * P:r * T + T],
                                              ncum[:, t, h:h + 1], 0.0, ALU.add, ALU.min).then_inc(S["seg_done"], 1)
                if 2 <= n <= pairs + 1:
                    m = n - 2
                    at = COLS["d_skip"] + m
                    vec.wait_ge(S["y_done"], m + 1)
                    vec.scalar_tensor_tensor(xbc[:, m, :], xbc[:, m, :], cols[:, at:at + 1],
                                             banks[:, 5 + m % 2, 0:T], ALU.mult, ALU.add).then_inc(S["y_skip"], 1)
                if n >= 4 and n % 2 == 0 and n < pairs + 4:
                    g = (n - 4) // 2
                    vec.wait_ge(S["y_sums"], g + 1)
                    vec.tensor_scalar(st[:, g % 2, :], banks[:, 7, 0:T], EPS, None, ALU.add).then_inc(S["y_var"], 1)
                if 5 <= n < pairs + 5 and n % 2 == 1:
                    g = (n - 5) // 2
                    vec.wait_ge(S["y_root"], g + 1)
                    step(vec.reciprocal(st[:, 2 + g % 2, :], st[:, g % 2, :]))
                    for m in (2 * g, 2 * g + 1):
                        at = COLS["ssm_norm"] + m
                        vec.scalar_tensor_tensor(xbc[:, m, :], xbc[:, m, :], cols[:, at:at + 1], st[:, 2 + g % 2, :],
                                                 ALU.mult, ALU.mult).then_inc(S["y_f"], 1)
                if n < pairs and n % 2:
                    g = n // 2
                    vec.wait_ge(panel_used, FIRST_PANEL[rest] + n + 1)
                    if g:
                        vec.wait_ge(S["mod_cols"], 1 + g)
                    vec.tensor_copy(mod_tail, banks[0:2, 0, :]).then_inc(summed, 1)
                if n < pairs:
                    q = FIRST_PANEL[rest] + n + SPLIT
                    split(q, q % RAW, q % SPLIT, q // RAW)
            mod_taken(2, banks[:, 1, 3 * P:3 * P + 32], 16, 32, 32)
            stage("branch_ssm", mix_post)
            stage_x("out", gated_x(16))
            variance(2, False, EPS, "out")
            inverse_root(2)
            apply_norm(1, ev8, mod[:, 32:40], mod[:, 24:32], False)
            stage("ff1", relu2_post)
            stage_x("ff2", gated_x(40))
            variance(3, False, EPS, "ff2")
            inverse_root(3)
            apply_norm(2, xb, cols[:, COLS["final"]:COLS["final"] + KD], None, False)

            norms = [3]

            def layer_norm(stage_name, i, last=False):
                k = norms[0]
                at = KD * i
                variance(k + 1, True, LN_EPS, stage_name)
                inverse_root(k + 1, True)
                apply_norm(k, xb, cols[:, COLS["ln_g"] + at:COLS["ln_g"] + at + KD],
                           cols[:, COLS["ln_b"] + at:COLS["ln_b"] + at + KD], True, not last)
                norms[0] += 1

            def feed_forward(i, ln, last=False):
                stage(f"gu{i}", glu_post)
                stage_x(f"down{i}", deep_x, norms[0] - 3)
                layer_norm(f"down{i}", ln, last)

            feed_forward(0, 0)
            stage("qkv", nothing, qkv)
            vec.wait_ge(S["near_loaded"], 16 * HEADS)
            for h in range(HEADS + 4):
                if h < HEADS:
                    vec.wait_ge(S["s_done"], h + 1)
                    if h >= 2:
                        vec.wait_ge(S["pt_done"], h - 1)
                    b = banks[:, 4 + h % 2, :]
                    pr = probs[:, h % 2, :]
                    vec.scalar_tensor_tensor(pr[:, 0:P], b[:, 0:P], SCALE, near[:, h, P:T], ALU.mult, ALU.add)\
                        .then_inc(S["s_biased"], 1)
                    vec.scalar_tensor_tensor(pr[:, P:3 * P], b[:, P:3 * P], SCALE, near[:, h, :], ALU.mult, ALU.add)\
                        .then_inc(S["s_biased"], 1)
                    vec.wait_ge(S["s_biased"], 2 * h + 1)
                    step(vec.reduce_max(sm[:, h, 0:1], pr[:, 0:P], AX.X))
                    vec.wait_ge(S["s_biased"], 2 * h + 2)
                    step(vec.reduce_max(sm[:, h, 1:2], pr[:, P:3 * P], AX.X))
                    vec.tensor_scalar(sm[:, h, 2:4], sm[:, h, 0:2], -1.0, None, ALU.mult).then_inc(S["s_max"], 1)
                if 1 <= h <= HEADS:
                    m = h - 1
                    vec.wait_ge(S["p_exp"], 2 * (m + 1))
                    step(vec.reciprocal(sm[:, m, 6:8], sm[:, m, 4:6]))
                    pr = probs[:, m % 2, :]
                    vec.tensor_scalar(pr[:, 0:P], pr[:, 0:P], sm[:, m, 6:7], None, ALU.mult)
                    vec.tensor_scalar(pr[:, P:3 * P], pr[:, P:3 * P], sm[:, m, 7:8], None, ALU.mult)\
                        .then_inc(S["p_norm"], 1)
                if 3 <= h <= HEADS + 2:
                    m = h - 3
                    vec.wait_ge(S["o_done"], m + 1)
                    if m >= 2:
                        vec.wait_ge(S["o_lo"], m - 1)
                    vec.tensor_copy(o_t[:, m % 2, :], banks[:, 7, 0:T]).then_inc(S["o_copied"], 1)
                if h >= 4:
                    m = h - 4
                    vec.wait_ge(S["o_hi"], m + 1)
                    vec.tensor_tensor(H[:, m, 1, :], o_t[:, m % 2, :], H[:, m, 0, :], ALU.subtract)\
                        .then_inc(S["o_lo"], 1)
            stage_x("att_out", deep_x, norms[0] - 3)
            layer_norm("att_out", 1)
            feed_forward(1, 2)
            feed_forward(2, 3)

            def pool_post(s, g, G):
                own_sum(s, g)
                src, reach = pu, 1
                for w in range(2 * g + 2):
                    b = slice(max(2 * w, BANKS * g), BANKS * g + BANKS)
                    mark(vec.tensor_copy(pw[:, w, b, 0:reach], src[:, b, 0:reach]))
                    step(vec.tensor_tensor(pw[:, w, b, reach:T], src[:, b, reach:T], src[:, b, 0:T - reach], ALU.add))
                    src, reach = pw[:, w, :, :], 2 * reach
                vec.wait_ge(S["inv_loaded"], 16)
                edge = max(WINDOWS)
                both = (2 * g, 2 * g + 1)
                for w in both:
                    b = slice(2 * w, 2 * w + 2)
                    mark(vec.tensor_tensor(pooled[:, b, 0:edge], pw[:, w, b, 0:edge],
                                           inv[:, w, :].unsqueeze(1).to_broadcast([P, 2, edge]), ALU.mult))
                    step(vec.scalar_tensor_tensor(pooled[:, b, edge:T], pw[:, w, b, edge:T], 1.0 / WINDOWS[w],
                                                  pu[:, b, edge:T], ALU.mult, ALU.subtract))
                b = slice(BANKS * g, BANKS * g + BANKS)
                vec.tensor_tensor(pooled[:, b, 0:edge], pooled[:, b, 0:edge], pu[:, b, 0:edge], ALU.subtract)\
                    .then_inc(S["pool_f"], 1)

            stage("pool_in", pool_post, pu)
            for g in range(2):
                b = slice(BANKS * g, BANKS * g + BANKS)
                vec.wait_ge(S["pool_hi"], g + 1)
                vec.tensor_tensor(PG[:, b, 1, :], pooled[:, b, :], PG[:, b, 0, :], ALU.subtract)\
                    .then_inc(S["pool_lo"], 1)
            stage("pool_group", scale_post)
            stage_x("pool_out", deep_x, norms[0] - 3)
            layer_norm("pool_out", 4)
            feed_forward(3, 5, last=True)


def kernel(**inputs):
    import numpy as np
    import concourse.bacc as bacc
    from concourse.bass_utils import run_bass_kernel_spmd as launch

    f = {n: np.asarray(a) for n, a in inputs.items()}

    def chunks(w):
        k, n = w.shape
        return w.reshape(k // P, P, n // CHUNK, CHUNK).transpose(2, 0, 1, 3).reshape(-1, P, CHUNK)

    def glu_chunks(w):
        k, n = w.shape
        return chunks(w.reshape(k, 2, n // 2 // T, T).transpose(0, 2, 1, 3).reshape(k, n))

    w_in, w_mod = f["w_in"][0], f["w_mod"][0]
    u, v, z, xbc, dt, ga, gb = np.split(w_in, np.cumsum([D, D, 2 * D, 4 * D, SSM_HEADS, D])[:], axis=1)
    gu, down = f["ffn_w_gu_2"], f["ffn_w_down_2"]
    a_in, b_in = f["a_w_in_2"][0], f["b_w_in_2"][0]
    grouped = f["b_w_group_2"][0].reshape(4, 2, P, T).transpose(0, 2, 1, 3).reshape(4, P, CHUNK)
    stream = np.concatenate([
        chunks(w_mod[:, :2 * D]), chunks(u), chunks(v), chunks(ga), chunks(gb), chunks(f["w_branch_gm"][0]),
        chunks(xbc), chunks(z), chunks(w_mod[:, 2 * D:]), chunks(f["w_branch_ssm"][0]), chunks(f["w_out"][0]),
        chunks(f["w_ff1"][0]), chunks(f["w_ff2"][0]),
        glu_chunks(gu[0, 0]), chunks(down[0, 0]), chunks(a_in), chunks(f["a_w_out_2"][0]),
        glu_chunks(gu[0, 1]), chunks(down[0, 1]), glu_chunks(gu[1, 0]), chunks(down[1, 0]),
        chunks(b_in), grouped, chunks(f["b_w_out_2"][0]), glu_chunks(gu[1, 1]), chunks(down[1, 1])])
    panels = stream.reshape(PANELS, 4, P, CHUNK).transpose(0, 2, 1, 3).reshape(PANELS, P, PANEL)

    def columns(a):
        return a.reshape(-1, P).T

    conv_w = f["conv_w"][0].reshape(CONV, 32, P).transpose(2, 1, 0).reshape(P, 32 * CONV)
    cols = np.concatenate([
        columns(f["b_mod"][0]), columns(f["gm_norm_w"][0]), columns(f["conv_b"][0]), conv_w,
        columns(f["ssm_norm_w"][0]), columns(f["final_norm_w"]), columns(f["ln_g_2"].reshape(-1)),
        columns(f["ln_b_2"].reshape(-1)), columns(f["b_scale_2"][0]),
        columns(np.repeat(f["d_skip"][0], HP))], axis=1)
    heads = np.broadcast_to(np.stack([f["dt_bias"][0], f["a_log"][0]]), (P, 2, SSM_HEADS))
    dist = T - 1 - np.arange(BIAS_COLS)
    near = np.maximum(dist, 1).astype(np.float32)
    large = 16 + (np.log(near / np.float32(16)) / np.float32(np.log(8.0)) * np.float32(16)).astype(np.int32)
    bucket = np.where(dist < 0, 32, np.where(dist < 16, dist, np.minimum(large, 31)))
    onehot = (np.arange(33)[:, None] == bucket[None, :]).astype(np.float32)
    tokens = np.arange(1, 17, dtype=np.float32)
    inv = np.broadcast_to(np.stack([1 / np.minimum(tokens, np.float32(w)) for w in WINDOWS]), (P, 4, 16))
    arrays = {
        "panels": panels,
        "x_t": f["x"][0].T.reshape(KD, P, T).transpose(1, 0, 2),
        "c_t": columns(f["c"][0]),
        "cols": cols,
        "heads": heads,
        "ws_t": f["gm_ws"][0].transpose(2, 0, 1),
        "bs": f["gm_bs"][0].reshape(1, -1),
        "wdt": dt.reshape(KD, P, SSM_HEADS).transpose(1, 0, 2),
        "rel": f["rel_bias_2"],
        "onehot": onehot,
        "inv": inv,
    }
    arrays = {f"in_{n}": np.ascontiguousarray(a, dtype=np.float32) for n, a in arrays.items()}
    nc = bacc.Bacc("TRN2", target_bir_lowering=False, num_devices=1)
    args = [nc.dram_tensor(n, a.shape, F32, kind="ExternalInput").ap() for n, a in arrays.items()]
    args.append(nc.dram_tensor("bias_rows", (P, HEADS * BIAS_COLS), F32).ap())
    args.append(nc.dram_tensor("out_t", (P, KD, T), F32, kind="ExternalOutput").ap())
    two_blocks(nc, *args)
    result = launch(nc, [arrays], core_ids=[0]).results[0]["out_t"]
    return result.transpose(1, 0, 2).reshape(D, T).T[None]
```

```python
import concourse.bass as bass
from concourse import mybir
from contextlib import ExitStack

F32 = mybir.dt.float32
F32R = mybir.dt.float32r
ACT = mybir.ActivationFunctionType
ALU = mybir.AluOpType
AX = mybir.AxisListType

P = 128
T = 256
TT = T // P
D = 1024
KD = D // P
CHUNK = 512
PANEL = 4 * CHUNK
BANKS = 4
RAW = 4
SPLIT = 2
EPS = 1e-6
LN_EPS = 1e-5
ALPHA = (2 * 2) ** 0.25
HEADS = 8
HEAD_DIM = 128
SCALE = HEAD_DIM ** -0.5
SSM_HEADS = 32
HP = 64
SSM_GROUPS = 8
CONV = 4
WINDOWS = (2, 4, 8, 16)
MASKED = -1e30
BIAS_COLS = 2 * T

STAGES = (
    ("mod_norm", 8, 4, "mod"), ("u", 8, 2, "act"), ("v", 8, 2, "act"), ("gate_a", 8, 2, "act"),
    ("gate_b", 8, 2, "act"), ("branch_gm", 8, 2, "gate"), ("xbc", 8, 8, "conv"), ("z", 8, 4, "act"),
    ("mod_rest", 8, 8, "mod"), ("branch_ssm", 16, 2, "mix"), ("out", 8, 2, "add1"),
    ("ff1", 8, 8, "relu2"), ("ff2", 32, 2, "add1"),
    ("gu0", 8, 11, "glu"), ("down0", 22, 2, "deep"), ("qkv", 8, 6, "keep"), ("att_out", 8, 2, "deep"),
    ("gu1", 8, 11, "glu"), ("down1", 22, 2, "deep"), ("gu2", 8, 11, "glu"), ("down2", 22, 2, "deep"),
    ("pool_in", 8, 2, "keep"), ("pool_group", 2, 2, "scale"), ("pool_out", 8, 2, "deep"),
    ("gu3", 8, 11, "glu"), ("down3", 22, 2, "deep"),
)
INDEX = {s[0]: n for n, s in enumerate(STAGES)}
NORMED = ("out", "ff2", "down0", "att_out", "down1", "down2", "pool_out", "down3")
_ALL = ("mod", "act", "gate", "conv", "mix", "add1", "relu2", "glu", "deep", "keep", "scale")
COUNTED = {
    "corrected": _ALL[1:],
    "summed": _ALL,
    "activated": ("act", "conv", "glu"),
    "posted": ("gate", "conv", "mix", "add1", "relu2", "glu", "deep", "scale"),
    "operand": ("mix", "relu2", "glu", "scale"),
}


URGENT = ("mix", "add1", "deep", "keep", "scale")


def panels_of(stage):
    name, kb, groups, kind = stage
    return kb * groups // 4


def before(sem, stage):
    return sum(s[2] for s in STAGES[:stage] if s[3] in COUNTED[sem])


FIRST_PANEL = [sum(map(panels_of, STAGES[:n])) for n in range(len(STAGES) + 1)]
FIRST_GROUP = [sum(s[2] for s in STAGES[:n]) for n in range(len(STAGES) + 1)]
PANELS = FIRST_PANEL[-1]

COLS, _at = {}, 0
for _name, _n in (("b_mod", 48), ("gm_norm", 8), ("conv_b", 32), ("conv_w", 32 * CONV), ("ssm_norm", 16),
                  ("final", 8), ("ln_g", 48), ("ln_b", 48), ("pool_scale", 8), ("d_skip", 16)):
    COLS[_name] = _at
    _at += _n
NCOLS = _at


def two_blocks(nc, panels, x_in, c_in, cols_in, heads_in, ws_in, bs_in, wdt_in, rel_in, onehot_in, inv_in,
               skew, out):
    ctx = ExitStack()
    with ctx:
        def sb(name, shape, dt=F32, stack=ctx):
            return stack.enter_context(nc.sbuf_tensor(name, shape, dt))

        raw = sb("raw", [P, RAW, PANEL])
        w_hi = sb("w_hi", [P, SPLIT, PANEL], F32R)
        w_lo = sb("w_lo", [P, SPLIT, PANEL], F32R)
        ev = sb("ev", [P, 2, BANKS, T])
        XS = sb("XS", [P, KD, 2, T])
        st = sb("st", [P, 4, T])
        part = sb("part", [P, 2, T])
        ident = sb("ident", [P, P])
        ident_r = sb("ident_r", [P, P], F32R)
        never = sb("never", [P, P], F32R)
        ones = sb("ones", [P, P])
        mean_w = sb("mean_w", [P, P])
        gmean_w = sb("gmean_w", [P, P])
        cols = sb("cols", [P, NCOLS])
        tiny = sb("tiny", [P, 2])
        mod = sb("mod", [P, 48])
        phase = ExitStack()
        H = sb("H", [P, KD, 2, T], F32R, phase)
        u_t = sb("u_t", [P, KD, T], F32, phase)
        v_t = sb("v_t", [P, KD, T], F32, phase)
        gate_a = sb("gate_a", [P, KD, T], F32, phase)
        gate_b = sb("gate_b", [P, KD, T], F32, phase)
        early = ExitStack()
        ws = sb("ws", [P, KD, P], F32, early)
        bs = sb("bs", [1, KD * P], F32, early)
        v_nat = sb("v_nat", [P, KD, TT, P], F32, early)
        YA = sb("YA", [P, KD, 2, T], F32R, early)
        mod_row = sb("mod_row", [2, 4 * CHUNK], F32, early)
        c_f = sb("c_f", [P, KD], F32, early)
        c_s = sb("c_s", [P, KD], F32, early)
        rel = sb("rel", [33, HEADS], F32, early)
        onehot = sb("onehot", [33, BIAS_COLS], F32, early)
        early.close()
        after_ssd = ExitStack()
        MX = sb("MX", [P, KD, 2, T], F32R, after_ssd)
        after_ssd.close()
        xbc = sb("xbc", [P, 32, T], F32, phase)
        conv_stack = ExitStack()
        pad = sb("pad", [P, BANKS, T + 4], F32, conv_stack)
        conv_stack.close()
        z_t = sb("z_t", [P, 16, T], F32, phase)
        tri = sb("tri", [P, P], F32, phase)
        heads = sb("heads", [P, 2, 32], F32, phase)
        c_r = sb("c_r", [P, KD, P], F32R, phase)
        dt_stack = ExitStack()
        wdt = sb("wdt", [P, KD, 32], F32, dt_stack)
        wdt_r = sb("wdt_r", [P, KD, 2, 32], F32R, dt_stack)
        dt_stack.close()
        cb = sb("cb", [P, 2, 3 * P], F32, phase)
        dtv = sb("dtv", [P, 5, TT, 32], F32, phase)
        ea = sb("ea", [P, 32], F32, phase)
        cum_r = sb("cum_r", [32, 2, T], F32R, phase)
        phase.close()
        rev_stack = ExitStack()
        for k in range(2):
            sb(f"rev_skip{k}", [P, 2 * KD, T], F32, rev_stack)
        rev = sb("rev", [P, HEADS, BIAS_COLS], F32, rev_stack)
        rev_stack.close()
        yb_stack = ExitStack()
        YB = sb("YB", [P, 16, 2, T], F32R, yb_stack)
        yb_stack.close()
        second = ExitStack()
        sb("H_again", [P, KD, 2, T], F32, second)
        near = sb("near", [P, HEADS, T], F32, second)
        mlp = ExitStack()
        HH = sb("HH", [P, 32, 2, T], F32R, mlp)
        mlp.close()
        attn = ExitStack()
        qkv = sb("qkv", [P, 24, T], F32, attn)
        v_tok = sb("v_tok", [P, TT, D], F32, attn)
        probs = sb("probs", [P, 3, 3 * P], F32, attn)
        probs_t = sb("probs_t", [P, 2, 3 * P], F32, attn)
        sm = sb("sm", [P, HEADS, 8], F32, attn)
        o_t = sb("o_t", [P, 2, T], F32, attn)
        attn.close()
        pooling = ExitStack()
        PG = sb("PG", [P, KD, 2, T], F32R, pooling)
        pu = sb("pu", [P, KD, T], F32, pooling)
        pw = sb("pw", [P, 4, KD, T], F32, pooling)
        pooled = sb("pooled", [P, KD, T], F32, pooling)
        pooling.close()
        inv_stack = ExitStack()
        sb("inv_skip", [P, 32, 2, T], F32, inv_stack)
        inv = sb("inv", [P, 4, 16], F32, inv_stack)
        inv_stack.close()
        second.close()

        banks = ctx.enter_context(nc.psum_tensor("banks", [P, 2 * BANKS, CHUNK], F32))

        def sem(name):
            return ctx.enter_context(nc.semaphore(name))

        loaded = [sem(f"panel_loaded_{r}") for r in range(RAW)]
        panel_hi, panel_lo, panel_used = sem("panel_hi"), sem("panel_lo"), sem("panel_used")
        corrected, summed, activated = sem("corrected"), sem("summed"), sem("activated")
        posted, operand_hi, operand_lo = sem("posted"), sem("operand_hi"), sem("operand_lo")
        bank_done, bank_corr, bank_sum, bank_x = (sem(f"bank_{n}") for n in ("done", "corrected", "summed", "x"))
        act_step = sem("act_step")
        vec_step = sem("vec_step")
        S = {n: sem(n) for n in (
            "x_loaded params_loaded c_loaded late_loaded consts_ready c_silu c_hi c_lo c_zero mod_cols mod_ready "
            "squares stat_sums stat_var stat_root stat_mean norm_part norm_centred norm_y norm_hi norm_lo norm_x "
            "ident_r_ready "
            "sgu_vn sgu_vt sgu_vcopy sgu_mix sgu_y sgu_hi sgu_lo ws_masked "
            "wdt_hi wdt_lo dt_raw dt_y dt_exp dt_one dt_ln dt_ea dt_a cum_done cum_got cum_hi cum_lo "
            "cb_done cb_copied xt_done xdt_done row_done exp_done never_set m_done y_done y_skip "
            "y_gated y_sq y_sums y_var y_root y_f y_hi y_lo "
            "rel_loaded rel_masked rev_done rev_copied rev_stored near_loaded "
            "conv_first conv_tap tiny_set vt_done v_copied s_done s_biased s_max p_exp p_norm "
            "pt_done pt_copied o_done o_copied o_hi o_lo "
            "pool_hi pool_lo pool_lo_wide pool_f inv_loaded x_stored").split()}

        block = ctx.enter_context(nc.Block())
        xb = XS[:, :, 0, :]
        conv_w = cols[:, COLS["conv_w"]:COLS["conv_w"] + 32 * CONV].rearrange("p (g n) -> p g n", n=BANKS * CONV)
        conv_b = cols[:, COLS["conv_b"]:COLS["conv_b"] + 32].rearrange("p (g b) -> p g b", b=BANKS)
        sq = XS[:, :, 1, :]
        ev8 = ev[:, :, :, :].rearrange("p a b t -> p (a b) t")

        def decay(n):
            flat = ev[:, :, :, :].rearrange("p a b t -> p (a b t)")
            return flat[:, n % 2 * 6 * P:(n % 2 + 1) * 6 * P]

        mod_tail = ev[0:2, :, :, :].rearrange("p a b t -> p (a b t)")[:, 12 * P:16 * P]

        def xdt(g, t):
            return XS[:, 4 + 2 * (g % 2) + t, 1, :]

        def stat_bank(stage):
            if stage == "x":
                return 3
            return 0 if stage is None else BANKS * (FIRST_GROUP[INDEX[stage] + 1] % 2)

        def by_group(t):
            return t.rearrange("p (g b) t -> p g b t", b=BANKS)

        def need(eng, s, value):
            if not (isinstance(value, int) and value <= 0):
                eng.wait_ge(s, value)

        def groups(eng, s, body):
            n = STAGES[s][2]
            if n >= 4 and s:
                with eng.Fori(0, n // 2) as turn:
                    body(2 * turn, 0, turn)
                    body(2 * turn + 1, 1, turn)
                if n % 2:
                    body(n - 1, 0, None)
            else:
                for g in range(n):
                    body(g, g % 2, None)

        def by_bank(s, g):
            return STAGES[s][0] in NORMED and isinstance(g, int) and g == STAGES[s][2] - 1

        def bank_count(s, b):
            return (BANKS - 1) * NORMED.index(STAGES[s][0]) + b + 1

        def split_slot(s, u, p):
            return (FIRST_PANEL[s] + 2 * u + p) % SPLIT

        def ahead(s, g, u, turn, p):
            q = FIRST_PANEL[s] + 2 * g + p + SPLIT
            place = FIRST_PANEL[s] + 2 * u + p + SPLIT
            if turn is None:
                return q, q % RAW, q % SPLIT, q // RAW
            return q, place % RAW, place % SPLIT, turn + place // RAW

        def through(s, g):
            kb = STAGES[s][1]
            return FIRST_PANEL[s] + (2 * g + 2 if kb == 8 else -(-kb * (g + 1) // 4))

        def run(eng, s, split, take_up, last_split=True):
            kb, n, kind = STAGES[s][1:4]
            if kb == 8:
                def body(g, u, turn):
                    split(*ahead(s, g, u, turn, 0))
                    last = kind in URGENT and isinstance(g, int) and g == n - 1
                    if last:
                        take_up(s, g, (FIRST_GROUP[s] + u) % 2)
                    if not last or last_split:
                        split(*ahead(s, g, u, turn, 1))
                    if not last:
                        take_up(s, g, (FIRST_GROUP[s] + u) % 2)
                groups(eng, s, body)
                return
            for q in range(FIRST_PANEL[s], FIRST_PANEL[s + 1]):
                a = q + SPLIT
                last = q == FIRST_PANEL[s + 1] - 1
                early = STAGES[s][0] == "branch_ssm" and q == FIRST_PANEL[s]
                if a < PANELS and not last and not early:
                    split(a, a % RAW, a % SPLIT, a // RAW)
                for g in range(n):
                    if through(s, g) == q + 1:
                        take_up(s, g, (FIRST_GROUP[s] + g) % 2)
                if a < PANELS and last and last_split:
                    split(a, a % RAW, a % SPLIT, a // RAW)

        @block.sync
        def _(sp):
            sp.dma_start(cols[:, :], cols_in).then_inc(S["params_loaded"], 16)
            sp.dma_start(c_f[:, :], c_in).then_inc(S["c_loaded"], 16)
            sp.dma_start(raw[:, 0, :], panels[0]).then_inc(loaded[0], 16)
            sp.dma_start(raw[:, 1, :], panels[1]).then_inc(loaded[1], 16)
            sp.dma_start(xb, x_in).then_inc(S["x_loaded"], 16)
            for r in range(2, RAW):
                sp.dma_start(raw[:, r, :], panels[r]).then_inc(loaded[r], 16)

            def refill(n, r):
                sp.wait_ge(panel_lo, 2 * (RAW * n + r - RAW + 1))
                sp.dma_start(raw[:, r, :], panels[RAW * n + r]).then_inc(loaded[r], 16)

            with sp.Fori(1, PANELS // RAW) as n:
                for r in range(RAW):
                    refill(n, r)
            for q in range(PANELS // RAW * RAW, PANELS):
                refill(q // RAW, q % RAW)
            for g in range(2):
                sp.wait_ge(S["norm_x"], KD * 5 + BANKS * (g + 1))
                half = slice(BANKS * g, BANKS * g + BANKS)
                sp.dma_start(out[:, half, :], xb[:, half, :]).then_inc(S["x_stored"], 16)
            sp.wait_ge(S["x_stored"], 32)

        @block.gpsimd
        def _(pool):
            pool.memset(c_r[:, :, :].bitcast(F32), 0.0).then_inc(S["c_zero"], 1)
            pool.memset(ident[:, :], 0.0).then_inc(S["consts_ready"], 1)
            pool.memset(ones[:, :], 1.0).then_inc(S["consts_ready"], 1)
            pool.memset(mean_w[:, :], 1.0 / D).then_inc(S["consts_ready"], 1)
            pool.memset(gmean_w[:, :], 1.0 / T).then_inc(S["consts_ready"], 1)
            pool.memset(tri[:, :], 1.0).then_inc(S["consts_ready"], 1)
            pool.wait_ge(S["consts_ready"], 5)
            pool.affine_select(out=ident[:, :], in_=ident[:, :], compare_op=ALU.not_equal, fill=1.0,
                               base=0, pattern=[[-1, P]], channel_multiplier=1).then_inc(S["consts_ready"], 1)
            pool.affine_select(out=tri[:, :], in_=tri[:, :], compare_op=ALU.is_ge, fill=0.0,
                               base=0, pattern=[[1, P]], channel_multiplier=-1).then_inc(S["consts_ready"], 1)
            pool.dma_start(ws[:, :, :], ws_in).then_inc(S["late_loaded"], 16)
            pool.dma_start(bs[:, :], bs_in).then_inc(S["late_loaded"], 16)
            pool.dma_start(wdt[:, :, :], wdt_in).then_inc(S["late_loaded"], 16)
            pool.dma_start(heads[:, :, :], heads_in).then_inc(S["late_loaded"], 16)
            pool.wait_ge(S["late_loaded"], 64)
            pool.affine_select(out=ws[:, :, :], in_=ws[:, :, :], compare_op=ALU.is_ge, fill=0.0, base=0,
                               pattern=[[0, KD], [1, P]], channel_multiplier=-1).then_inc(S["ws_masked"], 1)
            pool.wait_ge(S["ws_masked"], 1)
            pool.memset(rel[32:33, :], MASKED).then_inc(S["rel_masked"], 1)
            pool.dma_start(rel[0:32, :], rel_in).then_inc(S["rel_loaded"], 16)
            pool.dma_start(onehot[:, :], onehot_in).then_inc(S["rel_loaded"], 16)
            pool.wait_ge(S["rev_copied"], HEADS)
            pool.dma_start(skew.rearrange("q (h t) -> q h t", t=BIAS_COLS), rev[:, :, :]).then_inc(S["rev_stored"], 16)
            pool.wait_ge(S["rev_stored"], 16)
            pairs = 2 * SSM_GROUPS
            for n in range(pairs + 6):
                if n < pairs:
                    pool.wait_ge(S["exp_done"], 4 * (n + 1))
                    pool.wait_ge(S["cb_copied"], n // 2 + 1)
                    two = decay(n).rearrange("p (r i) -> p r i", r=2)
                    pool.tensor_tensor(two, two, cb[:, n // 2 % 2, :].unsqueeze(1).to_broadcast([P, 2, 3 * P]),
                                       ALU.mult).then_inc(S["m_done"], 1)
                if 2 <= n < pairs + 2:
                    m = n - 2
                    pool.wait_ge(S["y_skip"], m + 1)
                    pool.tensor_tensor(xbc[:, m, :], xbc[:, m, :], z_t[:, m, :], ALU.mult).then_inc(S["y_gated"], 1)
                if n >= 8 and n % 4 in (0, 1):
                    g = (n - 7) // 2
                    two = slice(2 * g, 2 * g + 2)
                    pool.wait_ge(S["y_hi"], g + 1)
                    pool.tensor_tensor(YB[:, two, 1, :], xbc[:, two, :], YB[:, two, 0, :], ALU.subtract)\
                        .then_inc(S["y_lo"], 1)
            pool.wait_ge(panel_used, FIRST_PANEL[INDEX["out"]])
            row = HEADS * BIAS_COLS - 1
            skewed = skew.rearrange("q n -> (q n)")[P - 1:P - 1 + P * row].rearrange("(q n) -> q n", n=row)
            for h in range(HEADS):
                pool.dma_start(near[:, h, :], skewed[:, h * BIAS_COLS:h * BIAS_COLS + T]).then_inc(S["near_loaded"], 16)
            def add_first_group(n):
                k = n - 2
                pool.wait_ge(posted, before("posted", INDEX[NORMED[k]]) + 1)
                pool.wait_ge(S["squares"], KD * n + BANKS)
                pool.wait_ge(S["stat_sums"], n)
                total = part[:, :, :]
                for b in range(1, BANKS):
                    if b > 1:
                        pool.wait_ge(S["norm_part"], 3 * k + b - 1)
                    pool.tensor_tensor(total, XS[:, 0, :, :] if b == 1 else total, XS[:, b, :, :], ALU.add)\
                        .then_inc(S["norm_part"], 1)

            add_first_group(2)
            pool.wait_ge(panel_used, FIRST_PANEL[INDEX["ff1"]])
            pool.dma_start(inv[:, :, :], inv_in).then_inc(S["inv_loaded"], 16)
            add_first_group(3)
            for i in range(6):
                if NORMED[i + 2] == "pool_out":
                    b = slice(BANKS, KD)
                    pool.wait_ge(S["pool_hi"], 1)
                    pool.tensor_tensor(PG[:, b, 1, :], pooled[:, b, :], PG[:, b, 0, :], ALU.subtract)\
                        .then_inc(S["pool_lo_wide"], 1)
                add_first_group(4 + i)
                pool.wait_ge(S["stat_mean"], i + 1)
                pool.wait_ge(S["stat_sums"], 5 + i)
                for m in range(KD):
                    pool.tensor_tensor(xb[:, m, :], xb[:, m, :], st[:, 0, :], ALU.subtract)\
                        .then_inc(S["norm_centred"], 1)
                for m in range(KD if i < 5 else 0):
                    pool.wait_ge(S["norm_lo"], KD * (3 + i) + m + 1)
                    at = COLS["ln_b"] + KD * i + m
                    pool.tensor_scalar(xb[:, m, :], xb[:, m, :], cols[:, at:at + 1], None, ALU.add)\
                        .then_inc(S["norm_x"], 1)

        @block.tensor
        def _(pe):
            def products(group_u, panel_slot, operand, k, starts, stops, chunks=range(4), ready=None, each=None):
                order = [(b, c) for b in range(BANKS) for c in chunks]
                if ready is not None:
                    order.sort(key=lambda bc: bc[1])
                for b, c in order:
                    acc = banks[:, BANKS * group_u + b, :]
                    at = c * CHUNK + b * P
                    kk = k + c - chunks[0]
                    if ready is not None and b == 0:
                        ready(kk + 1)
                    pair = operand[:, kk, :, :].rearrange("p a t -> p (a t)")
                    pe.matmul(acc, w_hi[:, panel_slot, at:at + P], pair,
                              start=starts and c == chunks[0], stop=False)
                    last = pe.matmul(acc[:, 0:T], w_lo[:, panel_slot, at:at + P], pair[:, 0:T],
                                     start=False, stop=stops and c == chunks[-1])
                    if each is not None and b < BANKS - 1 and c == chunks[-1]:
                        last.then_inc(each, 1)
                return last

            def psum_free(s, g):
                need(pe, summed, FIRST_GROUP[s] + g - 1)

            def stage_k8(name, operand, ready=None):
                s = INDEX[name]

                def body(g, u, turn):
                    for p in range(2):
                        pe.wait_ge(panel_lo, 2 * (FIRST_PANEL[s] + 2 * g + p + 1))
                        if p == 0:
                            psum_free(s, g)
                        first = isinstance(g, int) and g == 0
                        products((FIRST_GROUP[s] + u) % 2, split_slot(s, u, p), operand, 4 * p, p == 0, p == 1,
                                 ready=ready if first else None, each=bank_done if p and by_bank(s, g) else None)\
                            .then_inc(panel_used, 1)

                n = STAGES[s][2]
                if ready is None or n < 4:
                    groups(pe, s, body)
                    return
                body(0, 0, None)
                with pe.Fori(0, (n - 1) // 2) as turn:
                    body(2 * turn + 1, 1, turn)
                    body(2 * turn + 2, 0, turn)
                if n % 2 == 0:
                    body(n - 1, 1, None)

            def norm_block(n):
                return lambda k: pe.wait_ge(S["norm_lo"], KD * n + k)

            def operand_of(name, blocks):
                return lambda k: pe.wait_ge(operand_lo, before("operand", INDEX[name]) + -(-k // blocks))

            def stage_long(name, operand, kb, ready, part=slice(None)):
                s = INDEX[name]
                for q in range(panels_of(STAGES[s]))[part]:
                    pe.wait_ge(panel_lo, 2 * (FIRST_PANEL[s] + q + 1))
                    parts = {}
                    for c in range(4):
                        parts.setdefault((4 * q + c) // kb, []).append(c)
                    for g, chunks in parts.items():
                        k = 4 * q + chunks[0] - g * kb
                        if k == 0:
                            psum_free(s, g)
                        if g == 0:
                            ready(k + len(chunks))
                        last = products((FIRST_GROUP[s] + g) % 2, (FIRST_PANEL[s] + q) % SPLIT, operand, k,
                                        k == 0, k + len(chunks) == kb, chunks=chunks,
                                        each=bank_done if k + len(chunks) == kb and by_bank(s, g) else None)
                    last.then_inc(panel_used, 1)

            def mod_panel(s, g, p, acc):
                q = FIRST_PANEL[s] + 2 * g + p
                pe.wait_ge(panel_lo, 2 * (q + 1))
                if p == 0:
                    need(pe, summed, FIRST_GROUP[s] + g - (0 if s else 1))
                for c in range(4):
                    w = slice(c * CHUNK, c * CHUNK + CHUNK)
                    pe.matmul(acc, c_r[:, 4 * p + c, :], w_hi[:, q % SPLIT, w], start=p == 0 and c == 0, stop=False)
                    last = pe.matmul(acc, c_r[:, 4 * p + c, :], w_lo[:, q % SPLIT, w], start=False,
                                     stop=p == 1 and c == 3)
                last.then_inc(panel_used, 1)

            def mod_columns(rows, to, n):
                for m in range(n):
                    last = pe.matmul(to[:, m:m + 1], rows[0:2, m * P:m * P + P], ones[0:2, 0:1], start=True, stop=True)
                last.then_inc(S["mod_cols"], 1)

            def stats(n, mean, stage=None):
                b = stat_bank(stage)
                to = banks[:, b, :] if mean else banks[:, b, T:2 * T]
                first = BANKS - 1 if stage in NORMED else 0
                for m in range(first, KD):
                    if stage in NORMED and m == first:
                        pe.wait_ge(S["norm_part"], 3 * NORMED.index(stage) + 3)
                        both = part[:, :, :]
                    else:
                        pe.wait_ge(S["squares"], KD * n + m + 1)
                        both = XS[:, m, :, :]
                    rhs = both.rearrange("p a t -> p (a t)") if mean else both[:, 1, :]
                    last = pe.matmul(to, mean_w[:, :], rhs, start=m == first, stop=m == KD - 1)
                last.then_inc(S["stat_sums"], 1)

            def bias_rows(first, n):
                for h in range(first, first + n):
                    if h >= 2:
                        pe.wait_ge(S["rev_copied"], h - 1)
                    pe.matmul(banks[:, 1 + h % 2, :], rel[0:33, h:h + 1].to_broadcast([33, P]), onehot[:, :],
                              start=True, stop=True).then_inc(S["rev_done"], 1)

            pe.wait_ge(S["consts_ready"], 7)
            pe.wait_ge(S["c_lo"], 1)
            for g in range(4):
                for p in range(2):
                    mod_panel(0, g, p, banks[:, BANKS * (g % 2), :])
                if g == 1:
                    stats(0, False, "x")
                    pe.wait_ge(S["rel_loaded"], 32)
                    pe.wait_ge(S["rel_masked"], 1)
                if g:
                    bias_rows((0, 2, 5)[g - 1], (2, 3, 3)[g - 1])
            pe.wait_ge(summed, 4)
            mod_columns(mod_row, banks[:, 7, 0:16], 16)
            pe.wait_ge(S["rev_copied"], HEADS)
            stage_k8("u", H, norm_block(0))
            for name in ("v", "gate_a", "gate_b"):
                stage_k8(name, H)

            pe.wait_ge(summed, FIRST_GROUP[INDEX["branch_gm"]] - 1)
            stats(1, False)
            pe.wait_ge(summed, FIRST_GROUP[INDEX["branch_gm"]])
            for m in range(KD):
                pe.wait_ge(S["sgu_vn"], m + 1)
                for t in range(TT):
                    last = pe.transpose(banks[:, 1 + m // 2, (m % 2 * TT + t) * P:(m % 2 * TT + t + 1) * P],
                                        v_t[:, m, t * P:t * P + P], ident[:, :])
                if m % 2:
                    last.then_inc(S["sgu_vt"], 1)
            pe.wait_ge(S["ws_masked"], 1)
            for m in range(KD):
                if m % 2 == 0:
                    pe.wait_ge(S["sgu_vcopy"], m // 2 + 1)
                for t in range(TT):
                    to = banks[:, (5, 6, 7, 0)[m // 2], (m % 2 * TT + t) * P:(m % 2 * TT + t + 1) * P]
                    pe.matmul(to, v_nat[:, m, t, :], ws[:, m, :], start=True, stop=False)
                    last = pe.matmul(to, ones[0:1, :], bs[0:1, m * P:m * P + P], start=False, stop=True)
                if m % 2:
                    last.then_inc(S["sgu_mix"], 1)
            stage_k8("branch_gm", YA, lambda k: pe.wait_ge(S["sgu_lo"], 4))
            stage_k8("xbc", H)
            stage_k8("z", H)

            pe.wait_ge(summed, FIRST_GROUP[INDEX["mod_rest"]] - 1)
            pe.wait_ge(S["wdt_lo"], 1)
            for t in range(TT):
                acc = banks[:, 0, t * 64:t * 64 + 64]
                for k in range(KD):
                    pe.matmul(acc, H[:, k, 0, t * P:t * P + P], wdt_r[:, k, :, :].rearrange("p a h -> p (a h)"),
                              start=k == 0, stop=False)
                    last = pe.matmul(acc[:, 0:32], H[:, k, 1, t * P:t * P + P], wdt_r[:, k, 0, :],
                                     start=False, stop=k == KD - 1)
            last.then_inc(S["dt_raw"], 1)
            a_v = dtv[:, 3, :, :]
            pe.wait_ge(S["dt_a"], 1)
            pe.matmul(banks[:, 1, 0:32], tri[:, :], a_v[:, 0, :], start=True, stop=True)
            pe.matmul(banks[:, 1, 32:64], ones[:, :], a_v[:, 0, :], start=True, stop=False)
            pe.matmul(banks[:, 1, 32:64], tri[:, :], a_v[:, 1, :], start=False, stop=True)
            pe.matmul(banks[0:32, 2, 0:P], a_v[:, 0, :], tri[:, :], start=True, stop=True)
            pe.matmul(banks[0:32, 2, P:T], a_v[:, 0, :], ones[:, :], start=True, stop=False)
            pe.matmul(banks[0:32, 2, P:T], a_v[:, 1, :], tri[:, :], start=False, stop=True)\
                .then_inc(S["cum_done"], 1)

            B = xbc[:, 16:24, :]
            C = xbc[:, 24:32, :]

            rest = INDEX["mod_rest"]

            def rest_columns(g):
                pe.wait_ge(summed, FIRST_GROUP[rest] + g + 1)
                mod_columns(mod_tail, banks[:, 1, 3 * P + 4 * g:3 * P + 4 * g + 4], 4)

            def scores_and_tokens(g):
                if g:
                    pe.wait_ge(S["cb_copied"], g)
                pe.matmul(banks[:, 1, 0:T], B[:, g, 0:P], C[:, g, :], start=True, stop=True)
                pe.matmul(banks[:, 1, T:3 * P], B[:, g, P:T], C[:, g, P:T], start=True, stop=True)\
                    .then_inc(S["cb_done"], 1)
                if g:
                    pe.wait_ge(S["xdt_done"], 2 * g)
                for t in range(TT):
                    for m in range(2):
                        last = pe.transpose(banks[:, 2, (2 * t + m) * P:(2 * t + m + 1) * P],
                                            xbc[:, 2 * g + m, t * P:t * P + P], ident[:, :])
                last.then_inc(S["xt_done"], 1)

            def decay_rows(n):
                for r in range(2):
                    if n:
                        pe.wait_ge(S["exp_done"], 4 * (n - 1) + 2 * (r + 1))
                    h = 2 * n + r
                    pick = ident_r[0:32, h:h + 1].to_broadcast([32, P])
                    for at, tokens in ((0, slice(0, T)), (T, slice(P, T))):
                        to = banks[:, 3 + r, at:at + tokens.stop - tokens.start]
                        pe.matmul(to, pick, cum_r[:, 0, tokens], start=at == 0, stop=False)
                        pe.matmul(to, pick, cum_r[:, 1, tokens], start=False, stop=False)
                    diagonal = banks[:, 3 + r, :].rearrange("p (a i) -> p a i", i=P)[:, 0:3:2, :]
                    last = pe.matmul(diagonal, ident_r[:, :], never[:, :].unsqueeze(1).to_broadcast([P, 2, P]),
                                     start=False, stop=True)
                last.then_inc(S["row_done"], 1)

            def head_outputs(n):
                g = n // 2
                pe.wait_ge(S["m_done"], n + 1)
                pe.wait_ge(S["xdt_done"], 2 * (g + 1))
                if n >= 2:
                    pe.wait_ge(S["y_skip"], n - 1)
                m_of = decay(n)
                for r in range(2):
                    to = banks[HP * r:HP * r + HP, 5 + n % 2, 0:T]
                    cut = slice((n % 2 * 2 + r) * HP, (n % 2 * 2 + r + 1) * HP)
                    pe.matmul(to, xdt(g, 0)[:, cut], m_of[:, r * 3 * P:r * 3 * P + T], start=True, stop=False)
                    last = pe.matmul(to[:, P:T], xdt(g, 1)[:, cut], m_of[:, r * 3 * P + T:(r + 1) * 3 * P],
                                     start=False, stop=True)
                last.then_inc(S["y_done"], 1)

            def group_sums(g):
                pe.wait_ge(S["y_sq"], 2 * (g + 1))
                if g:
                    pe.wait_ge(S["y_var"], g)
                for m in range(2):
                    last = pe.matmul(banks[:, 7, 0:T], gmean_w[:, :], sq[:, 2 * (g % 2) + m, :],
                                     start=m == 0, stop=m == 1)
                last.then_inc(S["y_sums"], 1)

            def normed_y(k):
                pe.wait_ge(S["y_lo"], k // 2)

            pe.wait_ge(S["cum_lo"], 1)
            pe.wait_ge(S["cum_got"], 1)
            pe.wait_ge(summed, FIRST_GROUP[INDEX["mod_rest"]])
            pe.wait_ge(S["ident_r_ready"], 1)
            pe.wait_ge(S["never_set"], 1)
            pairs = 2 * SSM_GROUPS
            for n in range(pairs + 3):
                if n == pairs:
                    pe.wait_ge(S["cb_copied"], SSM_GROUPS)
                    rest_columns(SSM_GROUPS - 1)
                if n == pairs + 1:
                    pe.wait_ge(S["mod_ready"], 2)
                    stage_long("branch_ssm", YB, 16, normed_y, slice(0, 1))
                if n < pairs and n % 2 == 0:
                    scores_and_tokens(n // 2)
                if n < pairs:
                    decay_rows(n)
                    if n % 2 and n > 1:
                        pe.wait_ge(S["cb_copied"], n // 2 + 1)
                        rest_columns(n // 2 - 1)
                    mod_panel(rest, n // 2, n % 2, banks[:, 0, :])
                if 0 < n <= pairs:
                    head_outputs(n - 1)
                if n >= 4 and n % 2 == 0:
                    group_sums((n - 4) // 2)

            stage_long("branch_ssm", YB, 16, normed_y, slice(1, None))
            stage_k8("out", MX, operand_of("branch_ssm", 4))
            stats(2, False, "out")
            stage_k8("ff1", H, norm_block(1))
            stage_long("ff2", HH, 32, operand_of("ff1", 4))
            stats(3, False, "ff2")

            norm = [4]

            def feed_forward(i):
                stage_k8(f"gu{i}", H, norm_block(norm[0] - 2))
                stage_long(f"down{i}", HH, 22, operand_of(f"gu{i}", 2))
                stats(norm[0], True, f"down{i}")
                norm[0] += 1

            feed_forward(0)

            stage_k8("qkv", H, norm_block(norm[0] - 2))
            for h in range(HEADS):
                if h % 4 == 0:
                    pe.wait_ge(summed, FIRST_GROUP[INDEX["att_out"]] - 1 + h // 4)
                for t in range(TT):
                    last = pe.transpose(banks[:, 4 + h // 2, (h % 2 * TT + t) * P:(h % 2 * TT + t + 1) * P],
                                        qkv[:, 16 + h, t * P:t * P + P], ident[:, :])
                if h % 2:
                    last.then_inc(S["vt_done"], 1)

            def att_scores(h):
                if h >= 2:
                    pe.wait_ge(S["s_max"], h - 1)
                to = banks[:, h % 2, :]
                pe.matmul(to[:, 0:P], qkv[:, h, 0:P], qkv[:, 8 + h, 0:P], start=True, stop=True)
                pe.matmul(to[:, P:3 * P], qkv[:, h, P:T], qkv[:, 8 + h, :], start=True, stop=True)\
                    .then_inc(S["s_done"], 1)

            def att_transpose(h):
                pe.wait_ge(S["p_norm"], h + 1)
                if h >= 1:
                    pe.wait_ge(S["pt_copied"], h)
                for n in range(3):
                    last = pe.transpose(banks[:, 2, n * P:n * P + P], probs[:, h % 3, n * P:n * P + P], ident[:, :])
                last.then_inc(S["pt_done"], 1)

            def att_values(h):
                pe.wait_ge(S["pt_copied"], h + 1)
                if h >= 1:
                    pe.wait_ge(S["o_copied"], h)
                pe.matmul(banks[:, 3, 0:T], v_tok[:, 0, h * P:h * P + P], probs_t[:, h % 2, 0:T], start=True, stop=False)
                pe.matmul(banks[:, 3, P:T], v_tok[:, 1, h * P:h * P + P], probs_t[:, h % 2, T:3 * P],
                          start=False, stop=True).then_inc(S["o_done"], 1)

            for h in range(HEADS + 3):
                if h < HEADS:
                    att_scores(h)
                if 2 <= h < HEADS + 2:
                    att_transpose(h - 2)
                if h == 3:
                    pe.wait_ge(S["v_copied"], 4)
                if h >= 3:
                    att_values(h - 3)
            pe.wait_ge(S["o_lo"], HEADS)
            stage_k8("att_out", H)
            stats(norm[0], True, "att_out")
            norm[0] += 1
            feed_forward(1)
            feed_forward(2)

            stage_k8("pool_in", H, norm_block(norm[0] - 2))
            s = INDEX["pool_group"]
            pe.wait_ge(panel_lo, 2 * (FIRST_PANEL[s] + 1))
            pe.wait_ge(summed, FIRST_GROUP[s])
            for m in (4, 5, 6, 7, 0, 1, 2, 3):
                if m % 4 == 0:
                    pe.wait_ge(S["pool_lo_wide" if m else "pool_lo"], 1)
                for k in range(2):
                    at = (m // 2) * CHUNK + k * T + (m % 2) * P
                    pair = PG[:, m // 2 * 2 + k, :, :].rearrange("p a t -> p (a t)")
                    acc = banks[:, BANKS * ((FIRST_GROUP[s] + m // 4) % 2) + m % 4, :]
                    pe.matmul(acc, w_hi[:, FIRST_PANEL[s] % SPLIT, at:at + P], pair, start=k == 0, stop=False)
                    last = pe.matmul(acc[:, 0:T], w_lo[:, FIRST_PANEL[s] % SPLIT, at:at + P], pair[:, 0:T],
                                     start=False, stop=k == 1)
            last.then_inc(panel_used, 1)
            stage_k8("pool_out", H, operand_of("pool_group", 4))
            stats(norm[0], True, "pool_out")
            norm[0] += 1
            feed_forward(3)

        @block.scalar
        def _(act):
            def split(q, r, sl, turn):
                act.wait_ge(loaded[r], 16 * turn + 16)
                need(act, panel_used, q - SPLIT + 1)
                for half in range(2):
                    w = slice(half * PANEL // 2, (half + 1) * PANEL // 2)
                    act.activation(w_hi[:, sl, w], raw[:, r, w], ACT.Copy).then_inc(panel_hi, 1)

            def square(s, g, b):
                if b < BANKS - 1:
                    act.wait_ge(bank_x, bank_count(s, b))
                else:
                    act.wait_ge(posted, before("posted", s) + g + 1)
                act.activation(sq[:, BANKS * g + b, :], xb[:, BANKS * g + b, :], ACT.Square).then_inc(S["squares"], 1)

            def correction(s, g, G):
                kind = STAGES[s][3]
                if kind in ("act", "conv"):
                    need(act, activated, before("activated", s) + g - 1)
                elif kind in ("gate", "add1", "deep"):
                    need(act, posted, before("posted", s) + g - 1)
                elif kind in COUNTED["operand"]:
                    need(act, operand_lo, before("operand", s) + g - 1)
                elif kind == "keep":
                    need(act, summed, FIRST_GROUP[s] + g - 1)
                if by_bank(s, g):
                    for b in range(BANKS):
                        if b < BANKS - 1:
                            act.wait_ge(bank_done, bank_count(s, b))
                        else:
                            act.wait_ge(panel_used, through(s, g))
                        act.activation(ev[:, G, b, :], banks[:, BANKS * G + b, T:CHUNK], ACT.Copy)\
                            .then_inc(bank_corr if b < BANKS - 1 else corrected, 1)
                        if b:
                            square(s, g, b - 1)
                    square(s, g, BANKS - 1)
                    return
                act.wait_ge(panel_used, through(s, g))
                act.activation(ev[:, G, :, :], banks[:, BANKS * G:BANKS * G + BANKS, T:CHUNK], ACT.Copy)\
                    .then_inc(corrected, 1)

            def stage(name, post):
                def take_up(s, g, G):
                    if STAGES[s][3] != "mod":
                        correction(s, g, G)
                    post(s, g, G)
                run(act, INDEX[name], split, take_up)

            def nothing(s, g, G):
                pass

            def activate_into(func, dest):
                def post(s, g, G):
                    act.wait_ge(summed, FIRST_GROUP[s] + g + 1)
                    act.activation(by_group(dest[:, :, :])[:, g, :, :], ev[:, G, :, :], func).then_inc(activated, 1)
                return post

            def v_post(s, g, G):
                activate_into(ACT.Gelu_apprx_tanh, v_t)(s, g, G)
                act.wait_ge(activated, before("activated", s) + g + 1)
                act.activation(by_group(sq)[:, g, :, :], by_group(v_t[:, :, :])[:, g, :, :], ACT.Square)\
                    .then_inc(S["squares"], BANKS)

            def conv_first_tap(s, g, G):
                act.wait_ge(summed, FIRST_GROUP[s] + g + 1)
                for b in range(BANKS):
                    act.activation(ev[:, G, b, :], pad[:, b, 0:T], ACT.Identity, bias=conv_b[:, g, b:b + 1],
                                   scale=conv_w[:, g, CONV * b:CONV * b + 1]).then_inc(S["conv_first"], 1)

            def conv_silu(s, g, G):
                act.wait_ge(posted, before("posted", s) + g + 1)
                act.activation(by_group(xbc[:, :, :])[:, g, :, :], ev[:, G, :, :], ACT.Silu).then_inc(activated, 1)

            def round_into(dest, blocks=BANKS):
                view = dest[:, :, 0, :].rearrange("p (g b) t -> p g b t", b=blocks)

                def post(s, g, G):
                    act.wait_ge(posted, before("posted", s) + g + 1)
                    act.activation(view[:, g, :, :], ev[:, G, 0:blocks, :], ACT.Copy).then_inc(operand_hi, 1)
                return post

            def glu_post(s, g, G):
                act.wait_ge(summed, FIRST_GROUP[s] + g + 1)
                act.activation(ev[:, G, 0:2, :], ev[:, G, 0:2, :], ACT.Silu).then_inc(activated, 1)
                round_into(HH, 2)(s, g, G)

            def squares_post(s, g, G):
                if by_bank(s, g):
                    return
                act.wait_ge(posted, before("posted", s) + g + 1)
                act.activation(by_group(sq)[:, g, :, :], by_group(xb)[:, g, :, :], ACT.Square)\
                    .then_inc(S["squares"], BANKS)

            act.wait_ge(S["tiny_set"], 1)

            def load_table(func):
                act.activation(tiny[:, 1:2], tiny[:, 0:1], func).then_inc(act_step, 1)

            def root(n):
                load_table(ACT.Sqrt)
                act.wait_ge(S["stat_var"], n + 1)
                act.activation(st[:, 1, :], st[:, 1, :], ACT.Sqrt).then_inc(S["stat_root"], 1)

            def norm_rounded(k, src, bias):
                for m in range(KD):
                    act.wait_ge(S["norm_y"], KD * k + m + 1)
                    if bias is None:
                        ins = act.activation(H[:, m, 0, :], src[:, m, :], ACT.Copy)
                    else:
                        ins = act.activation(H[:, m, 0, :], src[:, m, :], ACT.Identity, bias=bias[:, m:m + 1])
                    ins.then_inc(S["norm_hi"], 1)

            act.wait_ge(S["c_loaded"], 16)
            act.activation(c_s[:, :], c_f[:, :], ACT.Silu).then_inc(S["c_silu"], 1)
            act.wait_ge(S["c_silu"], 1)
            act.wait_ge(S["c_zero"], 1)
            act.activation(c_r[:, :, 0], c_s[:, :], ACT.Copy).then_inc(S["c_hi"], 1)
            split(0, 0, 0, 0)
            split(1, 1, 1, 0)

            def start_work(s, g, G):
                if g == 0:
                    act.wait_ge(S["x_loaded"], 16)
                    for half in range(2):
                        act.activation(by_group(sq)[:, half, :, :], by_group(xb)[:, half, :, :], ACT.Square)\
                            .then_inc(S["squares"], BANKS)
                    return
                for h in range(*((0, 2), (2, 5), (5, 8))[g - 1]):
                    act.wait_ge(S["rev_done"], h + 1)
                    act.activation(rev[:, h, :], banks[:, 1 + h % 2, :], ACT.Copy).then_inc(S["rev_copied"], 1)

            stage("mod_norm", start_work)
            act.wait_ge(S["consts_ready"], 7)
            act.activation(ident_r[:, :], ident[:, :], ACT.Copy).then_inc(S["ident_r_ready"], 1)
            root(0)
            norm_rounded(0, ev8, mod[:, 0:8])

            stage("u", activate_into(ACT.Gelu_apprx_tanh, u_t))
            stage("v", v_post)
            act.wait_ge(S["rev_stored"], 16)
            stage("gate_a", activate_into(ACT.Sigmoid, gate_a))
            stage("gate_b", activate_into(ACT.Sigmoid, gate_b))
            root(1)
            for j in range(4):
                act.wait_ge(S["sgu_vt"], j + 1)
                act.activation(v_nat[:, 2 * j:2 * j + 2, :, :].rearrange("p m t d -> p (m t d)"),
                               banks[:, 1 + j, :], ACT.Copy).then_inc(S["sgu_vcopy"], 1)
            for j in range(4):
                act.wait_ge(S["sgu_y"], j + 1)
                act.activation(YA[:, 2 * j:2 * j + 2, 0, :], ev8[:, 2 * j:2 * j + 2, :], ACT.Copy)\
                    .then_inc(S["sgu_hi"], 1)
            stage("branch_gm", nothing)
            load_table(ACT.Silu)
            s = INDEX["xbc"]
            G = FIRST_GROUP[s] % 2

            def conv_body(g, u, turn, silu=True):
                split(*ahead(s, g, u, turn, 0))
                split(*ahead(s, g, u, turn, 1))
                correction(s, g, (G + u) % 2)
                conv_first_tap(s, g, (G + u) % 2)
                if silu:
                    conv_silu(s, g - 1, (G + u + 1) % 2)

            n = STAGES[s][2]
            conv_body(0, 0, None, False)
            conv_body(1, 1, None)
            with act.Fori(1, n // 2) as turn:
                conv_body(2 * turn, 0, turn)
                conv_body(2 * turn + 1, 1, turn)
            conv_silu(s, n - 1, (G + 1) % 2)
            act.wait_ge(S["late_loaded"], 64)
            act.activation(wdt_r[:, :, 0, :], wdt[:, :, :], ACT.Copy).then_inc(S["wdt_hi"], 1)
            stage("z", activate_into(ACT.Silu, z_t))

            act.activation(ea[:, :], heads[:, 1, :], ACT.Exp).then_inc(S["dt_ea"], 1)
            act.wait_ge(S["dt_y"], 1)
            act.activation(dtv[:, 0, :, :], dtv[:, 0, :, :], ACT.Exp).then_inc(S["dt_exp"], 1)
            act.wait_ge(S["dt_one"], 1)
            act.activation(dtv[:, 0, :, :], dtv[:, 0, :, :], ACT.Ln).then_inc(S["dt_ln"], 1)
            act.wait_ge(S["cum_done"], 1)
            act.activation(cum_r[:, 0, :], banks[0:32, 2, 0:T], ACT.Copy).then_inc(S["cum_hi"], 1)

            act.wait_ge(S["cum_got"], 1)
            pairs = 2 * SSM_GROUPS
            for n in range(pairs + 5):
                if n < pairs and n % 2 == 0:
                    g = n // 2
                    act.wait_ge(S["cb_done"], g + 1)
                    if g >= 2:
                        act.wait_ge(S["m_done"], 2 * (g - 1))
                    act.activation(cb[:, g % 2, :], banks[:, 1, 0:3 * P], ACT.Copy).then_inc(S["cb_copied"], 1)
                if n < pairs:
                    act.wait_ge(S["row_done"], n + 1)
                    if n >= 2:
                        act.wait_ge(S["y_done"], n - 1)
                    for r in range(2):
                        h = 2 * n + r
                        for t, (at, size) in enumerate(((0, T), (T, P))):
                            act.activation(decay(n)[:, 3 * P * r + at:3 * P * r + at + size],
                                           banks[:, 3 + r, at:at + size], ACT.Exp,
                                           bias=dtv[:, 4, t, h:h + 1]).then_inc(S["exp_done"], 1)
                    q = FIRST_PANEL[INDEX["mod_rest"]] + n + SPLIT
                    split(q, q % RAW, q % SPLIT, q // RAW)
                if 2 <= n < pairs + 2:
                    m = n - 2
                    act.wait_ge(S["y_gated"], m + 1)
                    if m >= 4:
                        act.wait_ge(S["y_sums"], m // 2 - 1)
                    act.activation(sq[:, m % 4, :], xbc[:, m, :], ACT.Square).then_inc(S["y_sq"], 1)
                if n == pairs + 2:
                    q = FIRST_PANEL[INDEX["branch_ssm"]] + SPLIT
                    split(q, q % RAW, q % SPLIT, q // RAW)
                if n >= 6 and n % 4 == 2:
                    j = (n - 6) // 4
                    act.wait_ge(S["y_var"], 2 * j + 2)
                    act.activation(st[:, 0:2, :], st[:, 0:2, :], ACT.Sqrt).then_inc(S["y_root"], 1)
                if n >= 7 and n % 4 in (3, 0):
                    g = (n - 6) // 2
                    act.wait_ge(S["y_f"], 2 * (g + 1))
                    act.activation(YB[:, 2 * g:2 * g + 2, 0, :], xbc[:, 2 * g:2 * g + 2, :], ACT.Copy)\
                        .then_inc(S["y_hi"], 1)
            stage("branch_ssm", round_into(MX))
            stage("out", squares_post)
            root(2)
            norm_rounded(1, ev8, mod[:, 24:32])
            stage("ff1", round_into(HH))
            stage("ff2", squares_post)
            root(3)
            norm_rounded(2, xb, None)

            norms = [3]

            def layer_norm(last=False):
                root(norms[0] + 1)
                if not last:
                    at = COLS["ln_b"] + KD * (norms[0] - 3)
                    norm_rounded(norms[0], xb, cols[:, at:at + KD])
                norms[0] += 1

            def feed_forward(i, last=False):
                load_table(ACT.Silu)
                stage(f"gu{i}", glu_post)
                stage(f"down{i}", squares_post)
                layer_norm(last)

            feed_forward(0)
            stage("qkv", nothing)
            for j in range(4):
                act.wait_ge(S["vt_done"], j + 1)
                act.activation(v_tok[:, :, 2 * j * P:(2 * j + 2) * P].rearrange("p t (h d) -> p h t d", h=2),
                               banks[:, 4 + j, :].rearrange("p (h t d) -> p h t d", h=2, t=TT), ACT.Copy)\
                    .then_inc(S["v_copied"], 1)
            for h in range(HEADS + 4):
                if h < HEADS:
                    act.wait_ge(S["s_max"], h + 1)
                    act.activation(probs[:, h % 3, 0:P], probs[:, h % 3, 0:P], ACT.Exp, bias=sm[:, h, 2:3],
                                   accum_out=sm[:, h, 4:5]).then_inc(S["p_exp"], 1)
                    act.activation(probs[:, h % 3, P:3 * P], probs[:, h % 3, P:3 * P], ACT.Exp, bias=sm[:, h, 3:4],
                                   accum_out=sm[:, h, 5:6]).then_inc(S["p_exp"], 1)
                if 2 <= h < HEADS + 2:
                    m = h - 2
                    act.wait_ge(S["pt_done"], m + 1)
                    if m >= 2:
                        act.wait_ge(S["o_done"], m - 1)
                    act.activation(probs_t[:, m % 2, :], banks[:, 2, 0:3 * P], ACT.Copy).then_inc(S["pt_copied"], 1)
                if h >= 4:
                    m = h - 4
                    act.wait_ge(S["o_copied"], m + 1)
                    act.activation(H[:, m, 0, :], o_t[:, m % 2, :], ACT.Copy).then_inc(S["o_hi"], 1)
            stage("att_out", squares_post)
            layer_norm()
            feed_forward(1)
            feed_forward(2)
            stage("pool_in", nothing)
            for n, g in enumerate((1, 0)):
                b = slice(BANKS * g, BANKS * g + BANKS)
                act.wait_ge(S["pool_f"], n + 1)
                act.activation(PG[:, b, 0, :], pooled[:, b, :], ACT.Copy).then_inc(S["pool_hi"], 1)
            stage("pool_group", round_into(H))
            stage("pool_out", squares_post)
            layer_norm()
            feed_forward(3, last=True)

        @block.vector
        def _(vec):
            steps = [0]

            def step(ins):
                steps[0] += 1
                ins.then_inc(vec_step, 1)
                vec.wait_ge(vec_step, steps[0])

            def mark(ins):
                steps[0] += 1
                ins.then_inc(vec_step, 1)

            def split(q, r, sl, turn, halves=(0, 1)):
                for half in halves:
                    w = slice(half * PANEL // 2, (half + 1) * PANEL // 2)
                    vec.wait_ge(panel_hi, 2 * q + half + 1)
                    vec.tensor_tensor(w_lo[:, sl, w], raw[:, r, w], w_hi[:, sl, w], ALU.subtract).then_inc(panel_lo, 1)

            def take_sum(s, g, G, dest=None):
                vec.wait_ge(corrected, before("corrected", s) + g + 1)
                to = ev[:, G, :, :] if dest is None else dest
                vec.tensor_tensor(to, banks[:, BANKS * G:BANKS * G + BANKS, 0:T], ev[:, G, :, :], ALU.add)\
                    .then_inc(summed, 1)

            def own_sum(s, g):
                vec.wait_ge(summed, FIRST_GROUP[s] + g + 1)

            def bank_post(s, g, G, b, new_x):
                last = b == BANKS - 1
                e = ev[:, G, b, :]
                if last:
                    vec.wait_ge(corrected, before("corrected", s) + g + 1)
                else:
                    vec.wait_ge(bank_corr, bank_count(s, b))
                vec.tensor_tensor(e, banks[:, BANKS * G + b, 0:T], e, ALU.add).then_inc(summed if last else bank_sum, 1)
                if last:
                    own_sum(s, g)
                else:
                    vec.wait_ge(bank_sum, bank_count(s, b))
                new_x(BANKS * g + b, e).then_inc(posted if last else bank_x, 1)

            def stage(name, post, dest=None):
                def take_up(s, g, G):
                    if STAGES[s][3] == "mod":
                        vec.wait_ge(panel_used, through(s, g))
                        vec.tensor_copy(dest[0:2, g, :], banks[0:2, BANKS * G, :]).then_inc(summed, 1)
                        return
                    take_sum(s, g, G, None if dest is None else by_group(dest[:, :, :])[:, g, :, :])
                    post(s, g, G)
                run(vec, INDEX[name], split, take_up)

            def nothing(s, g, G):
                pass

            def lo_into(dest, blocks=BANKS):
                view = dest.rearrange("p (g b) a t -> p g b a t", b=blocks)

                def post(s, g, G):
                    vec.wait_ge(operand_hi, before("operand", s) + g + 1)
                    vec.tensor_tensor(view[:, g, :, 1, :], ev[:, G, 0:blocks, :], view[:, g, :, 0, :], ALU.subtract)\
                        .then_inc(operand_lo, 1)
                return post

            def glu_post(s, g, G):
                vec.wait_ge(activated, before("activated", s) + g + 1)
                vec.scalar_tensor_tensor(ev[:, G, 0:2, :], ev[:, G, 0:2, :], 0.5, ev[:, G, 2:4, :], ALU.mult, ALU.mult)\
                    .then_inc(posted, 1)
                lo_into(HH[:, 0:22, :, :], 2)(s, g, G)

            def relu2_post(s, g, G):
                own_sum(s, g)
                vec.scalar_tensor_tensor(ev[:, G, :, :], ev[:, G, :, :], 0.0, ev[:, G, :, :], ALU.max, ALU.mult)\
                    .then_inc(posted, 1)
                lo_into(HH[:, :, :, :])(s, g, G)

            def deep_x(m, e):
                return vec.scalar_tensor_tensor(xb[:, m, :], xb[:, m, :], ALPHA, e, ALU.mult, ALU.add)

            def gated_x(col):
                def new_x(m, e):
                    return vec.scalar_tensor_tensor(xb[:, m, :], e, mod[:, col + m:col + m + 1], xb[:, m, :],
                                                    ALU.mult, ALU.add)
                return new_x

            def stage_x(name, new_x, biased=0):
                def take_up(s, g, G):
                    if biased:
                        vec.wait_ge(S["norm_x"], KD * biased)
                    if by_bank(s, g):
                        for b in range(BANKS):
                            bank_post(s, g, G, b, new_x)
                        return
                    take_sum(s, g, G)
                    own_sum(s, g)
                    for b in range(BANKS):
                        last = new_x(BANKS * g + b, ev[:, G, b, :])
                    last.then_inc(posted, 1)
                run(vec, INDEX[name], split, take_up, last_split=False)

            def split_after(stage_name, half):
                q = FIRST_PANEL[INDEX[stage_name] + 1] - 1 + SPLIT
                if q < PANELS:
                    split(q, q % RAW, q % SPLIT, q // RAW, (half,))

            def gate_post(s, g, G):
                own_sum(s, g)
                a = by_group(gate_a[:, :, :])[:, g, :, :]
                vec.tensor_tensor(a, a, ev[:, G, :, :], ALU.mult).then_inc(posted, 1)

            def mix_post(s, g, G):
                own_sum(s, g)
                e = ev[:, G, :, :]
                step(vec.tensor_tensor(e, e, by_group(gate_b[:, :, :])[:, g, :, :], ALU.mult))
                vec.tensor_tensor(e, e, by_group(gate_a[:, :, :])[:, g, :, :], ALU.add).then_inc(posted, 1)
                lo_into(MX[:, :, :, :])(s, g, G)

            def scale_post(s, g, G):
                own_sum(s, g)
                for b in range(BANKS):
                    at = COLS["pool_scale"] + BANKS * g + b
                    last = vec.tensor_scalar(ev[:, G, b, :], ev[:, G, b, :], cols[:, at:at + 1], None, ALU.mult)
                last.then_inc(posted, 1)
                lo_into(H[:, :, :, :])(s, g, G)

            def variance(n, mean, eps, stage=None):
                vec.wait_ge(S["stat_sums"], n + 1)
                b = stat_bank(stage)
                if mean:
                    vec.tensor_copy(st[:, 0, :], banks[:, b, 0:T]).then_inc(S["stat_mean"], 1)
                    vec.wait_ge(S["stat_mean"], n - 3)
                    step(vec.tensor_tensor(st[:, 3, :], st[:, 0, :], st[:, 0, :], ALU.mult))
                    step(vec.tensor_tensor(st[:, 1, :], banks[:, b, T:2 * T], st[:, 3, :], ALU.subtract))
                    vec.tensor_scalar(st[:, 1, :], st[:, 1, :], 0.0, eps, ALU.max, ALU.add).then_inc(S["stat_var"], 1)
                else:
                    vec.tensor_scalar(st[:, 1, :], banks[:, b, T:2 * T], eps, None, ALU.add).then_inc(S["stat_var"], 1)

            def inverse_root(n):
                vec.wait_ge(S["stat_root"], n + 1)
                step(vec.reciprocal(st[:, 2, :], st[:, 1, :]))

            def apply_norm(k, dest, scale, bias, mean, operand=True, behind=None):
                def scaled(m):
                    if mean:
                        vec.wait_ge(S["norm_centred"], KD * (k - 3) + m + 1)
                    vec.scalar_tensor_tensor(dest[:, m, :], xb[:, m, :], scale[:, m:m + 1], st[:, 2, :], ALU.mult,
                                             ALU.mult).then_inc(S["norm_y"], 1)

                def lo(m):
                    vec.wait_ge(S["norm_hi"], KD * k + m + 1)
                    if bias is None:
                        ins = vec.tensor_tensor(H[:, m, 1, :], dest[:, m, :], H[:, m, 0, :], ALU.subtract)
                    else:
                        ins = vec.scalar_tensor_tensor(H[:, m, 1, :], dest[:, m, :], bias[:, m:m + 1], H[:, m, 0, :],
                                                       ALU.add, ALU.subtract)
                    ins.then_inc(S["norm_lo"], 1)

                def biased(m):
                    vec.wait_ge(S["norm_y"], KD * k + m + 1)
                    vec.tensor_scalar(dest[:, m, :], dest[:, m, :], bias[:, m:m + 1], None, ALU.add)\
                        .then_inc(S["norm_x"], 1)

                for m in range(KD + 1):
                    if m == 5 and behind is not None:
                        split_after(behind, 1)
                    if m < KD:
                        scaled(m)
                    if m:
                        (lo if operand else biased)(m - 1)

            def mod_taken(n, taken, first, count, scales):
                vec.wait_ge(S["mod_cols"], 1 if n == 1 else 1 + SSM_GROUPS)
                step(vec.tensor_tensor(mod[:, first:first + count], taken,
                                       cols[:, COLS["b_mod"] + first:COLS["b_mod"] + first + count], ALU.add))
                vec.tensor_scalar(mod[:, scales:scales + 8], mod[:, scales:scales + 8], 1.0, None, ALU.add)\
                    .then_inc(S["mod_ready"], 1)
                vec.wait_ge(S["mod_ready"], n)

            vec.memset(tiny[:, :], 1.0).then_inc(S["tiny_set"], 1)
            vec.wait_ge(S["c_hi"], 1)
            vec.tensor_tensor(c_r[:, :, 1], c_s[:, :], c_r[:, :, 0], ALU.subtract).then_inc(S["c_lo"], 1)
            vec.wait_ge(S["params_loaded"], 16)
            split(0, 0, 0, 0)
            split(1, 1, 1, 0)
            stage("mod_norm", None, mod_row[:, :].rearrange("p (g n) -> p g n", n=CHUNK))
            variance(0, False, EPS, "x")
            inverse_root(0)
            mod_taken(1, banks[:, 7, 0:16], 0, 16, 8)
            apply_norm(0, ev8, mod[:, 8:16], mod[:, 0:8], False)

            stage("u", nothing)
            stage("v", nothing)
            stage("gate_a", nothing)
            stage("gate_b", nothing)

            variance(1, False, EPS)
            inverse_root(1)
            for m in range(KD):
                at = COLS["gm_norm"] + m
                vec.scalar_tensor_tensor(v_t[:, m, :], v_t[:, m, :], cols[:, at:at + 1], st[:, 2, :], ALU.mult,
                                         ALU.mult).then_inc(S["sgu_vn"], 1)
            for j in range(5):
                if j < 4:
                    two = slice(2 * j, 2 * j + 2)
                    vec.wait_ge(S["sgu_mix"], j + 1)
                    mixed = banks[:, (5, 6, 7, 0)[j], :].rearrange("p (m t) -> p m t", m=2)
                    vec.tensor_tensor(ev8[:, two, :], mixed, u_t[:, two, :], ALU.mult).then_inc(S["sgu_y"], 1)
                if j:
                    two = slice(2 * j - 2, 2 * j)
                    vec.wait_ge(S["sgu_hi"], j)
                    vec.tensor_tensor(YA[:, two, 1, :], ev8[:, two, :], YA[:, two, 0, :], ALU.subtract)\
                        .then_inc(S["sgu_lo"], 1)
            stage("branch_gm", gate_post)

            step(vec.memset(pad[:, :, 0:CONV - 1], 0.0))

            def conv_post(s, g, G):
                own_sum(s, g)
                for tap in range(1, CONV):
                    if tap > 1:
                        vec.wait_ge(S["conv_tap"], (CONV - 2) * g + tap - 1)
                    for b in range(BANKS):
                        if tap == 1:
                            vec.wait_ge(S["conv_first"], BANKS * g + b + 1)
                        w = conv_w[:, g, CONV * b + tap:CONV * b + tap + 1]
                        last = vec.scalar_tensor_tensor(ev[:, G, b, :], pad[:, b, tap:tap + T], w, ev[:, G, b, :],
                                                        ALU.mult, ALU.add)
                    last.then_inc(S["conv_tap"] if tap < CONV - 1 else posted, 1)

            def conv_take_up(s, g, G):
                vec.wait_ge(posted, before("posted", s) + g)
                take_sum(s, g, G, pad[:, :, CONV - 1:CONV - 1 + T])
                conv_post(s, g, G)

            run(vec, INDEX["xbc"], split, conv_take_up)
            vec.wait_ge(S["wdt_hi"], 1)
            vec.tensor_tensor(wdt_r[:, :, 1, :], wdt[:, :, :], wdt_r[:, :, 0, :], ALU.subtract).then_inc(S["wdt_lo"], 1)
            stage("z", nothing)

            vec.wait_ge(S["consts_ready"], 7)
            vec.tensor_scalar(never[:, :], tri[:, :], -1.0, -MASKED, ALU.add, ALU.mult).then_inc(S["never_set"], 1)
            scratch, y_v, dt_v, a_v, ncum = (dtv[:, n, :, :] for n in range(5))
            vec.wait_ge(S["dt_raw"], 1)
            step(vec.tensor_copy(scratch, banks[:, 0, 0:P].rearrange("p (t a h) -> p t a h", t=TT, a=2)[:, :, 1, :]))
            step(vec.tensor_tensor(y_v, banks[:, 0, 0:P].rearrange("p (t a h) -> p t a h", t=TT, a=2)[:, :, 0, :],
                                   scratch, ALU.add))
            step(vec.tensor_tensor(y_v, y_v, heads[:, 0, :].unsqueeze(1).to_broadcast([P, TT, 32]), ALU.add))
            vec.scalar_tensor_tensor(scratch, y_v, -1.0, y_v, ALU.mult, ALU.min).then_inc(S["dt_y"], 1)
            vec.wait_ge(S["dt_exp"], 1)
            vec.tensor_scalar(scratch, scratch, 1.0, None, ALU.add).then_inc(S["dt_one"], 1)
            vec.wait_ge(S["dt_ln"], 1)
            step(vec.scalar_tensor_tensor(dt_v, y_v, 0.0, scratch, ALU.max, ALU.add))
            vec.wait_ge(S["dt_ea"], 1)
            vec.scalar_tensor_tensor(a_v, dt_v, -1.0, ea[:, :].unsqueeze(1).to_broadcast([P, TT, 32]),
                                     ALU.mult, ALU.mult).then_inc(S["dt_a"], 1)
            vec.wait_ge(S["cum_done"], 1)
            vec.tensor_scalar(ncum, banks[:, 1, 0:64].rearrange("p (t h) -> p t h", t=TT), -1.0, None, ALU.mult)\
                .then_inc(S["cum_got"], 1)
            vec.wait_ge(S["cum_hi"], 1)
            vec.tensor_tensor(cum_r[:, 1, :], banks[0:32, 2, 0:T], cum_r[:, 0, :], ALU.subtract)\
                .then_inc(S["cum_lo"], 1)
            vec.wait_ge(S["cum_got"], 1)

            pairs = 2 * SSM_GROUPS
            rest = INDEX["mod_rest"]
            for n in range(pairs + 5):
                if n == pairs:
                    mod_taken(2, banks[:, 1, 3 * P:3 * P + 32], 16, 32, 32)
                if n < pairs and n % 2 == 0:
                    g = n // 2
                    vec.wait_ge(S["xt_done"], g + 1)
                    if g >= 2:
                        vec.wait_ge(S["y_done"], 2 * (g - 1))
                    for t in range(TT):
                        vec.tensor_tensor(xdt(g, t).rearrange("p (h d) -> p h d", h=4),
                                          banks[:, 2, t * T:t * T + T].rearrange("p (h d) -> p h d", h=4),
                                          dtv[:, 2, t, 4 * g:4 * g + 4].unsqueeze(2).to_broadcast([P, 4, HP]),
                                          ALU.mult).then_inc(S["xdt_done"], 1)
                if 2 <= n <= pairs + 1:
                    m = n - 2
                    at = COLS["d_skip"] + m
                    vec.wait_ge(S["y_done"], m + 1)
                    vec.scalar_tensor_tensor(xbc[:, m, :], xbc[:, m, :], cols[:, at:at + 1],
                                             banks[:, 5 + m % 2, 0:T], ALU.mult, ALU.add).then_inc(S["y_skip"], 1)
                if n == pairs + 2:
                    q = FIRST_PANEL[INDEX["branch_ssm"]] + SPLIT
                    split(q, q % RAW, q % SPLIT, q // RAW)
                if n >= 4 and n % 2 == 0 and n < pairs + 4:
                    g = (n - 4) // 2
                    vec.wait_ge(S["y_sums"], g + 1)
                    vec.tensor_scalar(st[:, g % 2, :], banks[:, 7, 0:T], EPS, None, ALU.add).then_inc(S["y_var"], 1)
                if n >= 7 and n % 4 in (3, 0):
                    g = (n - 6) // 2
                    vec.wait_ge(S["y_root"], g // 2 + 1)
                    step(vec.reciprocal(st[:, 2 + g % 2, :], st[:, g % 2, :]))
                    for m in (2 * g, 2 * g + 1):
                        at = COLS["ssm_norm"] + m
                        vec.scalar_tensor_tensor(xbc[:, m, :], xbc[:, m, :], cols[:, at:at + 1], st[:, 2 + g % 2, :],
                                                 ALU.mult, ALU.mult).then_inc(S["y_f"], 1)
                if n < pairs and n % 2:
                    g = n // 2
                    vec.wait_ge(panel_used, FIRST_PANEL[rest] + n + 1)
                    if g:
                        vec.wait_ge(S["mod_cols"], 1 + g)
                    vec.tensor_copy(mod_tail, banks[0:2, 0, :]).then_inc(summed, 1)
                if n < pairs:
                    q = FIRST_PANEL[rest] + n + SPLIT
                    split(q, q % RAW, q % SPLIT, q // RAW)
            stage("branch_ssm", mix_post)
            stage_x("out", gated_x(16))
            split_after("out", 0)
            variance(2, False, EPS, "out")
            inverse_root(2)
            apply_norm(1, ev8, mod[:, 32:40], mod[:, 24:32], False, behind="out")
            stage("ff1", relu2_post)
            stage_x("ff2", gated_x(40))
            split_after("ff2", 0)
            variance(3, False, EPS, "ff2")
            inverse_root(3)
            apply_norm(2, xb, cols[:, COLS["final"]:COLS["final"] + KD], None, False, behind="ff2")

            norms = [3]

            def layer_norm(stage_name, i, last=False):
                k = norms[0]
                at = KD * i
                split_after(stage_name, 0)
                variance(k + 1, True, LN_EPS, stage_name)
                inverse_root(k + 1)
                apply_norm(k, xb, cols[:, COLS["ln_g"] + at:COLS["ln_g"] + at + KD],
                           cols[:, COLS["ln_b"] + at:COLS["ln_b"] + at + KD], True, not last, stage_name)
                norms[0] += 1

            def feed_forward(i, ln, last=False):
                stage(f"gu{i}", glu_post)
                stage_x(f"down{i}", deep_x, norms[0] - 3)
                layer_norm(f"down{i}", ln, last)

            feed_forward(0, 0)
            stage("qkv", nothing, qkv)
            vec.wait_ge(S["near_loaded"], 16 * HEADS)
            for h in range(HEADS + 5):
                if h < HEADS:
                    vec.wait_ge(S["s_done"], h + 1)
                    if h >= 3:
                        vec.wait_ge(S["pt_done"], h - 2)
                    b = banks[:, h % 2, :]
                    pr = probs[:, h % 3, :]
                    vec.scalar_tensor_tensor(pr[:, 0:P], b[:, 0:P], SCALE, near[:, h, P:T], ALU.mult, ALU.add)\
                        .then_inc(S["s_biased"], 1)
                    vec.scalar_tensor_tensor(pr[:, P:3 * P], b[:, P:3 * P], SCALE, near[:, h, :], ALU.mult, ALU.add)\
                        .then_inc(S["s_biased"], 1)
                    vec.wait_ge(S["s_biased"], 2 * h + 1)
                    step(vec.reduce_max(sm[:, h, 0:1], pr[:, 0:P], AX.X))
                    vec.wait_ge(S["s_biased"], 2 * h + 2)
                    step(vec.reduce_max(sm[:, h, 1:2], pr[:, P:3 * P], AX.X))
                    vec.tensor_scalar(sm[:, h, 2:4], sm[:, h, 0:2], -1.0, None, ALU.mult).then_inc(S["s_max"], 1)
                if 1 <= h <= HEADS:
                    m = h - 1
                    vec.wait_ge(S["p_exp"], 2 * (m + 1))
                    step(vec.reciprocal(sm[:, m, 6:8], sm[:, m, 4:6]))
                    pr = probs[:, m % 3, :]
                    vec.tensor_scalar(pr[:, 0:P], pr[:, 0:P], sm[:, m, 6:7], None, ALU.mult)
                    vec.tensor_scalar(pr[:, P:3 * P], pr[:, P:3 * P], sm[:, m, 7:8], None, ALU.mult)\
                        .then_inc(S["p_norm"], 1)
                if 4 <= h < HEADS + 4:
                    m = h - 4
                    vec.wait_ge(S["o_done"], m + 1)
                    if m >= 2:
                        vec.wait_ge(S["o_lo"], m - 1)
                    vec.tensor_copy(o_t[:, m % 2, :], banks[:, 3, 0:T]).then_inc(S["o_copied"], 1)
                if h >= 5:
                    m = h - 5
                    vec.wait_ge(S["o_hi"], m + 1)
                    vec.tensor_tensor(H[:, m, 1, :], o_t[:, m % 2, :], H[:, m, 0, :], ALU.subtract)\
                        .then_inc(S["o_lo"], 1)
            stage_x("att_out", deep_x, norms[0] - 3)
            layer_norm("att_out", 1)
            feed_forward(1, 2)
            feed_forward(2, 3)

            def pool_take_up(s, n, G):
                g = 1 - n
                take_sum(s, n, G, by_group(pu[:, :, :])[:, g, :, :])
                own_sum(s, n)
                src, reach = pu, 1
                for w in range(2 * g + 2):
                    b = slice(max(2 * w, BANKS * g), BANKS * g + BANKS)
                    mark(vec.tensor_copy(pw[:, w, b, 0:reach], src[:, b, 0:reach]))
                    step(vec.tensor_tensor(pw[:, w, b, reach:T], src[:, b, reach:T], src[:, b, 0:T - reach], ALU.add))
                    src, reach = pw[:, w, :, :], 2 * reach
                vec.wait_ge(S["inv_loaded"], 16)
                edge = max(WINDOWS)
                both = (2 * g, 2 * g + 1)
                for w in both:
                    b = slice(2 * w, 2 * w + 2)
                    mark(vec.tensor_tensor(pooled[:, b, 0:edge], pw[:, w, b, 0:edge],
                                           inv[:, w, :].unsqueeze(1).to_broadcast([P, 2, edge]), ALU.mult))
                    step(vec.scalar_tensor_tensor(pooled[:, b, edge:T], pw[:, w, b, edge:T], 1.0 / WINDOWS[w],
                                                  pu[:, b, edge:T], ALU.mult, ALU.subtract))
                b = slice(BANKS * g, BANKS * g + BANKS)
                vec.tensor_tensor(pooled[:, b, 0:edge], pooled[:, b, 0:edge], pu[:, b, 0:edge], ALU.subtract)\
                    .then_inc(S["pool_f"], 1)

            run(vec, INDEX["pool_in"], split, pool_take_up)
            b = slice(0, BANKS)
            vec.wait_ge(S["pool_hi"], 2)
            vec.tensor_tensor(PG[:, b, 1, :], pooled[:, b, :], PG[:, b, 0, :], ALU.subtract)\
                .then_inc(S["pool_lo"], 1)
            stage("pool_group", scale_post)
            stage_x("pool_out", deep_x, norms[0] - 3)
            layer_norm("pool_out", 4)
            feed_forward(3, 5, last=True)


def kernel(**inputs):
    import numpy as np
    import concourse.bacc as bacc
    from concourse.bass_utils import run_bass_kernel_spmd as launch

    f = {n: np.asarray(a) for n, a in inputs.items()}

    def chunks(w):
        k, n = w.shape
        return w.reshape(k // P, P, n // CHUNK, CHUNK).transpose(2, 0, 1, 3).reshape(-1, P, CHUNK)

    def glu_chunks(w):
        k, n = w.shape
        return chunks(w.reshape(k, 2, n // 2 // T, T).transpose(0, 2, 1, 3).reshape(k, n))

    w_in, w_mod = f["w_in"][0], f["w_mod"][0]
    u, v, z, xbc, dt, ga, gb = np.split(w_in, np.cumsum([D, D, 2 * D, 4 * D, SSM_HEADS, D])[:], axis=1)
    gu, down = f["ffn_w_gu_2"], f["ffn_w_down_2"]
    a_in, b_in = f["a_w_in_2"][0], f["b_w_in_2"][0]
    grouped = f["b_w_group_2"][0].reshape(4, 2, P, T).transpose(0, 2, 1, 3).reshape(4, P, CHUNK)
    stream = np.concatenate([
        chunks(w_mod[:, :2 * D]), chunks(u), chunks(v), chunks(ga), chunks(gb), chunks(f["w_branch_gm"][0]),
        chunks(xbc), chunks(z), chunks(w_mod[:, 2 * D:]), chunks(f["w_branch_ssm"][0]), chunks(f["w_out"][0]),
        chunks(f["w_ff1"][0]), chunks(f["w_ff2"][0]),
        glu_chunks(gu[0, 0]), chunks(down[0, 0]), chunks(a_in), chunks(f["a_w_out_2"][0]),
        glu_chunks(gu[0, 1]), chunks(down[0, 1]), glu_chunks(gu[1, 0]), chunks(down[1, 0]),
        chunks(np.concatenate([b_in[:, CHUNK:], b_in[:, :CHUNK]], axis=1)), grouped, chunks(f["b_w_out_2"][0]),
        glu_chunks(gu[1, 1]), chunks(down[1, 1])])
    panels = stream.reshape(PANELS, 4, P, CHUNK).transpose(0, 2, 1, 3).reshape(PANELS, P, PANEL)

    def columns(a):
        return a.reshape(-1, P).T

    conv_w = f["conv_w"][0].reshape(CONV, 32, P).transpose(2, 1, 0).reshape(P, 32 * CONV)
    cols = np.concatenate([
        columns(f["b_mod"][0]), columns(f["gm_norm_w"][0]), columns(f["conv_b"][0]), conv_w,
        columns(f["ssm_norm_w"][0]), columns(f["final_norm_w"]), columns(f["ln_g_2"].reshape(-1)),
        columns(f["ln_b_2"].reshape(-1)), columns(f["b_scale_2"][0]),
        columns(np.repeat(f["d_skip"][0], HP))], axis=1)
    heads = np.broadcast_to(np.stack([f["dt_bias"][0], f["a_log"][0]]), (P, 2, SSM_HEADS))
    dist = T - 1 - np.arange(BIAS_COLS)
    near = np.maximum(dist, 1).astype(np.float32)
    large = 16 + (np.log(near / np.float32(16)) / np.float32(np.log(8.0)) * np.float32(16)).astype(np.int32)
    bucket = np.where(dist < 0, 32, np.where(dist < 16, dist, np.minimum(large, 31)))
    onehot = (np.arange(33)[:, None] == bucket[None, :]).astype(np.float32)
    tokens = np.arange(1, 17, dtype=np.float32)
    inv = np.broadcast_to(np.stack([1 / np.minimum(tokens, np.float32(w)) for w in WINDOWS]), (P, 4, 16))
    arrays = {
        "panels": panels,
        "x_t": f["x"][0].T.reshape(KD, P, T).transpose(1, 0, 2),
        "c_t": columns(f["c"][0]),
        "cols": cols,
        "heads": heads,
        "ws_t": f["gm_ws"][0].transpose(2, 0, 1),
        "bs": f["gm_bs"][0].reshape(1, -1),
        "wdt": dt.reshape(KD, P, SSM_HEADS).transpose(1, 0, 2),
        "rel": f["rel_bias_2"],
        "onehot": onehot,
        "inv": inv,
    }
    arrays = {f"in_{n}": np.ascontiguousarray(a, dtype=np.float32) for n, a in arrays.items()}
    nc = bacc.Bacc("TRN2", target_bir_lowering=False, num_devices=1)
    args = [nc.dram_tensor(n, a.shape, F32, kind="ExternalInput").ap() for n, a in arrays.items()]
    args.append(nc.dram_tensor("bias_rows", (P, HEADS * BIAS_COLS), F32).ap())
    args.append(nc.dram_tensor("out_t", (P, KD, T), F32, kind="ExternalOutput").ap())
    two_blocks(nc, *args)
    result = launch(nc, [arrays], core_ids=[0]).results[0]["out_t"]
    return result.transpose(1, 0, 2).reshape(D, T).T[None]
```
